# Optimizing a Trainium2 kernel written in Bass

```python
import math
import jax, jax.numpy as jnp
from jax import lax
import numpy as np

D_MODEL = 2048
BATCH = 1
SEQ = 512
DEPTH = 1

N_HEADS = 32
N_KV_HEADS = 4
HEAD_DIM = 64
GROUP = N_HEADS // N_KV_HEADS
WINDOW = 128
BLOCK = WINDOW
ROPE_THETA = 500000.0
ROT_DIM = HEAD_DIM // 4
ATTN_SCALE = 1.0 / math.sqrt(HEAD_DIM)
D_CONV = D_MODEL // 2
CONV_WIDTH = 31
PEER_HEADS = 8
N_KEYS = 128
N_EXPERTS = N_KEYS * N_KEYS
D_KEY = 256
HALF_KEY = D_KEY // 2
TOPK = 16
TOKEN_CHUNK = 128
LN_EPS = 1e-5
ALPHA = (2 * DEPTH) ** 0.25
BETA = (8 * DEPTH) ** -0.25
Q_W = N_HEADS * HEAD_DIM
KV_W = N_KV_HEADS * HEAD_DIM
IN_COLS = 2 * D_CONV + Q_W + 2 * KV_W + 2 * D_MODEL
SPLITS = [2 * D_CONV, 2 * D_CONV + Q_W, 2 * D_CONV + Q_W + KV_W,
          2 * D_CONV + Q_W + 2 * KV_W, 2 * D_CONV + Q_W + 2 * KV_W + D_MODEL]

kernel_name = 'hybrid_conformer_swa_sink_peer_block'

def _layer_norm(x, g, b):
    xf = x.astype(jnp.float32)
    mu = xf.mean(-1, keepdims=True)
    var = jnp.square(xf - mu).mean(-1, keepdims=True)
    return ((xf - mu) * lax.rsqrt(var + LN_EPS) * g + b).astype(x.dtype)

def _rope_tables(positions, dtype):
    inv_freq = ROPE_THETA ** (-jnp.arange(0, ROT_DIM, 2, dtype=jnp.float32) / ROT_DIM)
    ang = positions.astype(jnp.float32)[..., None] * inv_freq
    return jnp.cos(ang)[:, :, None, :].astype(dtype), jnp.sin(ang)[:, :, None, :].astype(dtype)

def _rope_partial(t, cos, sin):
    half = ROT_DIM // 2
    t1, t2, rest = t[..., :half], t[..., half:ROT_DIM], t[..., ROT_DIM:]
    return jnp.concatenate([t1 * cos - t2 * sin, t2 * cos + t1 * sin, rest], axis=-1)

def _sliding_window_attention(q, k, v, sinks):
    B, S = q.shape[0], q.shape[1]
    nb = S // BLOCK
    qb = q.reshape(B, nb, BLOCK, N_KV_HEADS, GROUP, HEAD_DIM).transpose(1, 0, 2, 3, 4, 5)

    def band(t):
        tb = t.reshape(B, nb, BLOCK, N_KV_HEADS, HEAD_DIM)
        prev = jnp.pad(tb[:, :-1], ((0, 0), (1, 0), (0, 0), (0, 0), (0, 0)))
        return jnp.concatenate([prev, tb], axis=2).transpose(1, 0, 2, 3, 4)

    kb, vb = band(k), band(v)
    sink_logits = sinks.astype(jnp.float32).reshape(N_KV_HEADS, GROUP)
    qi = jnp.arange(BLOCK)[:, None]
    sj = jnp.arange(2 * BLOCK)[None, :]
    in_window = (sj > qi) & (sj <= qi + BLOCK)
    neg = jnp.finfo(jnp.float32).min

    def one_block(args):
        n, qn, kn, vn = args
        s = jnp.einsum('bqkgd,bskd->bkgqs', qn, kn,
                       preferred_element_type=jnp.float32) * ATTN_SCALE
        valid = in_window & (sj >= BLOCK * (1 - n))
        s = jnp.where(valid, s, neg)
        sink = jnp.broadcast_to(sink_logits[None, :, :, None, None], s.shape[:-1] + (1,))
        p = jax.nn.softmax(jnp.concatenate([s, sink], axis=-1), axis=-1)[..., :-1]
        return jnp.einsum('bkgqs,bskd->bqkgd', p.astype(vn.dtype), vn)

    out = lax.map(one_block, (jnp.arange(nb), qb, kb, vb))
    return out.transpose(1, 0, 2, 3, 4, 5).reshape(B, S, Q_W)

def _mixer(x, cos, sin, w_in, b_in, conv_dw_w, conv_dw_b, conv_ln_g, conv_ln_b,
           w_conv_out, attn_sinks, w_mix_out):
    B, S, _ = x.shape
    z = x @ w_in + b_in
    glu_in, q, k, v, gate_a, gate_b = jnp.split(z, SPLITS, axis=-1)
    ga, gb = jnp.split(glu_in, 2, axis=-1)
    u = ga * jax.nn.sigmoid(gb)
    u = lax.conv_general_dilated(u, conv_dw_w.astype(u.dtype), (1,), [(CONV_WIDTH - 1, 0)],
                                 dimension_numbers=('NWC', 'WIO', 'NWC'),
                                 feature_group_count=D_CONV) + conv_dw_b
    u = jax.nn.silu(_layer_norm(u, conv_ln_g, conv_ln_b))
    y_conv = u @ w_conv_out
    q = _rope_partial(q.reshape(B, S, N_HEADS, HEAD_DIM), cos, sin)
    k = _rope_partial(k.reshape(B, S, N_KV_HEADS, HEAD_DIM), cos, sin)
    v = v.reshape(B, S, N_KV_HEADS, HEAD_DIM)
    y_attn = _sliding_window_attention(q, k, v, attn_sinks)
    m = jax.nn.sigmoid(gate_a) * y_conv + jax.nn.sigmoid(gate_b) * y_attn
    return m @ w_mix_out

def _peer_chunk(xc, w_peer_q, sub_keys_1, sub_keys_2, expert_u, expert_v):
    C = xc.shape[0]
    q = (xc @ w_peer_q).reshape(C, PEER_HEADS, 2, HALF_KEY)
    s1 = jnp.einsum('chd,nd->chn', q[:, :, 0], sub_keys_1, preferred_element_type=jnp.float32)
    s2 = jnp.einsum('chd,nd->chn', q[:, :, 1], sub_keys_2, preferred_element_type=jnp.float32)
    v1, i1 = lax.top_k(s1, TOPK)
    v2, i2 = lax.top_k(s2, TOPK)
    cand = (v1[..., :, None] + v2[..., None, :]).reshape(C, PEER_HEADS, TOPK * TOPK)
    cidx = (i1[..., :, None] * N_KEYS + i2[..., None, :]).reshape(C, PEER_HEADS, TOPK * TOPK)
    best, pos = lax.top_k(cand, TOPK)
    eidx = jnp.take_along_axis(cidx, pos, axis=-1).reshape(C, PEER_HEADS * TOPK)
    g = jax.nn.softmax(best, axis=-1).reshape(C, PEER_HEADS * TOPK)
    u = expert_u[eidx]
    h = jnp.einsum('cd,ced->ce', xc, u, preferred_element_type=jnp.float32)
    a = (jax.nn.gelu(h, approximate=False) * g).astype(xc.dtype)
    return jnp.einsum('ce,ced->cd', a, expert_v[eidx])

def _peer(x, w_peer_q, sub_keys_1, sub_keys_2, expert_u, expert_v):
    B, S, D = x.shape
    xt = x.reshape(-1, TOKEN_CHUNK, D)
    y = lax.map(lambda xc: _peer_chunk(xc, w_peer_q, sub_keys_1, sub_keys_2,
                                       expert_u, expert_v), xt)
    return y.reshape(B, S, D)

def setup_inputs(seed: int = 0) -> dict:
    key = jax.random.key(seed)
    ks = jax.random.split(key, 24)
    f32 = jnp.float32
    nrm = lambda k, shape, scale: jax.random.normal(k, shape, f32) * scale
    sd = D_MODEL ** -0.5
    w_in = jnp.concatenate([
        nrm(ks[1], (DEPTH, D_MODEL, 2 * D_CONV), sd),
        nrm(ks[2], (DEPTH, D_MODEL, Q_W), sd),
        nrm(ks[3], (DEPTH, D_MODEL, KV_W), sd),
        nrm(ks[4], (DEPTH, D_MODEL, KV_W), sd * BETA),
        nrm(ks[5], (DEPTH, D_MODEL, 2 * D_MODEL), sd)], axis=-1)
    return {
        'x': jax.random.normal(ks[0], (BATCH, SEQ, D_MODEL), f32),
        'positions': jnp.broadcast_to(jnp.arange(SEQ, dtype=jnp.int32)[None, :], (BATCH, SEQ)),
        'w_in': w_in,
        'b_in': nrm(ks[6], (DEPTH, IN_COLS), 0.02),
        'conv_dw_w': nrm(ks[7], (DEPTH, CONV_WIDTH, 1, D_CONV), CONV_WIDTH ** -0.5),
        'conv_dw_b': nrm(ks[8], (DEPTH, D_CONV), 0.02),
        'conv_ln_g': 1.0 + nrm(ks[9], (DEPTH, D_CONV), 0.02),
        'conv_ln_b': nrm(ks[10], (DEPTH, D_CONV), 0.02),
        'w_conv_out': nrm(ks[11], (DEPTH, D_CONV, D_MODEL), D_CONV ** -0.5 * BETA),
        'attn_sinks': nrm(ks[12], (DEPTH, N_HEADS), 1.0),
        'w_mix_out': nrm(ks[13], (DEPTH, D_MODEL, D_MODEL), sd * BETA),
        'ln1_g': 1.0 + nrm(ks[14], (DEPTH, D_MODEL), 0.02),
        'ln1_b': nrm(ks[15], (DEPTH, D_MODEL), 0.02),
        'w_peer_q': nrm(ks[16], (DEPTH, D_MODEL, PEER_HEADS * D_KEY), sd),
        'sub_keys_1': nrm(ks[17], (DEPTH, N_KEYS, HALF_KEY), HALF_KEY ** -0.5),
        'sub_keys_2': nrm(ks[18], (DEPTH, N_KEYS, HALF_KEY), HALF_KEY ** -0.5),
        'expert_u': nrm(ks[19], (DEPTH, N_EXPERTS, D_MODEL), sd),
        'expert_v': nrm(ks[20], (DEPTH, N_EXPERTS, D_MODEL), BETA),
        'ln2_g': 1.0 + nrm(ks[21], (DEPTH, D_MODEL), 0.02),
        'ln2_b': nrm(ks[22], (DEPTH, D_MODEL), 0.02),
    }

def reference(x, positions, w_in, b_in, conv_dw_w, conv_dw_b, conv_ln_g, conv_ln_b,
              w_conv_out, attn_sinks, w_mix_out, ln1_g, ln1_b, w_peer_q, sub_keys_1,
              sub_keys_2, expert_u, expert_v, ln2_g, ln2_b):
    cos, sin = _rope_tables(positions, x.dtype)
    for l in range(DEPTH):
        mix = _mixer(x, cos, sin, w_in[l], b_in[l], conv_dw_w[l], conv_dw_b[l],
                     conv_ln_g[l], conv_ln_b[l], w_conv_out[l], attn_sinks[l], w_mix_out[l])
        x = _layer_norm(ALPHA * x + mix, ln1_g[l], ln1_b[l])
        ffn = _peer(x, w_peer_q[l], sub_keys_1[l], sub_keys_2[l], expert_u[l], expert_v[l])
        x = _layer_norm(ALPHA * x + ffn, ln2_g[l], ln2_b[l])
    return x


_drawn_inputs = setup_inputs


def setup_inputs(seed=0):
    import zlib

    import numpy as np

    out = dict(_drawn_inputs(seed))
    spreads = {}
    factors = {'conv_dw_b': 3.363,
     'conv_ln_g': 4.333,
     'conv_ln_b': 5.02,
     'attn_sinks': 8.0,
     'ln2_g': 2.767,
     'ln2_b': 2.827}
    for name, (base, spread) in spreads.items():
        noise = np.random.default_rng([zlib.crc32(name.encode()), seed]).standard_normal(out[name].shape)
        drawn = base * np.exp(spread * noise) if base else spread * noise
        out[name] = __import__('jax').numpy.asarray(drawn.astype(out[name].dtype))
    for name, factor in factors.items():
        out[name] = (out[name] * factor).astype(out[name].dtype)
    return out
```

```python
from contextlib import ExitStack

import numpy as np

import concourse.bass as bass
from concourse import mybir

F32 = mybir.dt.float32
F32R = mybir.dt.float32r
I32 = mybir.dt.int32
U32 = mybir.dt.uint32
ALU = mybir.AluOpType
ACT = mybir.ActivationFunctionType
AX = mybir.AxisListType.X
ds = bass.ds

P = 128
S = 512
D = 2048
KD = D // P
N_HEADS, N_KV, HEAD = 32, 4, 64
ROT = HEAD // 4
THETA = 500000.0
SCALE = HEAD ** -0.5
NB = S // P
CC = D // 2
KC = CC // P
TAPS = 31
PAD = TAPS - 1
SLOT = S + PAD
HEADS_R, NKEY, TOPK = 8, 128, 16
EPS = 1e-5
ALPHA = 2.0 ** 0.25
NEG = -3.0e38

T_GLU = 0
T_K = T_GLU + 2 * KC
T_V = T_K + 2
T_Q = T_V + 2
T_GATE = T_Q + KD
T_MIX = T_GATE + 2 * KD + KD // 2
T_ROUTE = T_MIX + KD
T_PEER = T_ROUTE + 2 * HEADS_R
EG = 8
N_GROUPS = NKEY // EG
GROUP_TILES = EG + KD // 2
N_TILES = T_PEER + N_GROUPS * GROUP_TILES
CG = 16
N_CG = S // CG
QUADS_OF = {3: 48, 4: 48, 5: 32}
POOL_Q = (T_Q + 2, T_Q + KD + 1)
POOL_R = (T_ROUTE + 2, T_PEER + EG + 1)

C_BIAS = 0
C_TAPS = C_BIAS + T_GATE + 2 * KD
C_CONVB = C_TAPS + KC * TAPS
C_CLNG = C_CONVB + KC
C_CLNB = C_CLNG + KC
C_SINK = C_CLNB + KC
C_LN1G = C_SINK + N_HEADS
C_LN1B = C_LN1G + KD
C_LN2G = C_LN1B + KD
C_LN2B = C_LN2G + KD
C_KEYS = C_LN2B + KD
N_PARAM = C_KEYS + 2 * NKEY

K_IDENT, K_IOTA, K_MASK, K_ROT, K_DUP, K_RDUP = 0, 128, 256, 512, 640, 896
K_FREQ = 1152
N_CONST = 1153

TWO_PI_A = 6.28125
TWO_PI_B = 1.9340515136718750e-03
TWO_PI_C = 2 * np.pi - TWO_PI_A - TWO_PI_B
ROUNDER = 1.5 * 2.0 ** 23


def build(nc, x_t, pos, w_in, w_conv, w_mix, w_route, exp_u, exp_v, params, consts, gates, out):
    with ExitStack() as ctx:
        base = -(-nc.sbuf_base // 32) * 32
        at = [base]

        def fixed(name, shape, dt):
            t = nc.alloc_sbuf_tensor_at(name, shape, dt, offset=at[0])
            at[0] += -(-4 * int(np.prod(shape[1:])) // 32) * 32
            return t

        act_hi = fixed("act_hi", [P, KD, S], F32R)
        act_lo = fixed("act_lo", [P, KD, S], F32R)
        mix = fixed("mix", [P, KD, S], F32)
        raw = [fixed(f"raw{i}", [P, 16, P], F32) for i in range(2)]
        w_hi = [fixed(f"w_hi{i}", [P, 16, P], F32R) for i in range(2)]
        w_lo = [fixed(f"w_lo{i}", [P, 16, P], F32R) for i in range(2)]
        ident = fixed("ident", [P, P], F32)
        iota = fixed("iota", [P, P], F32)
        ones = fixed("ones", [P, P], F32)
        par = fixed("par", [P, N_PARAM], F32)
        region = at[0]

        def shared(name, shape, dt, offset):
            return nc.alloc_sbuf_tensor_at(name, shape, dt, offset=region + offset)

        uT = shared("uT", [P, KC + 1, SLOT], F32, 0)
        kT = shared("kT", [P, N_KV, S], F32, 19520)
        vN = shared("vN", [P, NB, N_KV * HEAD], F32, 27712)
        mask = shared("mask", [P, 2 * P], F32, 31808)
        rope_m = shared("rope_m", [P, 5 * P + 1], F32, 32832)
        cosT = shared("cosT", [P, S], F32, 35424)
        sinT = shared("sinT", [P, S], F32, 37472)
        zt = [shared(f"zt{i}", [P, S], F32, 39520 + 2048 * i) for i in range(2)]
        t1 = [shared(f"t1_{i}", [P, S], F32, 43616 + 2048 * i) for i in range(2)]
        t2 = [shared(f"t2_{i}", [P, S], F32, 47712 + 2048 * i) for i in range(2)]
        half_b = shared("half_b", [P, 2 * KC], F32, 51808)
        posi = shared("posi", [P, S], I32, 51872)
        def ln_buffers(tag, offset):
            names = ("mean", "var", "sd", "rs", "tt")
            b = {m: shared(f"{tag}_{m}", [P, S], F32, offset + 2048 * i) for i, m in enumerate(names)}
            b["sq"] = [shared(f"{tag}_sq{i}", [P, 2, S], F32, offset + 10240 + 4096 * i) for i in range(2)]
            return b

        lnc = ln_buffers("lnc", 35424)
        ln1 = ln_buffers("ln1", 4096)
        ln2 = ln_buffers("ln2", 4096)
        prob = [shared(f"prob{i}", [P, 4, 2, 2 * P + 1], F32, 35424 + 8224 * i) for i in range(2)]
        prT = shared("prT", [P, 4, S], F32, 51872)
        smax = shared("smax", [P, 2, 4, 8], F32, 60064)
        u_hi = shared("u_hi", [P, KC, S], F32R, 19520)
        u_lo = shared("u_lo", [P, KC, S], F32R, 35904)
        sig_a = [shared(f"sig_a{i}", [P, S], F32, 52288 + 2048 * i) for i in range(2)]
        sig_b = [shared(f"sig_b{i}", [P, S], F32, 56384 + 2048 * i) for i in range(2)]
        x_res = [shared(f"x_res{i}", [P, S], F32, 2048 * i) for i in range(2)]
        rq = [shared(f"rq{i}", [P, S], F32, 22528 + 2048 * i) for i in range(2)]
        rest = shared("rest", [P, NB, NKEY], F32, 0)
        val = shared("val", [P, 2, NB, TOPK], F32, 2048)
        idx = shared("idx", [P, 2, NB, TOPK], U32, 2560)
        idxf = shared("idxf", [P, 2, NB, TOPK], F32, 3072)
        cand = shared("cand", [P, NB, TOPK * TOPK], F32, 3584)
        cand2 = shared("cand2", [P, NB, TOPK * TOPK], F32, 7680)
        best = shared("best", [P, NB, TOPK], F32, 11776)
        place = shared("place", [P, NB, TOPK], U32, 12032)
        digit = shared("digit", [P, 2, NB, TOPK], U32, 12288)
        digitf = shared("digitf", [P, 2, NB * TOPK], F32, 12800)
        expo = shared("expo", [P, 2, NB, TOPK], F32, 13312)
        esum = shared("esum", [P, 2, NB], F32, 13824)
        pick = shared("pick", [P, 2, NB * TOPK, TOPK], F32, 26624)
        sel_i = shared("sel_i", [P, 2, NB, P], F32, 34816)
        sel_g = shared("sel_g", [P, NB, P], F32, 38912)
        hot2 = shared("hot2", [P, 16, P], F32, 0)
        hot1 = shared("hot1", [P, 16, P], F32, 8192)
        i_t = shared("i_t", [P, 2, S], F32, 53248)
        g_t = shared("g_t", [P, S], F32, 57344)
        stage = [shared(f"stage{i}", [P, NKEY, CG], F32, 32768 + 8192 * i) for i in range(2)]
        a_hi = shared("a_hi", [P, EG, S], F32R, 0)
        a_lo = shared("a_lo", [P, EG, S], F32R, 16384)
        hid_0 = shared("hid_0", [P, EG, S], F32, 16384)
        gate = shared("gate", [P, N_CG, EG * CG], F32, 32768)
        hid = [shared(f"hid{i}", [P, S], F32, 49152 + 2048 * i) for i in range(2)]
        gated = [shared(f"gated{i}", [P, S], F32, 53248 + 2048 * i) for i in range(2)]

        z = ctx.enter_context(nc.psum_tensor("z", [P, 4, S], F32))
        aux = ctx.enter_context(nc.psum_tensor("aux", [P, 4, S], F32))

        def sem(name):
            return ctx.enter_context(nc.semaphore(name))

        w_landed = [sem("w_landed0"), sem("w_landed1")]
        hi_ready, lo_ready, tile_done = sem("hi_ready"), sem("lo_ready"), sem("tile_done")
        z_read = [sem("z_read0"), sem("z_read1")]
        x_landed = [sem(f"x_landed{i}") for i in range(4)]
        const_landed, pos_landed = sem("const_landed"), sem("pos_landed")
        x_hi_ready, x_lo_ready = sem("x_hi_ready"), sem("x_lo_ready")
        pads_ready, ones_ready = sem("pads_ready"), sem("ones_ready")
        angle_ready, sincos_ready = sem("angle_ready"), sem("sincos_ready")
        zt_used, k_rot = sem("zt_used"), sem("k_rot")
        v_turned, v_ready = sem("v_turned"), sem("v_ready")
        q_rot, rope_part, roped, tap_done = sem("q_rot"), sem("rope_part"), sem("roped"), sem("tap_done")
        lns = {}
        for tag in ("c", "1", "2"):
            lns[tag] = {m: sem(f"ln{tag}_{m}") for m in
                        ("sum", "centred", "squared", "sqsum", "var", "sd", "rs", "scaled", "done")}
        scored, masked, maxed, exped = sem("scored"), sem("masked"), sem("maxed"), sem("exped")
        sink_in, p_ready, p_turned, pT_ready = sem("sink_in"), sem("p_ready"), sem("p_turned"), sem("pT_ready")
        pv_done, y_ready = sem("pv_done"), sem("y_ready")
        u_hi_ready, u_lo_ready, gated_y, prod_y, mixed = (sem("u_hi_ready"), sem("u_lo_ready"), sem("gated_y"),
                                                          sem("prod_y"), sem("mixed"))
        m_hi_ready, m_lo_ready = sem("m_hi_ready"), sem("m_lo_ready")
        x_res_landed = [sem("x_res_landed0"), sem("x_res_landed1")]
        x1_ready, x1_hi_ready, x1_lo_ready, acc_ready = (sem("x1_ready"), sem("x1_hi_ready"), sem("x1_lo_ready"),
                                                         sem("acc_ready"))
        key_scored, keys_taken, chain, asked, exp_ready = (sem("key_scored"), sem("keys_taken"), sem("chain"),
                                                           sem("asked"), sem("exp_ready"))
        picked, pick_scaled = sem("picked"), sem("pick_scaled")
        sel_ready, sel_turned, sel_t_ready = sem("sel_ready"), sem("sel_turned"), sem("sel_t_ready")
        hot_matched = sem("hot_matched")
        hot_ready, quad_done, quad_staged = sem("hot_ready"), sem("quad_done"), sem("quad_staged")
        stage_out = [sem("stage_out0"), sem("stage_out1")]
        gate_landed, hid_ready, gated_ready = sem("gate_landed"), sem("hid_ready"), sem("gated_ready")
        a_hi_ready, a_lo_ready = sem("a_hi_ready"), sem("a_lo_ready")
        out_ready, out_stored = sem("out_ready"), sem("out_stored")

        block = ctx.enter_context(nc.Block())
        gates_r = gates.rearrange("c p (g f) -> p c g f", f=EG * CG)

        @block.sync
        def _(sp):
            def load(n, b, src):
                if not (isinstance(n, int) and n < 2):
                    sp.wait_ge(lo_ready, n - 1)
                sp.dma_start(raw[b][:].rearrange("p k c -> p (k c)"), src).then_inc(w_landed[b], 16)

            load(0, 0, w_in[0])
            for c in range(4):
                sp.dma_start(mix[:, 4 * c:4 * c + 4, :], x_t[:, 4 * c:4 * c + 4, :]).then_inc(x_landed[c], 16)
            load(1, 1, w_in[1])
            for dst, a, b in ((ident, K_IDENT, K_IOTA), (iota, K_IOTA, K_MASK), (mask, K_MASK, K_ROT),
                              (rope_m, K_ROT, N_CONST)):
                sp.dma_start(dst[:, :], consts[:, a:b]).then_inc(const_landed, 16)
            sp.dma_start(par[:, :], params).then_inc(const_landed, 16)
            sp.dma_start(posi[:, :], pos.to_broadcast([P, S])).then_inc(pos_landed, 16)
            pair = w_in.rearrange("(a b) p f -> a b p f", b=2)
            with sp.Fori(1, T_GATE // 2) as i:
                for b in range(2):
                    load(2 * i + b, b, pair[i, b])
            quad = w_in[T_GATE:, :, :].rearrange("(i h q) p f -> i h q p f", h=2, q=4)
            conv = w_conv.rearrange("(i h) p f -> i h p f", h=2)
            with sp.Fori(0, 4) as i:
                for h in range(2):
                    for q in range(5):
                        o = 5 * h + q
                        load(10 * i + T_GATE + o, o % 2, quad[i, h, q] if q < 4 else conv[i, h])
            wm = w_mix.rearrange("(a b) p f -> a b p f", b=2)
            xr = x_t.rearrange("p (a b) s -> a b p s", b=2)
            for b in range(2):
                load(T_MIX + b, b, wm[0, b])
                if b == 0:
                    sp.wait_ge(u_lo_ready, 1)
                sp.dma_start(x_res[b][:, :], xr[0, b]).then_inc(x_res_landed[b], 16)
            with sp.Fori(1, KD // 2) as i:
                for b in range(2):
                    load(2 * i + T_MIX + b, b, wm[i, b])
                    sp.wait_ge(z_read[b], i + T_MIX // 2)
                    sp.dma_start(x_res[b][:, :], xr[i, b]).then_inc(x_res_landed[b], 16)
            wr = w_route.rearrange("(a b) p f -> a b p f", b=2)
            with sp.Fori(0, HEADS_R) as i:
                for b in range(2):
                    load(2 * i + T_ROUTE + b, b, wr[i, b])
            u = exp_u.rearrange("(g e) p f -> g e p f", e=EG)
            v = exp_v.rearrange("(g e) p f -> g e p f", e=KD // 2)
            for e in range(EG - 1):
                load(T_PEER + e, e % 2, u[0, e])
            c = 0
            for e, quads in QUADS_OF.items():
                for _ in range(4 * quads // CG):
                    sp.wait_ge(quad_staged, CG // 4 * (c + 1))
                    sp.dma_start(gates[c], stage[c % 2][:].rearrange("p k c -> p (k c)")).then_inc(stage_out[c % 2], 16)
                    c += 1
                if c == N_CG:
                    sp.wait_ge(stage_out[0], 16 * (N_CG // 2))
                    sp.wait_ge(stage_out[1], 16 * (N_CG // 2))
                    sp.dma_start(gate[:], gates_r[:, :, 0, :]).then_inc(gate_landed, 16)
                n = T_PEER + e + 4
                load(n, n % 2, u[0, e + 4] if e + 4 < EG else v[0, e + 4 - EG])

            def group(g, first, last):
                n = GROUP_TILES * g + T_PEER
                for e in range(0 if first else EG):
                    load(n + e, e % 2, u[g, e])
                for e in range(2 if first else 0, KD // 2):
                    load(n + EG + e, e % 2, v[g, e])
                    if e == 2 and not last:
                        sp.wait_ge(gated_ready, EG * g + EG)
                        sp.dma_start(gate[:], gates_r[:, :, g + 1, :]).then_inc(gate_landed, 16)

            group(0, True, False)
            with sp.Fori(1, N_GROUPS - 1) as g:
                group(g, False, False)
            group(N_GROUPS - 1, False, True)
            for k in range(KD):
                sp.wait_ge(out_ready, k + 1)
                sp.dma_start(out[:, k, :], mix[:, k, :]).then_inc(out_stored, 16)
            sp.wait_ge(out_stored, 16 * KD)

        @block.tensor
        def _(pe):
            def tile(n, b, hi, lo, ready=None):
                pe.wait_ge(hi_ready, n + 1)
                pe.wait_ge(lo_ready, n + 1)
                if not (isinstance(n, int) and n < 2):
                    pe.wait_ge(z_read[b], half(n, b))
                for k in range(KD):
                    if ready:
                        ready(k)
                    pe.matmul(z[:, 2 * b, :], w_hi[b][:, k, :], hi[:, k, :], start=k == 0, stop=False)
                    pe.matmul(z[:, 2 * b, :], w_hi[b][:, k, :], lo[:, k, :], start=False, stop=False)
                    m = pe.matmul(z[:, 2 * b, :], w_lo[b][:, k, :], hi[:, k, :], start=False, stop=k == KD - 1)
                m.then_inc(tile_done, 1)

            def tile2(n, b, hi, lo, ready=None):
                pe.wait_ge(hi_ready, n + 1)
                pe.wait_ge(lo_ready, n + 1)
                pe.wait_ge(z_read[b], half(n, b))
                for s in range(2):
                    for k in range(8):
                        if ready and s == 0:
                            ready(k)
                        pe.matmul(z[:, 2 * b + s, :], w_hi[b][:, 8 * s + k, :], hi[:, k, :], start=k == 0, stop=False)
                        pe.matmul(z[:, 2 * b + s, :], w_hi[b][:, 8 * s + k, :], lo[:, k, :], start=False, stop=False)
                        m = pe.matmul(z[:, 2 * b + s, :], w_lo[b][:, 8 * s + k, :], hi[:, k, :],
                                      start=False, stop=k == 7)
                m.then_inc(tile_done, 1)

            def half(n, b):
                return n // 2 if isinstance(n, int) else n.half

            class Tile:
                def __init__(self, i, per, base, b):
                    self.n, self.half = 2 * per * i + base + b, per * i + base // 2

                def __add__(self, k):
                    return self.n + k

            def x_ready(k):
                if k % 4 == 0:
                    pe.wait_ge(x_hi_ready, k // 4 + 1)
                    pe.wait_ge(x_lo_ready, k // 4 + 1)

            tile(0, 0, act_hi, act_lo, x_ready)
            tile(1, 1, act_hi, act_lo)
            with pe.Fori(1, KC) as i:
                for b in range(2):
                    tile(Tile(i, 1, 0, b), b, act_hi, act_lo)
            pe.wait_ge(const_landed, 16 * 5)

            def keys(kt):
                pe.wait_ge(z_read[kt], T_K // 2 + 1)
                for g in range(2):
                    a, rot = 2 * g, 2 * g + 1
                    if kt:
                        pe.wait_ge(roped, g + 1)
                    pe.matmul(aux[:, a, :], rope_m[:, P * (1 + g):P * (2 + g)], zt[kt][:, :], start=True, stop=True)
                    pe.matmul(aux[:, rot, :], rope_m[:, P * (3 + g):P * (4 + g)], zt[kt][:, :],
                              start=True, stop=True).then_inc(k_rot, 1)

            def values(vt):
                pe.wait_ge(z_read[vt], T_V // 2 + 1)
                pe.wait_ge(roped, 4)
                for n in range(NB):
                    m = pe.transpose(aux[:, 2 + vt, n * P:n * P + P], zt[vt][:, n * P:n * P + P], ident[:, :])
                m.then_inc(v_turned, 1)

            tile(T_K, 0, act_hi, act_lo)
            tile(T_K + 1, 1, act_hi, act_lo)
            keys(0)
            tile(T_V, 0, act_hi, act_lo)
            keys(1)
            tile(T_V + 1, 1, act_hi, act_lo)
            values(0)
            values(1)

            with pe.Fori(0, KD // 2) as i:
                for b in range(2):
                    tile(Tile(i, 1, T_Q, b), b, act_hi, act_lo)
                for b in range(2):
                    pe.wait_ge(z_read[b], i + T_Q // 2 + 1)
                    pe.wait_ge(rope_part, 4 * i + 2 * b + 2 * N_KV - 3)
                    pe.matmul(aux[:, b, :], rope_m[:, 0:P], zt[b][:, :], start=True, stop=True).then_inc(q_rot, 1)

            def norm_sum(tag, src, nk, ready):
                for k in range(nk):
                    ready(k)
                    m = pe.matmul(aux[:, 0, :], ones[:, :], src(k), start=k == 0, stop=k == nk - 1)
                m.then_inc(lns[tag]["sum"], 1)

            def norm_sq(tag, sq, nk):
                for c in range(nk // 2):
                    pe.wait_ge(lns[tag]["squared"], c + 1)
                    for k in range(2):
                        m = pe.matmul(aux[:, 1, :], ones[:, :], sq[c % 2][:, k, :],
                                      start=c + k == 0, stop=2 * c + k == nk - 1)
                    m.then_inc(lns[tag]["sqsum"], 1)

            pe.wait_ge(ones_ready, 1)
            pe.wait_ge(roped, N_KV + KD)
            norm_sum("c", lambda k: uT[:, k, 0:S], KC, lambda k: pe.wait_ge(tap_done, TAPS * (k + 1)))
            norm_sq("c", lnc["sq"], KC)

            units = [(g, n) for g in range(N_KV) for n in range(NB)]

            def scores(u):
                g, n = units[u]
                lo_c, w = max(n - 1, 0) * P, P if n == 0 else 2 * P
                for j in range(4):
                    if u or j >= 2:
                        pe.wait_ge(masked, 4 * u + j - 1)
                    elif j == 0:
                        pe.wait_ge(lns["c"]["var"], 1)
                    for e in range(2):
                        m = pe.matmul(aux[:, 2 * (j % 2) + e, 0:w], mix[64 * e:64 * e + 64, 4 * g + j, n * P:n * P + P],
                                      kT[64 * e:64 * e + 64, g, lo_c:lo_c + w], start=True, stop=True)
                    m.then_inc(scored, 1)

            def turn(u):
                g, n = units[u]
                w = 1 if n == 0 else 2
                pe.wait_ge(p_ready, u + 1)
                for e in range(2):
                    for kb in range(w):
                        t = w * e + kb
                        if t == 3:
                            pe.wait_ge(pT_ready, turned_before(u) + 1)
                        elif u:
                            pe.wait_ge(pT_ready, turned_before(u))
                        for j in range(4):
                            m = pe.transpose(z[:, t % 3, j * P:j * P + P],
                                             prob[u % 2][:, j, e, 1 + kb * P:1 + kb * P + P], ident[:, :])
                        m.then_inc(p_turned, 1)

            def turned_before(u):
                return sum(2 if n == 0 else 4 for g, n in units[:u])

            def values_out(u):
                g, n = units[u]
                w = 1 if n == 0 else 2
                if u == 0:
                    pe.wait_ge(v_ready, 2)
                else:
                    pe.wait_ge(y_ready, u)
                for e in range(2):
                    for kb in range(w):
                        pe.wait_ge(pT_ready, turned_before(u) + w * e + kb + 1)
                        m = pe.matmul(z[64 * e:64 * e + 64, 3, :], vN[:, n - w + 1 + kb, g * HEAD:g * HEAD + HEAD],
                                      prT[:, w * e + kb, :], start=kb == 0, stop=kb == w - 1)
                m.then_inc(pv_done, 1)

            scores(0)
            for u in range(len(units)):
                if u + 1 < len(units):
                    scores(u + 1)
                turn(u)
                values_out(u)

            pe.wait_ge(y_ready, len(units))
            with pe.Fori(0, 4) as i:
                for h in range(2):
                    for q in range(5):
                        o = 5 * h + q
                        n = Tile(i, 5, T_GATE + o - o % 2, o % 2)
                        if q < 4:
                            tile(n, o % 2, act_hi, act_lo)
                        else:
                            pe.wait_ge(u_hi_ready, 1)
                            pe.wait_ge(u_lo_ready, 1)
                            tile2(n, o % 2, u_hi, u_lo)

            def m_ready(k):
                if k % 4 == 0:
                    pe.wait_ge(m_hi_ready, k // 4 + 1)
                    pe.wait_ge(m_lo_ready, k // 4 + 1)

            tile(T_MIX, 0, act_hi, act_lo, m_ready)
            tile(T_MIX + 1, 1, act_hi, act_lo)
            with pe.Fori(1, KD // 2) as i:
                for b in range(2):
                    tile(Tile(i, 1, T_MIX, b), b, act_hi, act_lo)
            norm_sum("1", lambda k: mix[:, k, :], KD, lambda k: pe.wait_ge(z_read[k % 2], (T_MIX + k) // 2 + 1))
            norm_sq("1", ln1["sq"], KD)

            def key_scores(t):
                pe.wait_ge(z_read[t % 2], (T_ROUTE + t) // 2 + 1)
                if t >= 2:
                    pe.wait_ge(keys_taken, t - 1)
                for c in range(NB):
                    m = pe.matmul(aux[:, t % 2, c * P:c * P + P], rq[t % 2][:, c * P:c * P + P],
                                  par[:, C_KEYS + (t % 2) * NKEY:C_KEYS + (t % 2 + 1) * NKEY], start=True, stop=True)
                m.then_inc(key_scored, 1)

            def x1_block(k):
                pe.wait_ge(x1_hi_ready, k + 1)
                pe.wait_ge(x1_lo_ready, k + 1)

            for t in range(2 * HEADS_R):
                tile(T_ROUTE + t, t % 2, act_hi, act_lo, x1_block if t == 0 else None)
                if t:
                    key_scores(t - 1)

            def turn_chosen():
                pe.wait_ge(sel_ready, HEADS_R)
                for m_, src in enumerate((lambda c: sel_i[:, 0, c, :], lambda c: sel_i[:, 1, c, :],
                                          lambda c: sel_g[:, c, :])):
                    for c in range(NB):
                        m = pe.transpose(aux[:, m_, c * P:c * P + P], src(c), ident[:, :])
                    m.then_inc(sel_turned, 1)

            def quad_mm(q):
                pe.wait_ge(hot_ready, q + 1)
                if q >= 4:
                    pe.wait_ge(quad_staged, q - 3)
                else:
                    pe.wait_ge(sel_t_ready, 3)
                for c in range(4):
                    s_ = 4 * (q % 4) + c
                    m = pe.matmul(aux[:, q % 4, c * P:c * P + P], hot2[:, s_, :], hot1[:, s_, :],
                                  start=True, stop=True)
                m.then_inc(quad_done, 1)

            quads = [0]
            for e in range(EG):
                first_k = 4 if e == min(QUADS_OF) else 0
                per_k = QUADS_OF.get(e, 0) // (KD - first_k)

                def beside(k):
                    if e == 0 and k == 2:
                        key_scores(2 * HEADS_R - 1)
                    if e == min(QUADS_OF) and k == 0:
                        turn_chosen()
                    if k >= first_k:
                        for _ in range(per_k):
                            quad_mm(quads[0])
                            quads[0] += 1
                tile(T_PEER + e, e % 2, act_hi, act_lo, beside)

            def outputs(g):
                for j in range(KD // 2):
                    def a_ready(k):
                        if j == 0:
                            pe.wait_ge(a_hi_ready, EG * g + k + 1)
                            pe.wait_ge(a_lo_ready, EG * g + k + 1)
                    n = T_PEER + EG + j if isinstance(g, int) else Tile(g, EG, T_PEER + EG + j - j % 2, j % 2)
                    tile2(n, j % 2, a_hi, a_lo, a_ready)

            outputs(0)
            with pe.Fori(1, N_GROUPS) as g:
                for e in range(EG):
                    tile(Tile(g, EG, T_PEER + e - e % 2, e % 2), e % 2, act_hi, act_lo)
                outputs(g)
            norm_sum("2", lambda k: mix[:, k, :], KD,
                     lambda k: pe.wait_ge(z_read[k // 2 % 2], (N_TILES - KD // 2 + k // 2) // 2 + 1))
            norm_sq("2", ln2["sq"], KD)

        @block.scalar
        def _(act):
            def hi(n, b):
                act.wait_ge(w_landed[b], 16 * (n // 2) + 16 if isinstance(n, int) else 8 * n + 16 - 8 * b)
                if not (isinstance(n, int) and n < 2):
                    act.wait_ge(tile_done, n - 1)
                act.activation(w_hi[b][:], raw[b][:], ACT.Copy).then_inc(hi_ready, 1)

            hi(0, 0)
            for c in range(4):
                act.wait_ge(x_landed[c], 16)
                act.activation(act_hi[:, 4 * c:4 * c + 4, :], mix[:, 4 * c:4 * c + 4, :], ACT.Copy)\
                   .then_inc(x_hi_ready, 1)
            hi(1, 1)
            act.wait_ge(angle_ready, 1)
            act.activation(sinT[:, :], t1[0][:, :], ACT.Sin).then_inc(sincos_ready, 1)
            act.wait_ge(angle_ready, 2)
            act.activation(cosT[:, :], t1[1][:, :], ACT.Sin).then_inc(sincos_ready, 1)

            with act.Fori(0, KC) as i:
                act.wait_ge(zt_used, i + 1)
                act.wait_ge(tile_done, 2 * i + 1)
                act.activation(zt[0][:, :], z[:, 0, :], ACT.Identity, scale=0.5,
                               bias=half_b[:, ds(2 * i, 1)]).then_inc(z_read[0], 1)
                hi(2 * i + 2, 0)
                act.wait_ge(tile_done, 2 * i + 2)
                act.activation(zt[1][:, :], z[:, 2, :], ACT.Tanh, scale=0.5,
                               bias=half_b[:, ds(2 * i + 1, 1)]).then_inc(z_read[1], 1)
                hi(2 * i + 3, 1)
            act.wait_ge(zt_used, KC + 1)
            for t in range(2):
                n = T_K + t
                act.wait_ge(tile_done, n + 1)
                act.activation(zt[t][:, :], z[:, 2 * t, :], ACT.Identity, bias=par[:, n:n + 1]).then_inc(z_read[t], 1)
                hi(n + 2, t)
            for t in range(2):
                n = T_V + t
                act.wait_ge(tile_done, n + 1)
                act.wait_ge(roped, 2 * t + 2)
                act.activation(zt[t][:, :], z[:, 2 * t, :], ACT.Identity, bias=par[:, n:n + 1]).then_inc(z_read[t], 1)
                hi(n + 2, t)
            act.wait_ge(v_turned, 2)
            for vt in range(2):
                act.activation(vN[:, :, vt * P:vt * P + P], aux[:, 2 + vt, :].rearrange("p (n f) -> p n f", n=NB),
                               ACT.Copy).then_inc(v_ready, 1)
            with act.Fori(0, KD // 2) as i:
                for b in range(2):
                    n = 2 * i + T_Q + b
                    act.wait_ge(rope_part, 4 * i + 2 * b + 2 * N_KV - 2)
                    act.wait_ge(tile_done, n + 1)
                    act.activation(zt[b][:, :], z[:, 2 * b, :], ACT.Identity, bias=par[:, ds(n, 1)])\
                       .then_inc(z_read[b], 1)
                    hi(n + 2, b)

            def norm(tag, bufs, src, nk):
                s = lns[tag]
                for c in range(nk // 2):
                    act.wait_ge(s["centred"], c + 1)
                    if c >= 2:
                        act.wait_ge(s["sqsum"], c - 1)
                    act.activation(bufs["sq"][c % 2][:], src(2 * c), ACT.Square).then_inc(s["squared"], 1)
                act.wait_ge(s["var"], 1)
                act.activation(bufs["sd"][:, :], bufs["var"][:, :], ACT.Sqrt).then_inc(s["sd"], 1)

            norm("c", lnc, lambda k: uT[:, k:k + 2, 0:S], KC)
            for k in range(KC):
                act.wait_ge(lns["c"]["scaled"], k + 1)
                act.activation(uT[:, k, 0:S], uT[:, k, 0:S], ACT.Silu, scale=par[:, C_CLNG + k:C_CLNG + k + 1],
                               bias=par[:, C_CLNB + k:C_CLNB + k + 1]).then_inc(lns["c"]["done"], 1)

            units = [(g, n) for g in range(N_KV) for n in range(NB)]
            turned = [0]

            def exps(u):
                g, n = units[u]
                w = P if n == 0 else 2 * P
                act.wait_ge(maxed, u + 1)
                for j in range(4):
                    for e in range(2):
                        row = prob[u % 2][:, j, e, 0:1 + w]
                        m = act.activation(row, row, ACT.Exp, bias=smax[:, u % 2, 1, 2 * j + e:2 * j + e + 1],
                                           accum_out=smax[:, u % 2, 2, 2 * j + e:2 * j + e + 1])
                m.then_inc(exped, 1)

            def copies(u):
                g, n = units[u]
                w = 1 if n == 0 else 2
                if u:
                    act.wait_ge(pv_done, u)
                for t in range(2 * w):
                    act.wait_ge(p_turned, turned[0] + 1)
                    act.activation(prT[:, t, :], z[:, t % 3, :], ACT.Copy).then_inc(pT_ready, 1)
                    turned[0] += 1

            def heads_out(u):
                g, n = units[u]
                act.wait_ge(pv_done, u + 1)
                act.activation(mix[:, 4 * g:4 * g + 4, n * P:n * P + P],
                               z[:, 3, :].rearrange("p (j q) -> p j q", j=4), ACT.Copy).then_inc(y_ready, 1)

            act.wait_ge(lns["c"]["done"], KC)
            exps(0)
            for u in range(len(units)):
                copies(u)
                if u + 1 < len(units):
                    exps(u + 1)
                heads_out(u)

            act.wait_ge(p_turned, turned[0])
            act.wait_ge(y_ready, len(units))
            act.activation(u_hi[:], uT[:, 0:KC, 0:S], ACT.Copy).then_inc(u_hi_ready, 1)
            with act.Fori(0, 4) as i:
                for h in range(2):
                    for q in range(5):
                        o = 5 * h + q
                        b = o % 2
                        n = 10 * i + T_GATE + o
                        act.wait_ge(tile_done, n + 1)
                        if q < 4:
                            dst = (sig_a, sig_b)[q % 2][q // 2]
                            act.wait_ge(lo_ready, n + 2)
                            act.activation(dst[:, :], z[:, 2 * b, :], ACT.Sigmoid,
                                           bias=par[:, ds(8 * i + (T_GATE + 4 * h + q), 1)]).then_inc(z_read[b], 1)
                        hi(n + 2, b)
            for c in range(4):
                act.wait_ge(mixed, 4 * c + 4)
                act.activation(act_hi[:, 4 * c:4 * c + 4, :], mix[:, 4 * c:4 * c + 4, :], ACT.Copy)\
                   .then_inc(m_hi_ready, 1)
            with act.Fori(0, KD // 2) as i:
                for b in range(2):
                    n = 2 * i + T_MIX + b
                    act.wait_ge(tile_done, n + 1)
                    hi(n + 2, b)
            norm("1", ln1, lambda k: mix[:, k:k + 2, :], KD)
            for k in range(KD):
                act.wait_ge(x1_ready, k + 1)
                act.activation(act_hi[:, k, :], mix[:, k, :], ACT.Copy).then_inc(x1_hi_ready, 1)

            def exp_head(h):
                act.wait_ge(asked, h + 1)
                act.activation(expo[:, 1, :, :], expo[:, 0, :, :], ACT.Exp).then_inc(exp_ready, 1)

            for t in range(2 * HEADS_R):
                b, n = t % 2, T_ROUTE + t
                act.wait_ge(tile_done, n + 1)
                if t >= 2:
                    act.wait_ge(key_scored, t - 1)
                act.activation(rq[b][:, :], z[:, 2 * b, :], ACT.Copy).then_inc(z_read[b], 1)
                hi(n + 2, b)
                if t % 2 and t > 1:
                    exp_head(t // 2 - 1)

            def quad_copy(q):
                act.wait_ge(quad_done, q + 1)
                c, r = divmod(q, CG // 4)
                if r == 0 and c >= 2:
                    act.wait_ge(stage_out[c % 2], 16 * (c // 2))
                dst = stage[c % 2][:, :, 4 * r:4 * r + 4].rearrange("p k c -> p c k")
                act.activation(dst, aux[:, q % 4, :].rearrange("p (c k) -> p c k", c=4), ACT.Copy)\
                   .then_inc(quad_staged, 1)

            quads = 0
            for e in range(EG):
                if e == min(QUADS_OF) - 1:
                    exp_head(HEADS_R - 1)
                if e == min(QUADS_OF):
                    for m_, dst in enumerate((i_t[:, 0, :], i_t[:, 1, :], g_t[:, :])):
                        act.wait_ge(sel_turned, m_ + 1)
                        act.activation(dst, aux[:, m_, :], ACT.Copy).then_inc(sel_t_ready, 1)
                for _ in range(QUADS_OF.get(e, 0)):
                    quad_copy(quads)
                    quads += 1
                act.wait_ge(tile_done, T_PEER + e + 1)
                if e == 3:
                    act.wait_ge(sel_ready, HEADS_R)
                act.activation(hid_0[:, e, :], z[:, 2 * (e % 2), :], ACT.Gelu).then_inc(z_read[e % 2], 1)
                hi(T_PEER + e + 2, e % 2)
            for e in range(EG):
                act.wait_ge(gated_ready, e + 1)
                act.activation(a_hi[:, e, :], gated[e % 2][:, :], ACT.Copy).then_inc(a_hi_ready, 1)

            def group(g, last):
                n0 = GROUP_TILES * g + T_PEER
                for e in range(0 if isinstance(g, int) and g == 0 else EG):
                    b = e % 2
                    act.wait_ge(gated_ready, EG * g + e - 1)
                    act.wait_ge(tile_done, n0 + e + 1)
                    act.activation(hid[b][:, :], z[:, 2 * b, :], ACT.Gelu).then_inc(z_read[b], 1)
                    hi(n0 + e + 2, b)
                    act.wait_ge(gated_ready, EG * g + e + 1)
                    act.activation(a_hi[:, e, :], gated[b][:, :], ACT.Copy).then_inc(a_hi_ready, 1)
                for j in range(KD // 2):
                    if last and j >= KD // 2 - 2:
                        continue
                    act.wait_ge(tile_done, n0 + EG + j + 1)
                    hi(n0 + EG + j + 2, j % 2)

            group(0, False)
            with act.Fori(1, N_GROUPS - 1) as g:
                group(g, False)
            group(N_GROUPS - 1, True)
            norm("2", ln2, lambda k: mix[:, k:k + 2, :], KD)

        @block.vector
        def _(dve):
            links = [0]

            def link(ins):
                links[0] += 1
                ins.then_inc(chain, 1)
                dve.wait_ge(chain, links[0])

            def lo(n, b):
                dve.wait_ge(hi_ready, n + 1)
                dve.tensor_tensor(w_lo[b][:], raw[b][:], w_hi[b][:].bitcast(F32), ALU.subtract).then_inc(lo_ready, 1)

            lo(0, 0)
            for c in range(4):
                dve.wait_ge(x_hi_ready, c + 1)
                dve.tensor_tensor(act_lo[:, 4 * c:4 * c + 4, :], mix[:, 4 * c:4 * c + 4, :],
                                  act_hi[:, 4 * c:4 * c + 4, :].bitcast(F32), ALU.subtract).then_inc(x_lo_ready, 1)
            lo(1, 1)
            dve.wait_ge(const_landed, 16 * 5)
            dve.wait_ge(pos_landed, 16)
            link(dve.tensor_copy(t2[0][:, :], posi[:, :]))
            link(dve.tensor_scalar(zt[0][:, :], t2[0][:, :], rope_m[:, 5 * P:5 * P + 1], None, ALU.mult))
            link(dve.tensor_scalar(t2[0][:, :], zt[0][:, :], float(1 / (2 * np.pi)), ROUNDER, ALU.mult, ALU.add))
            link(dve.tensor_scalar(t2[1][:, :], t2[0][:, :], ROUNDER, None, ALU.subtract))
            for c in (TWO_PI_A, TWO_PI_B, TWO_PI_C):
                link(dve.scalar_tensor_tensor(out=zt[0][:, :], in0=t2[1][:, :], scalar=-float(c), in1=zt[0][:, :],
                                              op0=ALU.mult, op1=ALU.add))
            dve.tensor_scalar(t1[0][:, :], zt[0][:, :], 3.1415925, -3.1415925, ALU.min, ALU.max)\
               .then_inc(angle_ready, 1)
            dve.wait_ge(angle_ready, 1)
            link(dve.scalar_tensor_tensor(out=t2[0][:, :], in0=t1[0][:, :], scalar=-1.0, in1=t1[0][:, :],
                                          op0=ALU.mult, op1=ALU.max))
            dve.tensor_scalar(t1[1][:, :], t2[0][:, :], -1.0, float(np.pi / 2), ALU.mult, ALU.add)\
               .then_inc(angle_ready, 1)
            dve.wait_ge(angle_ready, 2)
            dve.tensor_scalar(half_b[:, :], par[:, C_BIAS:C_BIAS + 2 * KC], 0.5, None, ALU.mult).then_inc(zt_used, 1)

            dve.wait_ge(pads_ready, 1)
            with dve.Fori(0, KC) as i:
                lo(2 * i + 2, 0)
                dve.wait_ge(z_read[0], i + 1)
                dve.wait_ge(z_read[1], i + 1)
                dve.scalar_tensor_tensor(out=uT[:, ds(i + 1, 1), PAD:SLOT].rearrange("p o s -> p (o s)"),
                                         in0=zt[1][:, :], scalar=1.0, in1=zt[0][:, :],
                                         op0=ALU.add, op1=ALU.mult).then_inc(zt_used, 1)
                lo(2 * i + 3, 1)

            dve.wait_ge(sincos_ready, 2)
            for kt in range(2):
                lo(T_K + kt + 2, kt)
            for g in range(N_KV):
                dve.wait_ge(k_rot, g + 1)
                a = 2 * (g % 2)
                dve.tensor_tensor(t1[0][:, :], aux[:, a + 1, :], sinT[:, :], ALU.mult).then_inc(rope_part, 1)
                dve.tensor_tensor(t2[0][:, :], aux[:, a, :], cosT[:, :], ALU.mult).then_inc(rope_part, 1)
                dve.wait_ge(rope_part, 2 * g + 2)
                m = dve.tensor_tensor(kT[:, g, :], t1[0][:, :], t2[0][:, :], ALU.add)
                m.then_inc(roped, 1)
                dve.wait_ge(roped, g + 1)
            for vt in range(2):
                lo(T_V + vt + 2, vt)

            def taps(i, a, b):
                for w in range(a, b):
                    src = uT[:, ds(i + 1, 1), w:w + S].rearrange("p o s -> p (o s)")
                    dst = uT[:, ds(i, 1), 0:S].rearrange("p o s -> p (o s)")
                    tap = par[:, ds(TAPS * i + C_TAPS + w, 1)]
                    if w == 0:
                        dve.wait_ge(tap_done, TAPS * i)
                        dve.tensor_scalar(dst, src, tap, par[:, ds(i + C_CONVB, 1)], ALU.mult, ALU.add)\
                           .then_inc(tap_done, 1)
                    else:
                        dve.wait_ge(tap_done, TAPS * i + w)
                        dve.scalar_tensor_tensor(out=dst, in0=src, scalar=tap, in1=dst,
                                                 op0=ALU.mult, op1=ALU.add).then_inc(tap_done, 1)

            dve.wait_ge(zt_used, KC + 1)
            with dve.Fori(0, KD // 2) as i:
                taps(i, 0, TAPS)
                for b in range(2):
                    dve.wait_ge(roped, 2 * i + b + N_KV - 1)
                    dve.wait_ge(q_rot, 2 * i + b + 1)
                    dve.tensor_tensor(t1[b][:, :], aux[:, b, :], sinT[:, :], ALU.mult).then_inc(rope_part, 1)
                    dve.tensor_tensor(t2[b][:, :], zt[b][:, :], cosT[:, :], ALU.mult).then_inc(rope_part, 1)
                    dve.wait_ge(rope_part, 4 * i + 2 * b + 2 * N_KV + 2)
                    dve.tensor_tensor(mix[:, ds(2 * i + b, 1), :].rearrange("p o s -> p (o s)"), t1[b][:, :],
                                      t2[b][:, :], ALU.add).then_inc(roped, 1)

            def norm(tag, bufs, src, nk, factor):
                s = lns[tag]
                dve.wait_ge(s["sum"], 1)
                link(dve.tensor_scalar(bufs["mean"][:, :], aux[:, 0, :], factor, None, ALU.mult))
                for c in range(nk // 2):
                    dve.tensor_tensor(src(2 * c), src(2 * c), bufs["mean"][:, :].unsqueeze(1).to_broadcast([P, 2, S]),
                                      ALU.subtract).then_inc(s["centred"], 1)
                dve.wait_ge(s["sqsum"], nk // 2)
                dve.tensor_scalar(bufs["var"][:, :], aux[:, 1, :], factor, EPS, ALU.mult, ALU.add).then_inc(s["var"], 1)
                dve.wait_ge(s["sd"], 1)
                link(dve.reciprocal(bufs["rs"][:, :], bufs["sd"][:, :]))
                link(dve.tensor_tensor(bufs["tt"][:, :], bufs["rs"][:, :], bufs["rs"][:, :], ALU.mult))
                link(dve.tensor_tensor(bufs["tt"][:, :], bufs["tt"][:, :], bufs["var"][:, :], ALU.mult))
                link(dve.tensor_scalar(bufs["tt"][:, :], bufs["tt"][:, :], -0.5, 1.5, ALU.mult, ALU.add))
                dve.tensor_tensor(bufs["rs"][:, :], bufs["rs"][:, :], bufs["tt"][:, :], ALU.mult).then_inc(s["rs"], 1)
                dve.wait_ge(s["rs"], 1)

            dve.wait_ge(tap_done, TAPS * KC)
            norm("c", lnc, lambda k: uT[:, k:k + 2, 0:S], KC, 1.0)
            for k in range(KC):
                dve.tensor_tensor(uT[:, k, 0:S], uT[:, k, 0:S], lnc["rs"][:, :], ALU.mult)\
                   .then_inc(lns["c"]["scaled"], 1)

            units = [(g, n) for g in range(N_KV) for n in range(NB)]

            def mask_and_max(u):
                g, n = units[u]
                w = P if n == 0 else 2 * P
                pr = prob[u % 2]
                if u == 0:
                    dve.wait_ge(lns["c"]["scaled"], KC)
                if u >= 2:
                    dve.wait_ge(p_turned, turned_upto(u - 2))
                dve.tensor_copy(pr[:, :, :, 0:1].rearrange("p j e o -> p (j e o)"),
                                par[:, C_SINK + 8 * g:C_SINK + 8 * g + 8]).then_inc(sink_in, 1)
                for j in range(4):
                    dve.wait_ge(scored, 4 * u + j + 1)
                    dve.scalar_tensor_tensor(
                        out=pr[:, j, :, 1:1 + w], in0=aux[:, 2 * (j % 2):2 * (j % 2) + 2, 0:w], scalar=SCALE,
                        in1=mask[:, 2 * P - w:2 * P].unsqueeze(1).to_broadcast([P, 2, w]),
                        op0=ALU.mult, op1=ALU.add).then_inc(masked, 1)
                dve.wait_ge(masked, 4 * u + 4)
                dve.wait_ge(sink_in, u + 1)
                link(dve.tensor_reduce(smax[:, u % 2, 0, :], pr[:, :, :, 0:1 + w].rearrange("p j e k -> p (j e) k"),
                                       AX, ALU.max))
                dve.tensor_scalar(smax[:, u % 2, 1, :], smax[:, u % 2, 0, :], -1.0, None, ALU.mult).then_inc(maxed, 1)

            def turned_upto(u):
                return sum(2 if n == 0 else 4 for g, n in units[:u + 1])

            def normalise(u):
                g, n = units[u]
                w = P if n == 0 else 2 * P
                dve.wait_ge(exped, u + 1)
                link(dve.reciprocal(smax[:, u % 2, 3, :], smax[:, u % 2, 2, :]))
                for j in range(4):
                    for e in range(2):
                        row = prob[u % 2][:, j, e, 1:1 + w]
                        m = dve.tensor_scalar(row, row, smax[:, u % 2, 3, 2 * j + e:2 * j + e + 1], None, ALU.mult)
                m.then_inc(p_ready, 1)

            mask_and_max(0)
            for u in range(len(units)):
                if u + 1 < len(units):
                    mask_and_max(u + 1)
                normalise(u)

            dve.wait_ge(lo_ready, POOL_Q[1] + 1)
            dve.wait_ge(u_hi_ready, 1)
            dve.tensor_tensor(u_lo[:], uT[:, 0:KC, 0:S], u_hi[:].bitcast(F32), ALU.subtract).then_inc(u_lo_ready, 1)
            with dve.Fori(0, 4) as i:
                for h in range(2):
                    for q in range(5):
                        o = 5 * h + q
                        b = o % 2
                        n = 10 * i + T_GATE + o
                        if q in (1, 3):
                            j = q // 2
                            row = mix[:, ds(4 * i + 2 * h + j, 1), :].rearrange("p o s -> p (o s)")
                            dve.wait_ge(z_read[b], 5 * i + (T_GATE + o - b) // 2 + 1)
                            dve.tensor_tensor(row, row, sig_b[j][:, :], ALU.mult).then_inc(gated_y, 1)
                        if q == 4:
                            for j in range(2):
                                if j == 0:
                                    dve.wait_ge(tile_done, n + 1)
                                    dve.wait_ge(z_read[1 - b], 5 * i + (T_GATE + o - 1 - (1 - b)) // 2 + 1)
                                m = dve.tensor_tensor(sig_a[j][:, :], sig_a[j][:, :], z[:, 2 * b + j, :], ALU.mult)
                                m.then_inc(*((z_read[b], 1) if j else (prod_y, 1)))
                            for j in range(2):
                                row = mix[:, ds(4 * i + 2 * h + j, 1), :].rearrange("p o s -> p (o s)")
                                if j == 0:
                                    dve.wait_ge(prod_y, 2 * i + h + 1)
                                    dve.wait_ge(z_read[b], 5 * i + (T_GATE + o - b) // 2 + 1)
                                    dve.wait_ge(gated_y, 4 * i + 2 * h + 2)
                                dve.tensor_tensor(row, row, sig_a[j][:, :], ALU.add).then_inc(mixed, 1)
                        lo(n + 2, b)
            for c in range(4):
                dve.wait_ge(m_hi_ready, c + 1)
                dve.tensor_tensor(act_lo[:, 4 * c:4 * c + 4, :], mix[:, 4 * c:4 * c + 4, :],
                                  act_hi[:, 4 * c:4 * c + 4, :].bitcast(F32), ALU.subtract).then_inc(m_lo_ready, 1)
            dve.wait_ge(m_lo_ready, 4)
            with dve.Fori(0, KD // 2) as i:
                for b in range(2):
                    n = 2 * i + T_MIX + b
                    dve.wait_ge(x_res_landed[b], 16 * i + 16)
                    dve.wait_ge(tile_done, n + 1)
                    dve.scalar_tensor_tensor(out=mix[:, ds(2 * i + b, 1), :].rearrange("p o s -> p (o s)"),
                                             in0=x_res[b][:, :], scalar=ALPHA, in1=z[:, 2 * b, :],
                                             op0=ALU.mult, op1=ALU.add).then_inc(z_read[b], 1)
                    lo(n + 2, b)
            norm("1", ln1, lambda k: mix[:, k:k + 2, :], KD, 0.5)
            for k in range(KD):
                link(dve.scalar_tensor_tensor(out=mix[:, k, :], in0=mix[:, k, :], scalar=par[:, C_LN1G + k:C_LN1G + k + 1],
                                              in1=ln1["rs"][:, :], op0=ALU.mult, op1=ALU.mult))
                dve.tensor_scalar(mix[:, k, :], mix[:, k, :], par[:, C_LN1B + k:C_LN1B + k + 1], None, ALU.add)\
                   .then_inc(x1_ready, 1)
                dve.wait_ge(x1_hi_ready, k + 1)
                dve.tensor_tensor(act_lo[:, k, :], mix[:, k, :], act_hi[:, k, :].bitcast(F32), ALU.subtract)\
                   .then_inc(x1_lo_ready, 1)
            dve.wait_ge(x1_lo_ready, KD)
            for c in range(4):
                dve.tensor_scalar(mix[:, 4 * c:4 * c + 4, :], mix[:, 4 * c:4 * c + 4, :], ALPHA, None, ALU.mult)\
                   .then_inc(acc_ready, 1)

            def top16(dst_v, dst_i, src, spare, last):
                for c in range(NB):
                    m = dve.max(dst_v[:, c, 0:8], src[:, c, :])
                link(m)
                for c in range(NB):
                    dve.max_index(dst_i[:, c, 0:8], dst_v[:, c, 0:8], src[:, c, :])
                for c in range(NB):
                    m = dve.match_replace(spare[:, c, :], dst_v[:, c, 0:8], src[:, c, :], NEG)
                    if c == NB - 1 and last is not None:
                        m.then_inc(last, 1)
                if last is None:
                    link(m)
                else:
                    takes[0] += 1
                    dve.wait_ge(last, takes[0])
                for c in range(NB):
                    m = dve.max(dst_v[:, c, 8:16], spare[:, c, :])
                link(m)
                for c in range(NB):
                    m = dve.max_index(dst_i[:, c, 8:16], dst_v[:, c, 8:16], spare[:, c, :])
                link(m)

            takes = [0]

            def combine(h):
                link(dve.tensor_copy(idxf[:], idx[:]))
                link(dve.tensor_tensor(cand[:].rearrange("p c (a b) -> p c a b", a=TOPK),
                                       val[:, 0, :, :].unsqueeze(3).to_broadcast([P, NB, TOPK, TOPK]),
                                       val[:, 1, :, :].unsqueeze(2).to_broadcast([P, NB, TOPK, TOPK]), ALU.add))
                top16(best, place, cand, cand2, None)
                dve.tensor_tensor(expo[:, 0, :, :], best[:], best[:, :, 0:1].to_broadcast([P, NB, TOPK]), ALU.subtract)\
                   .then_inc(asked, 1)
                dve.tensor_scalar(digit[:, 0, :, :], place[:], 4, None, ALU.logical_shift_right)
                link(dve.tensor_scalar(digit[:, 1, :, :], place[:], 15, None, ALU.bitwise_and))
                link(dve.tensor_copy(digitf[:], digit[:].rearrange("p d c k -> p d (c k)")))
                for d in range(2):
                    dve.tensor_tensor(pick[:, d, :, :], digitf[:, d, :].unsqueeze(2).to_broadcast([P, NB * TOPK, TOPK]),
                                      iota[:, 0:TOPK].unsqueeze(1).to_broadcast([P, NB * TOPK, TOPK]), ALU.is_equal)\
                       .then_inc(picked, 1)

            def keep(h):
                for d in range(2):
                    dve.wait_ge(pick_scaled, 2 * h + d + 1)
                    dve.tensor_reduce(sel_i[:, d, :, h * TOPK:h * TOPK + TOPK],
                                      pick[:, d, :, :].rearrange("p (c k) a -> p c k a", c=NB), AX, ALU.add)
                dve.wait_ge(exp_ready, h + 1)
                link(dve.tensor_reduce(esum[:, 0, :], expo[:, 1, :, :], AX, ALU.add))
                link(dve.reciprocal(esum[:, 1, :], esum[:, 0, :]))
                dve.tensor_tensor(sel_g[:, :, h * TOPK:h * TOPK + TOPK], expo[:, 1, :, :],
                                  esum[:, 1, :].unsqueeze(2).to_broadcast([P, NB, TOPK]), ALU.mult)\
                   .then_inc(sel_ready, 1)
                dve.wait_ge(sel_ready, h + 1)

            for t in range(2 * HEADS_R):
                dve.wait_ge(key_scored, t + 1)
                top16(val[:, t % 2, :, :], idx[:, t % 2, :, :],
                      aux[:, t % 2, :].rearrange("p (c k) -> p c k", c=NB), rest, keys_taken)
                if t % 2:
                    combine(t // 2)
                elif t:
                    keep(t // 2 - 1)
            keep(HEADS_R - 1)

            dve.wait_ge(sel_t_ready, 3)
            for q in range(S // 4):
                if q >= 4:
                    dve.wait_ge(quad_done, q - 3)
                for hot, half_ in ((hot1, 0), (hot2, 1)):
                    dve.tensor_tensor(hot[:, 4 * (q % 4):4 * (q % 4) + 4, :], iota[:, :].unsqueeze(1).to_broadcast([P, 4, P]),
                                      i_t[:, half_, 4 * q:4 * q + 4].unsqueeze(2).to_broadcast([P, 4, P]),
                                      ALU.is_equal).then_inc(hot_matched, 1)

            def group(g, last):
                n0 = GROUP_TILES * g + T_PEER
                first = isinstance(g, int) and g == 0
                dve.wait_ge(gate_landed, 16 * g + 16)
                for e in range(EG):
                    b = e % 2
                    dve.wait_ge(z_read[b], EG * g + T_PEER // 2 + e // 2 + 1)
                    if not (first and e < 2):
                        dve.wait_ge(a_lo_ready, EG * g + e - 1)
                    src = hid_0[:, e, :] if first else hid[b][:, :]
                    dve.tensor_tensor(gated[b][:, :].rearrange("p (c s) -> p c s", c=N_CG),
                                      src.rearrange("p (c s) -> p c s", c=N_CG),
                                      gate[:, :, e * CG:e * CG + CG], ALU.mult).then_inc(gated_ready, 1)
                    if not first:
                        lo(n0 + e + 2, b)
                    dve.wait_ge(a_hi_ready, EG * g + e + 1)
                    dve.tensor_tensor(a_lo[:, e, :], gated[b][:, :], a_hi[:, e, :].bitcast(F32), ALU.subtract)\
                       .then_inc(a_lo_ready, 1)
                if first:
                    dve.wait_ge(lo_ready, POOL_R[1] + 1)
                for j in range(KD // 2):
                    b = j % 2
                    dve.wait_ge(tile_done, n0 + EG + j + 1)
                    if isinstance(g, int) and g == 0:
                        dve.wait_ge(acc_ready, 4)
                    else:
                        dve.wait_ge(z_read[b], EG * g + (T_PEER + EG - GROUP_TILES + j - b) // 2 + 1)
                    for s_ in range(2):
                        k = 2 * j + s_
                        m = dve.tensor_tensor(mix[:, k, :], mix[:, k, :], z[:, 2 * b + s_, :], ALU.add)
                    m.then_inc(z_read[b], 1)
                    if not (last and j >= KD // 2 - 2):
                        lo(n0 + EG + j + 2, b)

            group(0, False)
            with dve.Fori(1, N_GROUPS - 1) as g:
                group(g, False)
            group(N_GROUPS - 1, True)
            norm("2", ln2, lambda k: mix[:, k:k + 2, :], KD, 0.5)
            for k in range(KD):
                link(dve.scalar_tensor_tensor(out=mix[:, k, :], in0=mix[:, k, :], scalar=par[:, C_LN2G + k:C_LN2G + k + 1],
                                              in1=ln2["rs"][:, :], op0=ALU.mult, op1=ALU.mult))
                dve.tensor_scalar(mix[:, k, :], mix[:, k, :], par[:, C_LN2B + k:C_LN2B + k + 1], None, ALU.add)\
                   .then_inc(out_ready, 1)

        @block.gpsimd
        def _(pool):
            pool.memset(uT[:, :, 0:PAD], 0.0).then_inc(pads_ready, 1)
            pool.memset(ones[:, :], 1.0 / CC).then_inc(ones_ready, 1)

            def lo(n, b):
                pool.wait_ge(hi_ready, n + 1)
                pool.tensor_tensor(w_lo[b][:], raw[b][:], w_hi[b][:].bitcast(F32), ALU.subtract).then_inc(lo_ready, 1)

            pool.wait_ge(lo_ready, POOL_Q[0])
            with pool.Fori(0, (POOL_Q[1] + 1 - POOL_Q[0]) // 2) as i:
                for b in range(2):
                    lo(2 * i + POOL_Q[0] + b, b)

            def scale_pick(h):
                for d in range(2):
                    v4 = pick[:, d, :, :].rearrange("p (c k) a -> p c k a", c=NB)
                    pool.wait_ge(picked, 2 * h + d + 1)
                    pool.tensor_tensor(v4, v4, idxf[:, d, :, :].unsqueeze(2).to_broadcast([P, NB, TOPK, TOPK]),
                                       ALU.mult).then_inc(pick_scaled, 1)

            pool.wait_ge(lo_ready, POOL_R[0])
            for t in range(2 * HEADS_R + 2):
                if t >= 3 and t % 2:
                    scale_pick(t // 2 - 1)
                lo(T_ROUTE + t + 2, t % 2)

            quads = 0
            for e in range(2, EG):
                if e == min(QUADS_OF):
                    pool.wait_ge(sel_t_ready, 3)
                for _ in range(QUADS_OF.get(e, 0)):
                    s_ = 4 * (quads % 4)
                    pool.wait_ge(hot_matched, 2 * quads + 2)
                    pool.tensor_tensor(hot1[:, s_:s_ + 4, :], hot1[:, s_:s_ + 4, :],
                                       g_t[:, 4 * quads:4 * quads + 4].unsqueeze(2).to_broadcast([P, 4, P]),
                                       ALU.mult).then_inc(hot_ready, 1)
                    quads += 1
                lo(T_PEER + e + 2, e % 2)


def _constants():
    c = np.zeros((P, N_CONST), np.float32)
    r = np.arange(P)
    c[:, K_IDENT:K_IDENT + P] = np.eye(P)
    c[:, K_IOTA:K_IOTA + P] = r
    c[:, K_MASK:K_MASK + P] = np.where(r[None, :] > r[:, None], 0.0, NEG)
    c[:, K_MASK + P:K_MASK + 2 * P] = np.where(r[None, :] <= r[:, None], 0.0, NEG)
    rot = np.zeros((P, P), np.float32)
    for m in range(P):
        if m % HEAD < ROT // 2:
            rot[m + ROT // 2, m] = -1.0
        elif m % HEAD < ROT:
            rot[m - ROT // 2, m] = 1.0
    c[:, K_ROT:K_ROT + P] = rot
    for g in range(2):
        for m in range(P):
            c[64 * g + m % 64, K_DUP + P * g + m] = 1.0
            c[64 * g:64 * g + 64, K_RDUP + P * g + m] = rot[0:64, m % 64]
    freq = np.float32(THETA) ** (-np.arange(0, ROT, 2, dtype=np.float32) / np.float32(ROT))
    c[:, K_FREQ] = [freq[m % HEAD % (ROT // 2)] if m % HEAD < ROT else 0.0 for m in range(P)]
    return c


def _tiles(w, n_in=KD):
    s = 16 // n_in
    t = w.reshape(n_in, P, -1, s, P).transpose(2, 1, 3, 0, 4)
    return np.ascontiguousarray(t).reshape(-1, P, 16 * P)


def _columns(v):
    return v.reshape(-1, P).T


def kernel(**inputs):
    import concourse.bacc as _bacc
    from concourse.bass_utils import run_bass_kernel_spmd as _run

    a = {k: np.asarray(v) for k, v in inputs.items()}
    nq, nk = KD, 2
    q0, k0 = 2 * KC, 2 * KC + nq
    v0, a0 = k0 + nk, k0 + 2 * nk
    order = [t for i in range(KC) for t in (i, KC + i)] + list(range(k0, a0)) + list(range(q0, k0))
    order += [t for j in range(KD) for t in (a0 + j, a0 + KD + j)]
    w_v = a["expert_v"][0].reshape(N_GROUPS, EG, P, KD // 2, 2, P).transpose(0, 3, 2, 4, 1, 5)
    params = np.concatenate([
        _columns(a["b_in"][0])[:, order],
        a["conv_dw_w"][0, :, 0, :].reshape(TAPS, KC, P).transpose(2, 1, 0).reshape(P, KC * TAPS),
        _columns(a["conv_dw_b"][0]), _columns(a["conv_ln_g"][0]), _columns(a["conv_ln_b"][0]),
        np.broadcast_to(a["attn_sinks"][0][None, :], (P, N_HEADS)),
        _columns(a["ln1_g"][0]), _columns(a["ln1_b"][0]), _columns(a["ln2_g"][0]), _columns(a["ln2_b"][0]),
        a["sub_keys_1"][0].T, a["sub_keys_2"][0].T], axis=1)
    arrays = {
        "x_t": a["x"][0].T.reshape(KD, P, S).transpose(1, 0, 2),
        "pos": a["positions"],
        "w_in": _tiles(a["w_in"][0])[order],
        "w_conv": _tiles(a["w_conv_out"][0], KC),
        "w_mix": _tiles(a["w_mix_out"][0]),
        "w_route": _tiles(a["w_peer_q"][0]),
        "exp_u": _tiles(a["expert_u"][0].T),
        "exp_v": w_v.reshape(N_GROUPS * KD // 2, P, 16 * P),
        "params": params,
        "consts": _constants(),
    }
    arrays = {k: np.ascontiguousarray(v) for k, v in arrays.items()}
    nc = _bacc.Bacc("TRN2", target_bir_lowering=False, num_devices=1)
    args = [nc.dram_tensor(k, v.shape, mybir.dt.from_np(v.dtype), kind="ExternalInput").ap() for k, v in arrays.items()]
    args.append(nc.dram_tensor("gates", (N_CG, P, NKEY * CG), F32, kind="Internal").ap())
    args.append(nc.dram_tensor("out", (P, KD, S), F32, kind="ExternalOutput").ap())
    build(nc, *args)
    r = _run(nc, [arrays], core_ids=[0])
    return r.results[0]["out"].transpose(1, 0, 2).reshape(1, D, S).transpose(0, 2, 1)
```

```python
from contextlib import ExitStack

import numpy as np

import concourse.bass as bass
from concourse import mybir

F32 = mybir.dt.float32
F32R = mybir.dt.float32r
I32 = mybir.dt.int32
U32 = mybir.dt.uint32
ALU = mybir.AluOpType
ACT = mybir.ActivationFunctionType
AX = mybir.AxisListType.X
ds = bass.ds

P = 128
S = 512
D = 2048
KD = D // P
N_HEADS, N_KV, HEAD = 32, 4, 64
ROT = HEAD // 4
THETA = 500000.0
SCALE = HEAD ** -0.5
NB = S // P
CC = D // 2
KC = CC // P
TAPS = 31
PAD = TAPS - 1
SLOT = S + PAD
HEADS_R, NKEY, TOPK = 8, 128, 16
EPS = 1e-5
ALPHA = 2.0 ** 0.25
NEG = -3.0e38

T_GLU = 0
T_K = T_GLU + 2 * KC
T_V = T_K + 2
T_Q = T_V + 2
T_GB = T_Q + KD
T_GA = T_GB + KD
T_MIX = T_GA + KD + KD // 2
T_ROUTE = T_MIX + KD
T_PEER = T_ROUTE + 2 * HEADS_R
EG = 8
N_GROUPS = NKEY // EG
GROUP_TILES = EG + KD // 2
N_TILES = T_PEER + N_GROUPS * GROUP_TILES
CG = 16
N_CG = S // CG
QUADS_OF = {3: 48, 4: 48, 5: 32}
LOOP_Q = KD - 4
T_SLOT = T_Q + LOOP_Q
N_UNITS = N_KV * NB
N_SLOTS = T_GA - T_SLOT
POOL_A = (2, T_GA + 1)
POOL_R = (T_ROUTE + 2, T_PEER + EG + 1)

C_BIAS = 0
C_TAPS = C_BIAS + T_GA + KD
C_CONVB = C_TAPS + KC * TAPS
C_CLNG = C_CONVB + KC
C_CLNB = C_CLNG + KC
C_SINK = C_CLNB + KC
C_LN1G = C_SINK + N_HEADS
C_LN1B = C_LN1G + KD
C_LN2G = C_LN1B + KD
C_LN2B = C_LN2G + KD
C_KEYS = C_LN2B + KD
N_PARAM = C_KEYS + 2 * NKEY

K_IDENT, K_IOTA, K_MASK, K_ROT, K_DUP, K_RDUP = 0, 128, 256, 512, 640, 896
K_FREQ = 1152
N_CONST = 1153

TWO_PI_A = 6.28125
TWO_PI_B = 1.9340515136718750e-03
TWO_PI_C = 2 * np.pi - TWO_PI_A - TWO_PI_B
ROUNDER = 1.5 * 2.0 ** 23


def build(nc, x_t, pos, w_in, w_conv, w_mix, w_route, exp_u, exp_v, params, consts, gates, u_kept, out):
    with ExitStack() as ctx:
        base = -(-nc.sbuf_base // 32) * 32
        at = [base]

        def fixed(name, shape, dt):
            t = nc.alloc_sbuf_tensor_at(name, shape, dt, offset=at[0])
            at[0] += -(-4 * int(np.prod(shape[1:])) // 32) * 32
            return t

        act_hi = fixed("act_hi", [P, KD, S], F32R)
        act_lo = fixed("act_lo", [P, KD, S], F32R)
        mix = fixed("mix", [P, KD, S], F32)
        raw = [fixed(f"raw{i}", [P, 16, P], F32) for i in range(2)]
        w_hi = [fixed(f"w_hi{i}", [P, 16, P], F32R) for i in range(2)]
        w_lo = [fixed(f"w_lo{i}", [P, 16, P], F32R) for i in range(2)]
        ident = fixed("ident", [P, P], F32)
        iota = fixed("iota", [P, P], F32)
        ones = fixed("ones", [P, P], F32)
        par = fixed("par", [P, N_PARAM], F32)
        region = at[0]

        def shared(name, shape, dt, offset):
            return nc.alloc_sbuf_tensor_at(name, shape, dt, offset=region + offset)

        uT = shared("uT", [P, KC + 1, SLOT], F32, 0)
        kT = shared("kT", [P, N_KV, S], F32, 19520)
        vN = shared("vN", [P, NB, N_KV * HEAD], F32, 27712)
        mask = shared("mask", [P, 2 * P], F32, 31808)
        rope_m = shared("rope_m", [P, 5 * P + 1], F32, 32832)
        cosT = shared("cosT", [P, S], F32, 35424)
        sinT = shared("sinT", [P, S], F32, 37472)
        zt = [shared(f"zt{i}", [P, S], F32, 39520 + 2048 * i) for i in range(2)]
        t1 = [shared(f"t1_{i}", [P, S], F32, 43616 + 2048 * i) for i in range(2)]
        t2 = [shared(f"t2_{i}", [P, S], F32, 47712 + 2048 * i) for i in range(2)]
        half_b = shared("half_b", [P, 2 * KC], F32, 51808)
        posi = shared("posi", [P, S], I32, 51872)
        lnc_mean = shared("lnc_mean", [P, S], F32, 51872)
        lnc_tt = shared("lnc_tt", [P, S], F32, 51872)
        lnc_sq = [shared("lnc_sq0", [P, S], F32, 17344), shared("lnc_sq1", [P, S], F32, 53920)]
        lnc_var = shared("lnc_var", [P, S], F32, 53920)
        lnc_sd = shared("lnc_sd", [P, S], F32, 55968)
        lnc_rs = shared("lnc_rs", [P, S], F32, 58016)
        prob = [shared(f"prob{i}", [P, 4, 2, 2 * P + 1], F32, 8224 * i) for i in range(2)]
        prT = shared("prT", [P, 4, S], F32, 51872)
        smax = shared("smax", [P, 2, 4, 8], F32, 60064)
        sig_b = [shared(f"sig_b{i}", [P, S], F32, 35904 + 2048 * i) for i in range(2)]
        u_back = shared("u_back", [P, KC, S], F32, 0)
        u_lo = shared("u_lo", [P, KC, S], F32R, 0)
        u_hi = shared("u_hi", [P, KC, S], F32R, 19520)
        sig_a = [shared(f"sig_a{i}", [P, S], F32, 40000 + 2048 * i) for i in range(2)]

        def ln_buffers(tag, offset):
            names = ("mean", "var", "sd", "rs", "tt")
            b = {m: shared(f"{tag}_{m}", [P, S], F32, offset + 2048 * i) for i, m in enumerate(names)}
            b["sq"] = [shared(f"{tag}_sq{i}", [P, 2, S], F32, offset + 10240 + 4096 * i) for i in range(2)]
            return b

        ln1 = ln_buffers("ln1", 4096)
        ln2 = ln_buffers("ln2", 4096)
        x_res = [shared(f"x_res{i}", [P, S], F32, 44096 + 2048 * i) for i in range(2)]
        rq = [shared(f"rq{i}", [P, S], F32, 22528 + 2048 * i) for i in range(2)]
        rest = shared("rest", [P, NB, NKEY], F32, 0)
        val = shared("val", [P, 2, NB, TOPK], F32, 2048)
        idx = shared("idx", [P, 2, NB, TOPK], U32, 2560)
        idxf = shared("idxf", [P, 2, NB, TOPK], F32, 3072)
        cand = shared("cand", [P, NB, TOPK * TOPK], F32, 3584)
        cand2 = shared("cand2", [P, NB, TOPK * TOPK], F32, 7680)
        best = shared("best", [P, NB, TOPK], F32, 11776)
        place = shared("place", [P, NB, TOPK], U32, 12032)
        digit = shared("digit", [P, 2, NB, TOPK], U32, 12288)
        digitf = shared("digitf", [P, 2, NB * TOPK], F32, 12800)
        expo = shared("expo", [P, 2, NB, TOPK], F32, 13312)
        esum = shared("esum", [P, 2, NB], F32, 13824)
        pick = shared("pick", [P, 2, NB * TOPK, TOPK], F32, 26624)
        sel_i = shared("sel_i", [P, 2, NB, P], F32, 34816)
        sel_g = shared("sel_g", [P, NB, P], F32, 38912)
        hot2 = shared("hot2", [P, 16, P], F32, 0)
        hot1 = shared("hot1", [P, 16, P], F32, 8192)
        i_t = shared("i_t", [P, 2, S], F32, 53248)
        g_t = shared("g_t", [P, S], F32, 57344)
        stage = [shared(f"stage{i}", [P, NKEY, CG], F32, 32768 + 8192 * i) for i in range(2)]
        a_hi = shared("a_hi", [P, EG, S], F32R, 0)
        a_lo = shared("a_lo", [P, EG, S], F32R, 16384)
        hid_0 = shared("hid_0", [P, EG, S], F32, 16384)
        gate = shared("gate", [P, N_CG, EG * CG], F32, 32768)
        hid = [shared(f"hid{i}", [P, S], F32, 49152 + 2048 * i) for i in range(2)]
        gated = [shared(f"gated{i}", [P, S], F32, 53248 + 2048 * i) for i in range(2)]

        z = ctx.enter_context(nc.psum_tensor("z", [P, 4, S], F32))
        aux = ctx.enter_context(nc.psum_tensor("aux", [P, 4, S], F32))

        def sem(name):
            return ctx.enter_context(nc.semaphore(name))

        w_landed = [sem("w_landed0"), sem("w_landed1")]
        hi_ready, lo_ready, tile_done = sem("hi_ready"), sem("lo_ready"), sem("tile_done")
        z_read = [sem("z_read0"), sem("z_read1")]
        x_landed = [sem(f"x_landed{i}") for i in range(4)]
        const_landed, pos_landed = sem("const_landed"), sem("pos_landed")
        x_hi_ready, x_lo_ready = sem("x_hi_ready"), sem("x_lo_ready")
        pads_ready, ones_ready = sem("pads_ready"), sem("ones_ready")
        angle_ready, sincos_ready = sem("angle_ready"), sem("sincos_ready")
        zt_used, k_rot = sem("zt_used"), sem("k_rot")
        v_turned, v_ready = sem("v_turned"), sem("v_ready")
        q_rot, rope_part, roped, tap_done = sem("q_rot"), sem("rope_part"), sem("roped"), sem("tap_done")
        lns = {}
        for tag in ("c", "1", "2"):
            lns[tag] = {m: sem(f"ln{tag}_{m}") for m in
                        ("sum", "centred", "squared", "sqsum", "var", "sd", "rs", "scaled", "done")}
        scored, masked, maxed, exped = sem("scored"), sem("masked"), sem("maxed"), sem("exped")
        sink_in, p_ready, p_turned, pT_ready = sem("sink_in"), sem("p_ready"), sem("p_turned"), sem("pT_ready")
        pv_done, y_ready = sem("pv_done"), sem("y_ready")
        u_stored, u_landed = sem("u_stored"), sem("u_landed")
        u_hi_ready, u_lo_ready, gated_y, prod_y, mixed = (sem("u_hi_ready"), sem("u_lo_ready"), sem("gated_y"),
                                                          sem("prod_y"), sem("mixed"))
        m_hi_ready, m_lo_ready = sem("m_hi_ready"), sem("m_lo_ready")
        x_res_landed = [sem("x_res_landed0"), sem("x_res_landed1")]
        x1_ready, x1_hi_ready, x1_lo_ready, acc_ready = (sem("x1_ready"), sem("x1_hi_ready"), sem("x1_lo_ready"),
                                                         sem("acc_ready"))
        key_scored, keys_taken, chain, asked, exp_ready = (sem("key_scored"), sem("keys_taken"), sem("chain"),
                                                           sem("asked"), sem("exp_ready"))
        picked, pick_scaled = sem("picked"), sem("pick_scaled")
        sel_ready, sel_turned, sel_t_ready = sem("sel_ready"), sem("sel_turned"), sem("sel_t_ready")
        hot_matched = sem("hot_matched")
        hot_ready, quad_done, quad_staged = sem("hot_ready"), sem("quad_done"), sem("quad_staged")
        stage_out = [sem("stage_out0"), sem("stage_out1")]
        gate_landed, hid_ready, gated_ready = sem("gate_landed"), sem("hid_ready"), sem("gated_ready")
        a_hi_ready, a_lo_ready = sem("a_hi_ready"), sem("a_lo_ready")
        out_ready, out_stored = sem("out_ready"), sem("out_stored")

        block = ctx.enter_context(nc.Block())
        gates_r = gates.rearrange("c p (g f) -> p c g f", f=EG * CG)

        @block.sync
        def _(sp):
            def load(n, b, src):
                if not (isinstance(n, int) and n < 2):
                    sp.wait_ge(lo_ready, n - 1)
                sp.dma_start(raw[b][:].rearrange("p k c -> p (k c)"), src).then_inc(w_landed[b], 16)

            load(0, 0, w_in[0])
            for c in range(4):
                sp.dma_start(mix[:, 4 * c:4 * c + 4, :], x_t[:, 4 * c:4 * c + 4, :]).then_inc(x_landed[c], 16)
            load(1, 1, w_in[1])
            for dst, a, b in ((ident, K_IDENT, K_IOTA), (iota, K_IOTA, K_MASK), (mask, K_MASK, K_ROT),
                              (rope_m, K_ROT, N_CONST)):
                sp.dma_start(dst[:, :], consts[:, a:b]).then_inc(const_landed, 16)
            sp.dma_start(par[:, :], params).then_inc(const_landed, 16)
            sp.dma_start(posi[:, :], pos.to_broadcast([P, S])).then_inc(pos_landed, 16)
            pair = w_in.rearrange("(a b) p f -> a b p f", b=2)
            with sp.Fori(1, T_GA // 2) as i:
                for b in range(2):
                    load(2 * i + b, b, pair[i, b])
            ga = w_in[T_GA:, :, :].rearrange("(i h q) p f -> i h q p f", h=2, q=2)
            conv = w_conv.rearrange("(i h) p f -> i h p f", h=2)
            with sp.Fori(0, KD // 4) as i:
                for h in range(2):
                    for q in range(3):
                        o = 3 * h + q
                        load(6 * i + T_GA + o, o % 2, ga[i, h, q] if q < 2 else conv[i, h])
            wm = w_mix.rearrange("(a b) p f -> a b p f", b=2)
            xr = x_t.rearrange("p (a b) s -> a b p s", b=2)
            for b in range(2):
                load(T_MIX + b, b, wm[0, b])
                sp.dma_start(x_res[b][:, :], xr[0, b]).then_inc(x_res_landed[b], 16)
            with sp.Fori(1, KD // 2) as i:
                for b in range(2):
                    load(2 * i + T_MIX + b, b, wm[i, b])
                    sp.wait_ge(z_read[b], i + T_MIX // 2)
                    sp.dma_start(x_res[b][:, :], xr[i, b]).then_inc(x_res_landed[b], 16)
            wr = w_route.rearrange("(a b) p f -> a b p f", b=2)
            with sp.Fori(0, HEADS_R) as i:
                for b in range(2):
                    load(2 * i + T_ROUTE + b, b, wr[i, b])
            u = exp_u.rearrange("(g e) p f -> g e p f", e=EG)
            v = exp_v.rearrange("(g e) p f -> g e p f", e=KD // 2)
            for e in range(EG - 1):
                load(T_PEER + e, e % 2, u[0, e])
            c = 0
            for e, quads in QUADS_OF.items():
                for _ in range(4 * quads // CG):
                    sp.wait_ge(quad_staged, CG // 4 * (c + 1))
                    sp.dma_start(gates[c], stage[c % 2][:].rearrange("p k c -> p (k c)")).then_inc(stage_out[c % 2], 16)
                    c += 1
                if c == N_CG:
                    sp.wait_ge(stage_out[0], 16 * (N_CG // 2))
                    sp.wait_ge(stage_out[1], 16 * (N_CG // 2))
                    sp.dma_start(gate[:], gates_r[:, :, 0, :]).then_inc(gate_landed, 16)
                n = T_PEER + e + 4
                load(n, n % 2, u[0, e + 4] if e + 4 < EG else v[0, e + 4 - EG])

            def group(g, first, last):
                n = GROUP_TILES * g + T_PEER
                for e in range(0 if first else EG):
                    load(n + e, e % 2, u[g, e])
                for e in range(2 if first else 0, KD // 2):
                    load(n + EG + e, e % 2, v[g, e])
                    if e == 2 and not last:
                        sp.wait_ge(gated_ready, EG * g + EG)
                        sp.dma_start(gate[:], gates_r[:, :, g + 1, :]).then_inc(gate_landed, 16)

            group(0, True, False)
            with sp.Fori(1, N_GROUPS - 1) as g:
                group(g, False, False)
            group(N_GROUPS - 1, False, True)
            for k in range(KD):
                sp.wait_ge(out_ready, k + 1)
                sp.dma_start(out[:, k, :], mix[:, k, :]).then_inc(out_stored, 16)
            sp.wait_ge(out_stored, 16 * KD)

        @block.tensor
        def _(pe):
            def tile(n, b, hi, lo, ready=None):
                pe.wait_ge(hi_ready, n + 1)
                pe.wait_ge(lo_ready, n + 1)
                if not (isinstance(n, int) and n < 2):
                    pe.wait_ge(z_read[b], half(n, b))
                for k in range(KD):
                    if ready:
                        ready(k)
                    pe.matmul(z[:, 2 * b, :], w_hi[b][:, k, :], hi[:, k, :], start=k == 0, stop=False)
                    pe.matmul(z[:, 2 * b, :], w_hi[b][:, k, :], lo[:, k, :], start=False, stop=False)
                    m = pe.matmul(z[:, 2 * b, :], w_lo[b][:, k, :], hi[:, k, :], start=False, stop=k == KD - 1)
                m.then_inc(tile_done, 1)

            def tile2(n, b, hi, lo, ready=None):
                pe.wait_ge(hi_ready, n + 1)
                pe.wait_ge(lo_ready, n + 1)
                pe.wait_ge(z_read[b], half(n, b))
                for s in range(2):
                    for k in range(8):
                        if ready and s == 0:
                            ready(k)
                        pe.matmul(z[:, 2 * b + s, :], w_hi[b][:, 8 * s + k, :], hi[:, k, :], start=k == 0, stop=False)
                        pe.matmul(z[:, 2 * b + s, :], w_hi[b][:, 8 * s + k, :], lo[:, k, :], start=False, stop=False)
                        m = pe.matmul(z[:, 2 * b + s, :], w_lo[b][:, 8 * s + k, :], hi[:, k, :],
                                      start=False, stop=k == 7)
                m.then_inc(tile_done, 1)

            def half(n, b):
                return n // 2 if isinstance(n, int) else n.half

            class Tile:
                def __init__(self, i, per, base, b):
                    self.n, self.half = 2 * per * i + base + b, per * i + base // 2

                def __add__(self, k):
                    return self.n + k

            def x_ready(k):
                if k % 4 == 0:
                    pe.wait_ge(x_hi_ready, k // 4 + 1)
                    pe.wait_ge(x_lo_ready, k // 4 + 1)

            tile(0, 0, act_hi, act_lo, x_ready)
            tile(1, 1, act_hi, act_lo)
            with pe.Fori(1, KC) as i:
                for b in range(2):
                    tile(Tile(i, 1, 0, b), b, act_hi, act_lo)
            pe.wait_ge(const_landed, 16 * 5)

            def keys(kt):
                pe.wait_ge(z_read[kt], T_K // 2 + 1)
                for g in range(2):
                    a, rot = 2 * g, 2 * g + 1
                    if kt:
                        pe.wait_ge(roped, g + 1)
                    pe.matmul(aux[:, a, :], rope_m[:, P * (1 + g):P * (2 + g)], zt[kt][:, :], start=True, stop=True)
                    pe.matmul(aux[:, rot, :], rope_m[:, P * (3 + g):P * (4 + g)], zt[kt][:, :],
                              start=True, stop=True).then_inc(k_rot, 1)

            def values(vt):
                pe.wait_ge(z_read[vt], T_V // 2 + 1)
                pe.wait_ge(roped, 4)
                for n in range(NB):
                    m = pe.transpose(aux[:, 2 + vt, n * P:n * P + P], zt[vt][:, n * P:n * P + P], ident[:, :])
                m.then_inc(v_turned, 1)

            tile(T_K, 0, act_hi, act_lo)
            tile(T_K + 1, 1, act_hi, act_lo)
            keys(0)
            pe.wait_ge(ones_ready, 1)
            pe.wait_ge(tap_done, TAPS * KC)
            for k in range(KC):
                m = pe.matmul(z[:, 1, :], ones[:, :], uT[:, k, 0:S], start=k == 0, stop=k == KC - 1)
            m.then_inc(lns["c"]["sum"], 1)
            tile(T_V, 0, act_hi, act_lo)
            keys(1)
            tile(T_V + 1, 1, act_hi, act_lo)
            values(0)
            for k in range(KC):
                pe.wait_ge(lns["c"]["squared"], k + 1)
                pe.matmul(z[:, 3, :], ones[:, :], lnc_sq[k % 2][:, :], start=k == 0, stop=k == KC - 1)\
                  .then_inc(lns["c"]["sqsum"], 1)
            values(1)

            with pe.Fori(0, LOOP_Q // 2) as i:
                for b in range(2):
                    tile(Tile(i, 1, T_Q, b), b, act_hi, act_lo)
                for b in range(2):
                    pe.wait_ge(z_read[b], i + T_Q // 2 + 1)
                    pe.wait_ge(rope_part, 4 * i + 2 * b + 2 * N_KV - 3)
                    pe.matmul(aux[:, b, :], rope_m[:, 0:P], zt[b][:, :], start=True, stop=True).then_inc(q_rot, 1)

            def norm_sum(tag, src, nk, ready):
                for k in range(nk):
                    ready(k)
                    m = pe.matmul(aux[:, 0, :], ones[:, :], src(k), start=k == 0, stop=k == nk - 1)
                m.then_inc(lns[tag]["sum"], 1)

            def norm_sq(tag, sq, nk):
                for c in range(nk // 2):
                    pe.wait_ge(lns[tag]["squared"], c + 1)
                    for k in range(2):
                        m = pe.matmul(aux[:, 1, :], ones[:, :], sq[c % 2][:, k, :],
                                      start=c + k == 0, stop=2 * c + k == nk - 1)
                    m.then_inc(lns[tag]["sqsum"], 1)

            units = [(g, n) for g in range(N_KV) for n in range(NB)]

            def scores(u, j):
                g, n = units[u]
                lo_c, w = max(n - 1, 0) * P, P if n == 0 else 2 * P
                if n == 0 and j == 0:
                    pe.wait_ge(roped, N_KV + max(4 * g + 4, LOOP_Q))
                if u or j:
                    pe.wait_ge(masked, 4 * u + j)
                for e in range(2):
                    m = pe.matmul(aux[:, e, 0:w], mix[64 * e:64 * e + 64, 4 * g + j, n * P:n * P + P],
                                  kT[64 * e:64 * e + 64, g, lo_c:lo_c + w], start=True, stop=True)
                m.then_inc(scored, 1)

            def turned_before(u):
                return sum(2 if n == 0 else 4 for g, n in units[:u])

            def turn(u, t):
                g, n = units[u]
                w = 1 if n == 0 else 2
                e, kb = t // w, t % w
                if t == 0:
                    pe.wait_ge(p_ready, u + 1)
                before = turned_before(u) + t - 1
                if before >= 1:
                    pe.wait_ge(pT_ready, before)
                else:
                    pe.wait_ge(v_ready, 2)
                for j in range(4):
                    m = pe.transpose(aux[:, 2 + t % 2, j * P:j * P + P],
                                     prob[u % 2][:, j, e, 1 + kb * P:1 + kb * P + P], ident[:, :])
                m.then_inc(p_turned, 1)

            def values_out(u, e):
                g, n = units[u]
                w = 1 if n == 0 else 2
                if u and e == 0:
                    pe.wait_ge(y_ready, u)
                for kb in range(w):
                    pe.wait_ge(pT_ready, turned_before(u) + w * e + kb + 1)
                    m = pe.matmul(z[64 * e:64 * e + 64, 1, :], vN[:, n - w + 1 + kb, g * HEAD:g * HEAD + HEAD],
                                  prT[:, w * e + kb, :], start=kb == 0, stop=kb == w - 1)
                if e == 1:
                    m.then_inc(pv_done, 1)

            def rotate(q):
                pe.wait_ge(z_read[q % 2], (T_Q + q) // 2 + 1)
                if q == LOOP_Q:
                    pe.wait_ge(lns["c"]["var"], 1)
                else:
                    pe.wait_ge(rope_part, 2 * N_KV + 2 * q - 1)
                pe.matmul(z[:, 3, :], rope_m[:, 0:P], zt[q % 2][:, :], start=True, stop=True).then_inc(q_rot, 1)

            for s in range(N_SLOTS):
                def beside(k):
                    if s < N_UNITS and k in (1, 4, 7, 10):
                        scores(s, k // 3)
                    if 1 <= s <= N_UNITS and k >= 11:
                        t = {11: 0, 12: 1, 14: 2, 15: 3}.get(k)
                        if t is not None and t < (2 if units[s - 1][1] == 0 else 4):
                            turn(s - 1, t)
                    if 2 <= s < N_UNITS + 2 and k in (2, 5):
                        values_out(s - 2, k // 3)
                    if 1 <= s <= KD - LOOP_Q and k == 8:
                        rotate(LOOP_Q + s - 1)
                tile(T_SLOT + s, s % 2, act_hi, act_lo, beside)

            with pe.Fori(0, KD // 4) as i:
                for h in range(2):
                    for q in range(3):
                        o = 3 * h + q
                        n = Tile(i, 3, T_GA + o - o % 2, o % 2)
                        if q < 2:
                            tile(n, o % 2, act_hi, act_lo)
                        else:
                            pe.wait_ge(u_hi_ready, 1)
                            pe.wait_ge(u_lo_ready, 1)
                            tile2(n, o % 2, u_hi, u_lo)

            def m_ready(k):
                if k % 4 == 0:
                    pe.wait_ge(m_hi_ready, k // 4 + 1)
                    pe.wait_ge(m_lo_ready, k // 4 + 1)

            tile(T_MIX, 0, act_hi, act_lo, m_ready)
            tile(T_MIX + 1, 1, act_hi, act_lo)
            with pe.Fori(1, KD // 2) as i:
                for b in range(2):
                    tile(Tile(i, 1, T_MIX, b), b, act_hi, act_lo)
            norm_sum("1", lambda k: mix[:, k, :], KD, lambda k: pe.wait_ge(z_read[k % 2], (T_MIX + k) // 2 + 1))
            norm_sq("1", ln1["sq"], KD)

            def key_scores(t):
                pe.wait_ge(z_read[t % 2], (T_ROUTE + t) // 2 + 1)
                if t >= 2:
                    pe.wait_ge(keys_taken, t - 1)
                for c in range(NB):
                    m = pe.matmul(aux[:, t % 2, c * P:c * P + P], rq[t % 2][:, c * P:c * P + P],
                                  par[:, C_KEYS + (t % 2) * NKEY:C_KEYS + (t % 2 + 1) * NKEY], start=True, stop=True)
                m.then_inc(key_scored, 1)

            def x1_block(k):
                pe.wait_ge(x1_hi_ready, k + 1)
                pe.wait_ge(x1_lo_ready, k + 1)

            for t in range(2 * HEADS_R):
                tile(T_ROUTE + t, t % 2, act_hi, act_lo, x1_block if t == 0 else None)
                if t:
                    key_scores(t - 1)

            def turn_chosen():
                pe.wait_ge(sel_ready, HEADS_R)
                for m_, src in enumerate((lambda c: sel_i[:, 0, c, :], lambda c: sel_i[:, 1, c, :],
                                          lambda c: sel_g[:, c, :])):
                    for c in range(NB):
                        m = pe.transpose(aux[:, m_, c * P:c * P + P], src(c), ident[:, :])
                    m.then_inc(sel_turned, 1)

            def quad_mm(q):
                pe.wait_ge(hot_ready, q + 1)
                if q >= 4:
                    pe.wait_ge(quad_staged, q - 3)
                else:
                    pe.wait_ge(sel_t_ready, 3)
                for c in range(4):
                    s_ = 4 * (q % 4) + c
                    m = pe.matmul(aux[:, q % 4, c * P:c * P + P], hot2[:, s_, :], hot1[:, s_, :],
                                  start=True, stop=True)
                m.then_inc(quad_done, 1)

            quads = [0]
            for e in range(EG):
                first_k = 4 if e == min(QUADS_OF) else 0
                per_k = QUADS_OF.get(e, 0) // (KD - first_k)

                def beside(k):
                    if e == 0 and k == 2:
                        key_scores(2 * HEADS_R - 1)
                    if e == min(QUADS_OF) and k == 0:
                        turn_chosen()
                    if k >= first_k:
                        for _ in range(per_k):
                            quad_mm(quads[0])
                            quads[0] += 1
                tile(T_PEER + e, e % 2, act_hi, act_lo, beside)

            def outputs(g):
                for j in range(KD // 2):
                    def a_ready(k):
                        if j == 0:
                            pe.wait_ge(a_hi_ready, EG * g + k + 1)
                            pe.wait_ge(a_lo_ready, EG * g + k + 1)
                    n = T_PEER + EG + j if isinstance(g, int) else Tile(g, EG, T_PEER + EG + j - j % 2, j % 2)
                    tile2(n, j % 2, a_hi, a_lo, a_ready)

            outputs(0)
            with pe.Fori(1, N_GROUPS) as g:
                for e in range(EG):
                    tile(Tile(g, EG, T_PEER + e - e % 2, e % 2), e % 2, act_hi, act_lo)
                outputs(g)
            norm_sum("2", lambda k: mix[:, k, :], KD,
                     lambda k: pe.wait_ge(z_read[k // 2 % 2], (N_TILES - KD // 2 + k // 2) // 2 + 1))
            norm_sq("2", ln2["sq"], KD)

        @block.scalar
        def _(act):
            def hi(n, b):
                act.wait_ge(w_landed[b], 16 * (n // 2) + 16 if isinstance(n, int) else 8 * n + 16 - 8 * b)
                if not (isinstance(n, int) and n < 2):
                    act.wait_ge(tile_done, n - 1)
                act.activation(w_hi[b][:], raw[b][:], ACT.Copy).then_inc(hi_ready, 1)

            hi(0, 0)
            for c in range(4):
                act.wait_ge(x_landed[c], 16)
                act.activation(act_hi[:, 4 * c:4 * c + 4, :], mix[:, 4 * c:4 * c + 4, :], ACT.Copy)\
                   .then_inc(x_hi_ready, 1)
            hi(1, 1)
            act.wait_ge(angle_ready, 1)
            act.activation(sinT[:, :], t1[0][:, :], ACT.Sin).then_inc(sincos_ready, 1)
            act.wait_ge(angle_ready, 2)
            act.activation(cosT[:, :], t1[1][:, :], ACT.Sin).then_inc(sincos_ready, 1)

            with act.Fori(0, KC) as i:
                act.wait_ge(zt_used, i + 1)
                act.wait_ge(tile_done, 2 * i + 1)
                act.activation(zt[0][:, :], z[:, 0, :], ACT.Identity, scale=0.5,
                               bias=half_b[:, ds(2 * i, 1)]).then_inc(z_read[0], 1)
                hi(2 * i + 2, 0)
                act.wait_ge(tile_done, 2 * i + 2)
                act.activation(zt[1][:, :], z[:, 2, :], ACT.Tanh, scale=0.5,
                               bias=half_b[:, ds(2 * i + 1, 1)]).then_inc(z_read[1], 1)
                hi(2 * i + 3, 1)
            act.wait_ge(zt_used, KC + 1)
            for t in range(2):
                n = T_K + t
                act.wait_ge(tile_done, n + 1)
                act.activation(zt[t][:, :], z[:, 2 * t, :], ACT.Identity, bias=par[:, n:n + 1]).then_inc(z_read[t], 1)
                hi(n + 2, t)
            lc = lns["c"]
            for t in range(2):
                n = T_V + t
                act.wait_ge(tile_done, n + 1)
                act.wait_ge(roped, 2 * t + 2)
                act.activation(zt[t][:, :], z[:, 2 * t, :], ACT.Identity, bias=par[:, n:n + 1]).then_inc(z_read[t], 1)
                hi(n + 2, t)
            for k in range(KC):
                act.wait_ge(lc["centred"], k + 1)
                if k >= 2:
                    act.wait_ge(lc["sqsum"], k - 1)
                act.activation(lnc_sq[k % 2][:, :], uT[:, k, 0:S], ACT.Square).then_inc(lc["squared"], 1)
            act.wait_ge(v_turned, 2)
            for vt in range(2):
                act.activation(vN[:, :, vt * P:vt * P + P], aux[:, 2 + vt, :].rearrange("p (n f) -> p n f", n=NB),
                               ACT.Copy).then_inc(v_ready, 1)

            def queries(q, n, b, bias):
                act.wait_ge(rope_part, 2 * q + 2 * N_KV - 2)
                act.wait_ge(tile_done, n + 1)
                act.activation(zt[b][:, :], z[:, 2 * b, :], ACT.Identity, bias=bias).then_inc(z_read[b], 1)

            for b in range(2):
                queries(b, T_Q + b, b, par[:, T_Q + b:T_Q + b + 1])
                hi(T_Q + b + 2, b)
            act.wait_ge(lc["var"], 1)
            act.activation(lnc_sd[:, :], lnc_var[:, :], ACT.Sqrt).then_inc(lc["sd"], 1)
            for k in range(KC):
                act.wait_ge(lc["scaled"], k + 1)
                act.activation(uT[:, k, 0:S], uT[:, k, 0:S], ACT.Silu, scale=par[:, C_CLNG + k:C_CLNG + k + 1],
                               bias=par[:, C_CLNB + k:C_CLNB + k + 1]).then_inc(lc["done"], 1)
            act.wait_ge(lc["done"], KC)
            act.dma_start(u_kept, uT[:, 0:KC, 0:S]).then_inc(u_stored, 16)
            with act.Fori(1, LOOP_Q // 2) as i:
                for b in range(2):
                    n = 2 * i + T_Q + b
                    queries(2 * i + b, n, b, par[:, ds(n, 1)])
                    hi(n + 2, b)

            def norm(tag, bufs, src, nk):
                s = lns[tag]
                for c in range(nk // 2):
                    act.wait_ge(s["centred"], c + 1)
                    if c >= 2:
                        act.wait_ge(s["sqsum"], c - 1)
                    act.activation(bufs["sq"][c % 2][:], src(2 * c), ACT.Square).then_inc(s["squared"], 1)
                act.wait_ge(s["var"], 1)
                act.activation(bufs["sd"][:, :], bufs["var"][:, :], ACT.Sqrt).then_inc(s["sd"], 1)

            units = [(g, n) for g in range(N_KV) for n in range(NB)]
            turned = [0]

            def exps(u):
                g, n = units[u]
                w = P if n == 0 else 2 * P
                act.wait_ge(maxed, u + 1)
                for j in range(4):
                    for e in range(2):
                        row = prob[u % 2][:, j, e, 0:1 + w]
                        m = act.activation(row, row, ACT.Exp, bias=smax[:, u % 2, 1, 2 * j + e:2 * j + e + 1],
                                           accum_out=smax[:, u % 2, 2, 2 * j + e:2 * j + e + 1])
                m.then_inc(exped, 1)

            def copies(u):
                g, n = units[u]
                if u:
                    act.wait_ge(pv_done, u)
                for t in range(2 if n == 0 else 4):
                    act.wait_ge(p_turned, turned[0] + 1)
                    act.activation(prT[:, t, :], aux[:, 2 + t % 2, :], ACT.Copy).then_inc(pT_ready, 1)
                    turned[0] += 1

            def heads_out(u):
                g, n = units[u]
                act.wait_ge(pv_done, u + 1)
                act.activation(mix[:, 4 * g:4 * g + 4, n * P:n * P + P],
                               z[:, 1, :].rearrange("p (j q) -> p j q", j=4), ACT.Copy).then_inc(y_ready, 1)

            def take(s):
                n, b = T_SLOT + s, s % 2
                if n < T_GB:
                    queries(n - T_Q, n, b, par[:, n:n + 1])
                else:
                    if n - T_GB >= 2:
                        act.wait_ge(gated_y, n - T_GB - 1)
                    elif n == T_GB:
                        act.wait_ge(roped, N_KV + KD)
                    act.wait_ge(tile_done, n + 1)
                    act.activation(sig_b[b][:, :], z[:, 2 * b, :], ACT.Sigmoid, bias=par[:, n:n + 1])\
                       .then_inc(z_read[b], 1)
                hi(n + 2, b)

            for s in range(N_SLOTS):
                if s:
                    take(s - 1)
                if 2 <= s < N_UNITS + 2:
                    heads_out(s - 2)
                if 1 <= s <= N_UNITS:
                    copies(s - 1)
                if s < N_UNITS:
                    exps(s)
                if s == N_UNITS + 1:
                    act.wait_ge(p_turned, turned[0])
                    act.wait_ge(u_stored, 16)
                    act.dma_start(u_back[:], u_kept).then_inc(u_landed, 16)
            take(N_SLOTS - 1)
            act.wait_ge(u_landed, 16)
            act.wait_ge(y_ready, N_UNITS)
            act.activation(u_hi[:], u_back[:], ACT.Copy).then_inc(u_hi_ready, 1)
            with act.Fori(0, KD // 4) as i:
                for h in range(2):
                    for q in range(3):
                        o = 3 * h + q
                        b = o % 2
                        n = 6 * i + T_GA + o
                        act.wait_ge(tile_done, n + 1)
                        if q < 2:
                            act.wait_ge(lo_ready, n + 2)
                            act.activation(sig_a[q][:, :], z[:, 2 * b, :], ACT.Sigmoid,
                                           bias=par[:, ds(4 * i + (T_GA + 2 * h + q), 1)]).then_inc(z_read[b], 1)
                        hi(n + 2, b)
            for c in range(4):
                act.wait_ge(mixed, 4 * c + 4)
                act.activation(act_hi[:, 4 * c:4 * c + 4, :], mix[:, 4 * c:4 * c + 4, :], ACT.Copy)\
                   .then_inc(m_hi_ready, 1)
            with act.Fori(0, KD // 2) as i:
                for b in range(2):
                    n = 2 * i + T_MIX + b
                    act.wait_ge(tile_done, n + 1)
                    hi(n + 2, b)
            norm("1", ln1, lambda k: mix[:, k:k + 2, :], KD)
            for k in range(KD):
                act.wait_ge(x1_ready, k + 1)
                act.activation(act_hi[:, k, :], mix[:, k, :], ACT.Copy).then_inc(x1_hi_ready, 1)

            def exp_head(h):
                act.wait_ge(asked, h + 1)
                act.activation(expo[:, 1, :, :], expo[:, 0, :, :], ACT.Exp).then_inc(exp_ready, 1)

            for t in range(2 * HEADS_R):
                b, n = t % 2, T_ROUTE + t
                act.wait_ge(tile_done, n + 1)
                if t >= 2:
                    act.wait_ge(key_scored, t - 1)
                act.activation(rq[b][:, :], z[:, 2 * b, :], ACT.Copy).then_inc(z_read[b], 1)
                hi(n + 2, b)
                if t % 2 and t > 1:
                    exp_head(t // 2 - 1)

            def quad_copy(q):
                act.wait_ge(quad_done, q + 1)
                c, r = divmod(q, CG // 4)
                if r == 0 and c >= 2:
                    act.wait_ge(stage_out[c % 2], 16 * (c // 2))
                dst = stage[c % 2][:, :, 4 * r:4 * r + 4].rearrange("p k c -> p c k")
                act.activation(dst, aux[:, q % 4, :].rearrange("p (c k) -> p c k", c=4), ACT.Copy)\
                   .then_inc(quad_staged, 1)

            quads = 0
            for e in range(EG):
                if e == min(QUADS_OF) - 1:
                    exp_head(HEADS_R - 1)
                if e == min(QUADS_OF):
                    for m_, dst in enumerate((i_t[:, 0, :], i_t[:, 1, :], g_t[:, :])):
                        act.wait_ge(sel_turned, m_ + 1)
                        act.activation(dst, aux[:, m_, :], ACT.Copy).then_inc(sel_t_ready, 1)
                for _ in range(QUADS_OF.get(e, 0)):
                    quad_copy(quads)
                    quads += 1
                act.wait_ge(tile_done, T_PEER + e + 1)
                if e == 3:
                    act.wait_ge(sel_ready, HEADS_R)
                act.activation(hid_0[:, e, :], z[:, 2 * (e % 2), :], ACT.Gelu).then_inc(z_read[e % 2], 1)
                hi(T_PEER + e + 2, e % 2)
            for e in range(EG):
                act.wait_ge(gated_ready, e + 1)
                act.activation(a_hi[:, e, :], gated[e % 2][:, :], ACT.Copy).then_inc(a_hi_ready, 1)

            def group(g, last):
                n0 = GROUP_TILES * g + T_PEER
                for e in range(0 if isinstance(g, int) and g == 0 else EG):
                    b = e % 2
                    act.wait_ge(gated_ready, EG * g + e - 1)
                    act.wait_ge(tile_done, n0 + e + 1)
                    act.activation(hid[b][:, :], z[:, 2 * b, :], ACT.Gelu).then_inc(z_read[b], 1)
                    hi(n0 + e + 2, b)
                    act.wait_ge(gated_ready, EG * g + e + 1)
                    act.activation(a_hi[:, e, :], gated[b][:, :], ACT.Copy).then_inc(a_hi_ready, 1)
                for j in range(KD // 2):
                    if last and j >= KD // 2 - 2:
                        continue
                    act.wait_ge(tile_done, n0 + EG + j + 1)
                    hi(n0 + EG + j + 2, j % 2)

            group(0, False)
            with act.Fori(1, N_GROUPS - 1) as g:
                group(g, False)
            group(N_GROUPS - 1, True)
            norm("2", ln2, lambda k: mix[:, k:k + 2, :], KD)

        @block.vector
        def _(dve):
            links = [0]

            def link(ins):
                links[0] += 1
                ins.then_inc(chain, 1)
                dve.wait_ge(chain, links[0])

            def lo(n, b):
                dve.wait_ge(hi_ready, n + 1)
                dve.tensor_tensor(w_lo[b][:], raw[b][:], w_hi[b][:].bitcast(F32), ALU.subtract).then_inc(lo_ready, 1)

            lo(0, 0)
            for c in range(4):
                dve.wait_ge(x_hi_ready, c + 1)
                dve.tensor_tensor(act_lo[:, 4 * c:4 * c + 4, :], mix[:, 4 * c:4 * c + 4, :],
                                  act_hi[:, 4 * c:4 * c + 4, :].bitcast(F32), ALU.subtract).then_inc(x_lo_ready, 1)
            lo(1, 1)
            dve.wait_ge(const_landed, 16 * 5)
            dve.wait_ge(pos_landed, 16)
            link(dve.tensor_copy(t2[0][:, :], posi[:, :]))
            link(dve.tensor_scalar(zt[0][:, :], t2[0][:, :], rope_m[:, 5 * P:5 * P + 1], None, ALU.mult))
            link(dve.tensor_scalar(t2[0][:, :], zt[0][:, :], float(1 / (2 * np.pi)), ROUNDER, ALU.mult, ALU.add))
            link(dve.tensor_scalar(t2[1][:, :], t2[0][:, :], ROUNDER, None, ALU.subtract))
            for c in (TWO_PI_A, TWO_PI_B, TWO_PI_C):
                link(dve.scalar_tensor_tensor(out=zt[0][:, :], in0=t2[1][:, :], scalar=-float(c), in1=zt[0][:, :],
                                              op0=ALU.mult, op1=ALU.add))
            dve.tensor_scalar(t1[0][:, :], zt[0][:, :], 3.1415925, -3.1415925, ALU.min, ALU.max)\
               .then_inc(angle_ready, 1)
            dve.wait_ge(angle_ready, 1)
            link(dve.scalar_tensor_tensor(out=t2[0][:, :], in0=t1[0][:, :], scalar=-1.0, in1=t1[0][:, :],
                                          op0=ALU.mult, op1=ALU.max))
            dve.tensor_scalar(t1[1][:, :], t2[0][:, :], -1.0, float(np.pi / 2), ALU.mult, ALU.add)\
               .then_inc(angle_ready, 1)
            dve.wait_ge(angle_ready, 2)
            dve.tensor_scalar(half_b[:, :], par[:, C_BIAS:C_BIAS + 2 * KC], 0.5, None, ALU.mult).then_inc(zt_used, 1)

            dve.wait_ge(pads_ready, 1)
            with dve.Fori(0, KC) as i:
                dve.wait_ge(z_read[0], i + 1)
                dve.wait_ge(z_read[1], i + 1)
                dve.scalar_tensor_tensor(out=uT[:, ds(i + 1, 1), PAD:SLOT].rearrange("p o s -> p (o s)"),
                                         in0=zt[1][:, :], scalar=1.0, in1=zt[0][:, :],
                                         op0=ALU.add, op1=ALU.mult).then_inc(zt_used, 1)
                for w in range(TAPS):
                    src = uT[:, ds(i + 1, 1), w:w + S].rearrange("p o s -> p (o s)")
                    dst = uT[:, ds(i, 1), 0:S].rearrange("p o s -> p (o s)")
                    tap = par[:, ds(TAPS * i + C_TAPS + w, 1)]
                    if w == 0:
                        dve.wait_ge(zt_used, i + 2)
                        dve.tensor_scalar(dst, src, tap, par[:, ds(i + C_CONVB, 1)], ALU.mult, ALU.add)\
                           .then_inc(tap_done, 1)
                    else:
                        dve.wait_ge(tap_done, TAPS * i + w)
                        dve.scalar_tensor_tensor(out=dst, in0=src, scalar=tap, in1=dst,
                                                 op0=ALU.mult, op1=ALU.add).then_inc(tap_done, 1)

            dve.wait_ge(sincos_ready, 2)

            def rope_keys(g):
                dve.wait_ge(k_rot, g + 1)
                a = 2 * (g % 2)
                dve.tensor_tensor(t1[0][:, :], aux[:, a + 1, :], sinT[:, :], ALU.mult).then_inc(rope_part, 1)
                dve.tensor_tensor(t2[0][:, :], aux[:, a, :], cosT[:, :], ALU.mult).then_inc(rope_part, 1)
                dve.wait_ge(rope_part, 2 * g + 2)
                dve.tensor_tensor(kT[:, g, :], t1[0][:, :], t2[0][:, :], ALU.add).then_inc(roped, 1)
                dve.wait_ge(roped, g + 1)

            lc = lns["c"]
            rope_keys(0)
            rope_keys(1)
            dve.wait_ge(lc["sum"], 1)
            link(dve.tensor_copy(lnc_mean[:, :], z[:, 1, :]))
            for k in range(KC):
                dve.tensor_tensor(uT[:, k, 0:S], uT[:, k, 0:S], lnc_mean[:, :], ALU.subtract).then_inc(lc["centred"], 1)
            rope_keys(2)
            rope_keys(3)

            def newton(rs, tt, sd, var, ready):
                link(dve.reciprocal(rs[:, :], sd[:, :]))
                link(dve.tensor_tensor(tt[:, :], rs[:, :], rs[:, :], ALU.mult))
                link(dve.tensor_tensor(tt[:, :], tt[:, :], var[:, :], ALU.mult))
                link(dve.tensor_scalar(tt[:, :], tt[:, :], -0.5, 1.5, ALU.mult, ALU.add))
                dve.tensor_tensor(rs[:, :], rs[:, :], tt[:, :], ALU.mult).then_inc(ready, 1)
                dve.wait_ge(ready, 1)

            def rope_query(q, b, rotated, row):
                dve.wait_ge(roped, q + N_KV - 1)
                dve.wait_ge(q_rot, q + 1)
                dve.tensor_tensor(t1[b][:, :], rotated, sinT[:, :], ALU.mult).then_inc(rope_part, 1)
                dve.tensor_tensor(t2[b][:, :], zt[b][:, :], cosT[:, :], ALU.mult).then_inc(rope_part, 1)
                dve.wait_ge(rope_part, 2 * q + 2 * N_KV + 2)
                dve.tensor_tensor(row, t1[b][:, :], t2[b][:, :], ALU.add).then_inc(roped, 1)

            dve.wait_ge(lc["sqsum"], KC)
            dve.tensor_scalar(lnc_var[:, :], z[:, 3, :], EPS, None, ALU.add).then_inc(lc["var"], 1)
            for b in range(2):
                rope_query(b, b, aux[:, b, :], mix[:, b, :])
            dve.wait_ge(lc["sd"], 1)
            newton(lnc_rs, lnc_tt, lnc_sd, lnc_var, lc["rs"])
            for k in range(KC):
                dve.tensor_tensor(uT[:, k, 0:S], uT[:, k, 0:S], lnc_rs[:, :], ALU.mult).then_inc(lc["scaled"], 1)
            with dve.Fori(1, LOOP_Q // 2) as i:
                for b in range(2):
                    rope_query(2 * i + b, b, aux[:, b, :], mix[:, ds(2 * i + b, 1), :].rearrange("p o s -> p (o s)"))

            def norm(tag, bufs, src, nk, factor):
                s = lns[tag]
                dve.wait_ge(s["sum"], 1)
                link(dve.tensor_scalar(bufs["mean"][:, :], aux[:, 0, :], factor, None, ALU.mult))
                for c in range(nk // 2):
                    dve.tensor_tensor(src(2 * c), src(2 * c), bufs["mean"][:, :].unsqueeze(1).to_broadcast([P, 2, S]),
                                      ALU.subtract).then_inc(s["centred"], 1)
                dve.wait_ge(s["sqsum"], nk // 2)
                dve.tensor_scalar(bufs["var"][:, :], aux[:, 1, :], factor, EPS, ALU.mult, ALU.add).then_inc(s["var"], 1)
                dve.wait_ge(s["sd"], 1)
                newton(bufs["rs"], bufs["tt"], bufs["sd"], bufs["var"], s["rs"])

            units = [(g, n) for g in range(N_KV) for n in range(NB)]

            def turned_upto(u):
                return sum(2 if n == 0 else 4 for g, n in units[:u + 1])

            def sinks(u):
                if u == 0:
                    dve.wait_ge(u_stored, 16)
                if u >= 2:
                    dve.wait_ge(p_turned, turned_upto(u - 2))
                g = units[u][0]
                dve.tensor_copy(prob[u % 2][:, :, :, 0:1].rearrange("p j e o -> p (j e o)"),
                                par[:, C_SINK + 8 * g:C_SINK + 8 * g + 8]).then_inc(sink_in, 1)

            def mask_scores(u, j):
                w = P if units[u][1] == 0 else 2 * P
                dve.wait_ge(scored, 4 * u + j + 1)
                dve.scalar_tensor_tensor(
                    out=prob[u % 2][:, j, :, 1:1 + w], in0=aux[:, 0:2, 0:w], scalar=SCALE,
                    in1=mask[:, 2 * P - w:2 * P].unsqueeze(1).to_broadcast([P, 2, w]),
                    op0=ALU.mult, op1=ALU.add).then_inc(masked, 1)

            def row_max(u):
                w = P if units[u][1] == 0 else 2 * P
                dve.wait_ge(masked, 4 * u + 4)
                dve.wait_ge(sink_in, u + 1)
                link(dve.tensor_reduce(smax[:, u % 2, 0, :],
                                       prob[u % 2][:, :, :, 0:1 + w].rearrange("p j e k -> p (j e) k"), AX, ALU.max))
                dve.tensor_scalar(smax[:, u % 2, 1, :], smax[:, u % 2, 0, :], -1.0, None, ALU.mult).then_inc(maxed, 1)

            def normalise(u):
                w = P if units[u][1] == 0 else 2 * P
                dve.wait_ge(exped, u + 1)
                link(dve.reciprocal(smax[:, u % 2, 3, :], smax[:, u % 2, 2, :]))
                for j in range(4):
                    for e in range(2):
                        row = prob[u % 2][:, j, e, 1:1 + w]
                        m = dve.tensor_scalar(row, row, smax[:, u % 2, 3, 2 * j + e:2 * j + e + 1], None, ALU.mult)
                m.then_inc(p_ready, 1)

            for s in range(N_SLOTS + 2):
                if s < N_UNITS:
                    sinks(s)
                    mask_scores(s, 0)
                    mask_scores(s, 1)
                if 1 <= s <= N_UNITS:
                    normalise(s - 1)
                k = T_SLOT + s - 2 - T_GB
                if k >= 0:
                    dve.wait_ge(z_read[k % 2], (T_GB + k) // 2 + 1)
                    dve.wait_ge(y_ready, NB * (k // 4 + 1))
                    dve.tensor_tensor(mix[:, k, :], mix[:, k, :], sig_b[k % 2][:, :], ALU.mult).then_inc(gated_y, 1)
                if s < N_UNITS:
                    mask_scores(s, 2)
                if 1 <= s <= KD - LOOP_Q:
                    q = LOOP_Q + s - 1
                    rope_query(q, q % 2, z[:, 3, :], mix[:, q, :])
                if s < N_UNITS:
                    mask_scores(s, 3)
                    row_max(s)

            dve.wait_ge(u_hi_ready, 1)
            dve.tensor_tensor(u_lo[:], u_back[:], u_hi[:].bitcast(F32), ALU.subtract).then_inc(u_lo_ready, 1)
            dve.wait_ge(lo_ready, POOL_A[1] + 1)
            dve.wait_ge(gated_y, KD)
            with dve.Fori(0, KD // 4) as i:
                for h in range(2):
                    for q in range(3):
                        o = 3 * h + q
                        b = o % 2
                        n = 6 * i + T_GA + o
                        if q == 2:
                            for j in range(2):
                                if j == 0:
                                    dve.wait_ge(tile_done, n + 1)
                                    dve.wait_ge(z_read[1 - b], 3 * i + (T_GA + o - 1) // 2 + 1)
                                m = dve.tensor_tensor(sig_a[j][:, :], sig_a[j][:, :], z[:, 2 * b + j, :], ALU.mult)
                                m.then_inc(*((z_read[b], 1) if j else (prod_y, 1)))
                            for j in range(2):
                                row = mix[:, ds(4 * i + 2 * h + j, 1), :].rearrange("p o s -> p (o s)")
                                if j == 0:
                                    dve.wait_ge(prod_y, 2 * i + h + 1)
                                    dve.wait_ge(z_read[b], 3 * i + (T_GA + o) // 2 + 1)
                                dve.tensor_tensor(row, row, sig_a[j][:, :], ALU.add).then_inc(mixed, 1)
                        lo(n + 2, b)
            for c in range(4):
                dve.wait_ge(m_hi_ready, c + 1)
                dve.tensor_tensor(act_lo[:, 4 * c:4 * c + 4, :], mix[:, 4 * c:4 * c + 4, :],
                                  act_hi[:, 4 * c:4 * c + 4, :].bitcast(F32), ALU.subtract).then_inc(m_lo_ready, 1)
            dve.wait_ge(m_lo_ready, 4)
            with dve.Fori(0, KD // 2) as i:
                for b in range(2):
                    n = 2 * i + T_MIX + b
                    dve.wait_ge(x_res_landed[b], 16 * i + 16)
                    dve.wait_ge(tile_done, n + 1)
                    dve.scalar_tensor_tensor(out=mix[:, ds(2 * i + b, 1), :].rearrange("p o s -> p (o s)"),
                                             in0=x_res[b][:, :], scalar=ALPHA, in1=z[:, 2 * b, :],
                                             op0=ALU.mult, op1=ALU.add).then_inc(z_read[b], 1)
                    lo(n + 2, b)
            norm("1", ln1, lambda k: mix[:, k:k + 2, :], KD, 0.5)
            for k in range(KD):
                link(dve.scalar_tensor_tensor(out=mix[:, k, :], in0=mix[:, k, :], scalar=par[:, C_LN1G + k:C_LN1G + k + 1],
                                              in1=ln1["rs"][:, :], op0=ALU.mult, op1=ALU.mult))
                dve.tensor_scalar(mix[:, k, :], mix[:, k, :], par[:, C_LN1B + k:C_LN1B + k + 1], None, ALU.add)\
                   .then_inc(x1_ready, 1)
                dve.wait_ge(x1_hi_ready, k + 1)
                dve.tensor_tensor(act_lo[:, k, :], mix[:, k, :], act_hi[:, k, :].bitcast(F32), ALU.subtract)\
                   .then_inc(x1_lo_ready, 1)
            dve.wait_ge(x1_lo_ready, KD)
            for c in range(4):
                dve.tensor_scalar(mix[:, 4 * c:4 * c + 4, :], mix[:, 4 * c:4 * c + 4, :], ALPHA, None, ALU.mult)\
                   .then_inc(acc_ready, 1)

            def top16(dst_v, dst_i, src, spare, last):
                for c in range(NB):
                    m = dve.max(dst_v[:, c, 0:8], src[:, c, :])
                link(m)
                for c in range(NB):
                    dve.max_index(dst_i[:, c, 0:8], dst_v[:, c, 0:8], src[:, c, :])
                for c in range(NB):
                    m = dve.match_replace(spare[:, c, :], dst_v[:, c, 0:8], src[:, c, :], NEG)
                    if c == NB - 1 and last is not None:
                        m.then_inc(last, 1)
                if last is None:
                    link(m)
                else:
                    takes[0] += 1
                    dve.wait_ge(last, takes[0])
                for c in range(NB):
                    m = dve.max(dst_v[:, c, 8:16], spare[:, c, :])
                link(m)
                for c in range(NB):
                    m = dve.max_index(dst_i[:, c, 8:16], dst_v[:, c, 8:16], spare[:, c, :])
                link(m)

            takes = [0]

            def combine(h):
                link(dve.tensor_copy(idxf[:], idx[:]))
                link(dve.tensor_tensor(cand[:].rearrange("p c (a b) -> p c a b", a=TOPK),
                                       val[:, 0, :, :].unsqueeze(3).to_broadcast([P, NB, TOPK, TOPK]),
                                       val[:, 1, :, :].unsqueeze(2).to_broadcast([P, NB, TOPK, TOPK]), ALU.add))
                top16(best, place, cand, cand2, None)
                dve.tensor_tensor(expo[:, 0, :, :], best[:], best[:, :, 0:1].to_broadcast([P, NB, TOPK]), ALU.subtract)\
                   .then_inc(asked, 1)
                dve.tensor_scalar(digit[:, 0, :, :], place[:], 4, None, ALU.logical_shift_right)
                link(dve.tensor_scalar(digit[:, 1, :, :], place[:], 15, None, ALU.bitwise_and))
                link(dve.tensor_copy(digitf[:], digit[:].rearrange("p d c k -> p d (c k)")))
                for d in range(2):
                    dve.tensor_tensor(pick[:, d, :, :], digitf[:, d, :].unsqueeze(2).to_broadcast([P, NB * TOPK, TOPK]),
                                      iota[:, 0:TOPK].unsqueeze(1).to_broadcast([P, NB * TOPK, TOPK]), ALU.is_equal)\
                       .then_inc(picked, 1)

            def keep(h):
                for d in range(2):
                    dve.wait_ge(pick_scaled, 2 * h + d + 1)
                    dve.tensor_reduce(sel_i[:, d, :, h * TOPK:h * TOPK + TOPK],
                                      pick[:, d, :, :].rearrange("p (c k) a -> p c k a", c=NB), AX, ALU.add)
                dve.wait_ge(exp_ready, h + 1)
                link(dve.tensor_reduce(esum[:, 0, :], expo[:, 1, :, :], AX, ALU.add))
                link(dve.reciprocal(esum[:, 1, :], esum[:, 0, :]))
                dve.tensor_tensor(sel_g[:, :, h * TOPK:h * TOPK + TOPK], expo[:, 1, :, :],
                                  esum[:, 1, :].unsqueeze(2).to_broadcast([P, NB, TOPK]), ALU.mult)\
                   .then_inc(sel_ready, 1)
                dve.wait_ge(sel_ready, h + 1)

            for t in range(2 * HEADS_R):
                dve.wait_ge(key_scored, t + 1)
                top16(val[:, t % 2, :, :], idx[:, t % 2, :, :],
                      aux[:, t % 2, :].rearrange("p (c k) -> p c k", c=NB), rest, keys_taken)
                if t % 2:
                    combine(t // 2)
                elif t:
                    keep(t // 2 - 1)
            keep(HEADS_R - 1)

            dve.wait_ge(sel_t_ready, 3)
            for q in range(S // 4):
                if q >= 4:
                    dve.wait_ge(quad_done, q - 3)
                for hot, half_ in ((hot1, 0), (hot2, 1)):
                    dve.tensor_tensor(hot[:, 4 * (q % 4):4 * (q % 4) + 4, :], iota[:, :].unsqueeze(1).to_broadcast([P, 4, P]),
                                      i_t[:, half_, 4 * q:4 * q + 4].unsqueeze(2).to_broadcast([P, 4, P]),
                                      ALU.is_equal).then_inc(hot_matched, 1)

            def group(g, last):
                n0 = GROUP_TILES * g + T_PEER
                first = isinstance(g, int) and g == 0
                dve.wait_ge(gate_landed, 16 * g + 16)
                for e in range(EG):
                    b = e % 2
                    dve.wait_ge(z_read[b], EG * g + T_PEER // 2 + e // 2 + 1)
                    if not (first and e < 2):
                        dve.wait_ge(a_lo_ready, EG * g + e - 1)
                    src = hid_0[:, e, :] if first else hid[b][:, :]
                    dve.tensor_tensor(gated[b][:, :].rearrange("p (c s) -> p c s", c=N_CG),
                                      src.rearrange("p (c s) -> p c s", c=N_CG),
                                      gate[:, :, e * CG:e * CG + CG], ALU.mult).then_inc(gated_ready, 1)
                    if not first:
                        lo(n0 + e + 2, b)
                    dve.wait_ge(a_hi_ready, EG * g + e + 1)
                    dve.tensor_tensor(a_lo[:, e, :], gated[b][:, :], a_hi[:, e, :].bitcast(F32), ALU.subtract)\
                       .then_inc(a_lo_ready, 1)
                if first:
                    dve.wait_ge(lo_ready, POOL_R[1] + 1)
                for j in range(KD // 2):
                    b = j % 2
                    dve.wait_ge(tile_done, n0 + EG + j + 1)
                    if isinstance(g, int) and g == 0:
                        dve.wait_ge(acc_ready, 4)
                    else:
                        dve.wait_ge(z_read[b], EG * g + (T_PEER + EG - GROUP_TILES + j - b) // 2 + 1)
                    for s_ in range(2):
                        k = 2 * j + s_
                        m = dve.tensor_tensor(mix[:, k, :], mix[:, k, :], z[:, 2 * b + s_, :], ALU.add)
                    m.then_inc(z_read[b], 1)
                    if not (last and j >= KD // 2 - 2):
                        lo(n0 + EG + j + 2, b)

            group(0, False)
            with dve.Fori(1, N_GROUPS - 1) as g:
                group(g, False)
            group(N_GROUPS - 1, True)
            norm("2", ln2, lambda k: mix[:, k:k + 2, :], KD, 0.5)
            for k in range(KD):
                link(dve.scalar_tensor_tensor(out=mix[:, k, :], in0=mix[:, k, :], scalar=par[:, C_LN2G + k:C_LN2G + k + 1],
                                              in1=ln2["rs"][:, :], op0=ALU.mult, op1=ALU.mult))
                dve.tensor_scalar(mix[:, k, :], mix[:, k, :], par[:, C_LN2B + k:C_LN2B + k + 1], None, ALU.add)\
                   .then_inc(out_ready, 1)

        @block.gpsimd
        def _(pool):
            pool.memset(uT[:, :, 0:PAD], 0.0).then_inc(pads_ready, 1)
            pool.memset(ones[:, :], 1.0 / CC).then_inc(ones_ready, 1)

            def lo(n, b):
                pool.wait_ge(hi_ready, n + 1)
                pool.tensor_tensor(w_lo[b][:], raw[b][:], w_hi[b][:].bitcast(F32), ALU.subtract).then_inc(lo_ready, 1)

            pool.wait_ge(lo_ready, POOL_A[0])
            with pool.Fori(0, (POOL_A[1] + 1 - POOL_A[0]) // 2) as i:
                for b in range(2):
                    lo(2 * i + POOL_A[0] + b, b)

            def scale_pick(h):
                for d in range(2):
                    v4 = pick[:, d, :, :].rearrange("p (c k) a -> p c k a", c=NB)
                    pool.wait_ge(picked, 2 * h + d + 1)
                    pool.tensor_tensor(v4, v4, idxf[:, d, :, :].unsqueeze(2).to_broadcast([P, NB, TOPK, TOPK]),
                                       ALU.mult).then_inc(pick_scaled, 1)

            pool.wait_ge(lo_ready, POOL_R[0])
            for t in range(2 * HEADS_R + 2):
                if t >= 3 and t % 2:
                    scale_pick(t // 2 - 1)
                lo(T_ROUTE + t + 2, t % 2)

            quads = 0
            for e in range(2, EG):
                if e == min(QUADS_OF):
                    pool.wait_ge(sel_t_ready, 3)
                for _ in range(QUADS_OF.get(e, 0)):
                    s_ = 4 * (quads % 4)
                    pool.wait_ge(hot_matched, 2 * quads + 2)
                    pool.tensor_tensor(hot1[:, s_:s_ + 4, :], hot1[:, s_:s_ + 4, :],
                                       g_t[:, 4 * quads:4 * quads + 4].unsqueeze(2).to_broadcast([P, 4, P]),
                                       ALU.mult).then_inc(hot_ready, 1)
                    quads += 1
                lo(T_PEER + e + 2, e % 2)


def _constants():
    c = np.zeros((P, N_CONST), np.float32)
    r = np.arange(P)
    c[:, K_IDENT:K_IDENT + P] = np.eye(P)
    c[:, K_IOTA:K_IOTA + P] = r
    c[:, K_MASK:K_MASK + P] = np.where(r[None, :] > r[:, None], 0.0, NEG)
    c[:, K_MASK + P:K_MASK + 2 * P] = np.where(r[None, :] <= r[:, None], 0.0, NEG)
    rot = np.zeros((P, P), np.float32)
    for m in range(P):
        if m % HEAD < ROT // 2:
            rot[m + ROT // 2, m] = -1.0
        elif m % HEAD < ROT:
            rot[m - ROT // 2, m] = 1.0
    c[:, K_ROT:K_ROT + P] = rot
    for g in range(2):
        for m in range(P):
            c[64 * g + m % 64, K_DUP + P * g + m] = 1.0
            c[64 * g:64 * g + 64, K_RDUP + P * g + m] = rot[0:64, m % 64]
    freq = np.float32(THETA) ** (-np.arange(0, ROT, 2, dtype=np.float32) / np.float32(ROT))
    c[:, K_FREQ] = [freq[m % HEAD % (ROT // 2)] if m % HEAD < ROT else 0.0 for m in range(P)]
    return c


def _tiles(w, n_in=KD):
    s = 16 // n_in
    t = w.reshape(n_in, P, -1, s, P).transpose(2, 1, 3, 0, 4)
    return np.ascontiguousarray(t).reshape(-1, P, 16 * P)


def _columns(v):
    return v.reshape(-1, P).T


def kernel(**inputs):
    import concourse.bacc as _bacc
    from concourse.bass_utils import run_bass_kernel_spmd as _run

    a = {k: np.asarray(v) for k, v in inputs.items()}
    nq, nk = KD, 2
    q0, k0 = 2 * KC, 2 * KC + nq
    v0, a0 = k0 + nk, k0 + 2 * nk
    order = [t for i in range(KC) for t in (i, KC + i)] + list(range(k0, a0)) + list(range(q0, k0))
    order += list(range(a0 + KD, a0 + 2 * KD)) + list(range(a0, a0 + KD))
    w_v = a["expert_v"][0].reshape(N_GROUPS, EG, P, KD // 2, 2, P).transpose(0, 3, 2, 4, 1, 5)
    params = np.concatenate([
        _columns(a["b_in"][0])[:, order],
        a["conv_dw_w"][0, :, 0, :].reshape(TAPS, KC, P).transpose(2, 1, 0).reshape(P, KC * TAPS),
        _columns(a["conv_dw_b"][0]), _columns(a["conv_ln_g"][0]), _columns(a["conv_ln_b"][0]),
        np.broadcast_to(a["attn_sinks"][0][None, :], (P, N_HEADS)),
        _columns(a["ln1_g"][0]), _columns(a["ln1_b"][0]), _columns(a["ln2_g"][0]), _columns(a["ln2_b"][0]),
        a["sub_keys_1"][0].T, a["sub_keys_2"][0].T], axis=1)
    arrays = {
        "x_t": a["x"][0].T.reshape(KD, P, S).transpose(1, 0, 2),
        "pos": a["positions"],
        "w_in": _tiles(a["w_in"][0])[order],
        "w_conv": _tiles(a["w_conv_out"][0], KC),
        "w_mix": _tiles(a["w_mix_out"][0]),
        "w_route": _tiles(a["w_peer_q"][0]),
        "exp_u": _tiles(a["expert_u"][0].T),
        "exp_v": w_v.reshape(N_GROUPS * KD // 2, P, 16 * P),
        "params": params,
        "consts": _constants(),
    }
    arrays = {k: np.ascontiguousarray(v) for k, v in arrays.items()}
    nc = _bacc.Bacc("TRN2", target_bir_lowering=False, num_devices=1)
    args = [nc.dram_tensor(k, v.shape, mybir.dt.from_np(v.dtype), kind="ExternalInput").ap() for k, v in arrays.items()]
    args.append(nc.dram_tensor("gates", (N_CG, P, NKEY * CG), F32, kind="Internal").ap())
    args.append(nc.dram_tensor("u_kept", (P, KC, S), F32, kind="Internal").ap())
    args.append(nc.dram_tensor("out", (P, KD, S), F32, kind="ExternalOutput").ap())
    build(nc, *args)
    r = _run(nc, [arrays], core_ids=[0])
    return r.results[0]["out"].transpose(1, 0, 2).reshape(1, D, S).transpose(0, 2, 1)
```

```python
from contextlib import ExitStack

import numpy as np

import concourse.bass as bass
from concourse import mybir

F32 = mybir.dt.float32
F32R = mybir.dt.float32r
I32 = mybir.dt.int32
U32 = mybir.dt.uint32
ALU = mybir.AluOpType
ACT = mybir.ActivationFunctionType
AX = mybir.AxisListType.X
ds = bass.ds

P = 128
S = 512
D = 2048
KD = D // P
N_HEADS, N_KV, HEAD = 32, 4, 64
ROT = HEAD // 4
THETA = 500000.0
SCALE = HEAD ** -0.5
NB = S // P
CC = D // 2
KC = CC // P
TAPS = 31
PAD = TAPS - 1
SLOT = S + PAD
HEADS_R, NKEY, TOPK = 8, 128, 16
EPS = 1e-5
ALPHA = 2.0 ** 0.25
NEG = -3.0e38

T_GLU = 0
T_K = T_GLU + 2 * KC
T_V = T_K + 2
T_Q = T_V + 2
T_GB = T_Q + KD
T_GA = T_GB + KD
T_MIX = T_GA + KD + KD // 2
T_ROUTE = T_MIX + KD
T_PEER = T_ROUTE + 2 * HEADS_R
EG = 8
N_GROUPS = NKEY // EG
GROUP_TILES = EG + KD // 2
N_TILES = T_PEER + N_GROUPS * GROUP_TILES
CG = 16
N_CG = S // CG
QUADS_OF = {3: 48, 4: 48, 5: 32}
LOOP_Q = KD - 4
T_SLOT = T_Q + LOOP_Q
N_UNITS = N_KV * NB
N_SLOTS = T_GA - T_SLOT
QUAD_LO = {56: T_PEER + 5, 104: T_PEER + 6}
POOL_A = (2, T_GA + 1)
X_PARTS = ((0, 2), (2, 4), (6, 4), (10, 4), (14, 2))
M_PARTS = ((0, 4), (4, 4), (8, 4), (12, 2), (14, 2))
POOL_R = (T_ROUTE + 2, T_PEER + EG + 1)

C_BIAS = 0
C_TAPS = C_BIAS + T_GA + KD
C_CONVB = C_TAPS + KC * TAPS
C_CLNG = C_CONVB + KC
C_CLNB = C_CLNG + KC
C_SINK = C_CLNB + KC
C_LN1G = C_SINK + N_HEADS
C_LN1B = C_LN1G + KD
C_LN2G = C_LN1B + KD
C_LN2B = C_LN2G + KD
C_KEYS = C_LN2B + KD
N_PARAM = C_KEYS + 2 * NKEY

K_IDENT, K_IOTA, K_MASK, K_ROT, K_DUP, K_RDUP = 0, 128, 256, 512, 640, 896
K_FREQ = 1152
N_CONST = 1153

TWO_PI_A = 6.28125
TWO_PI_B = 1.9340515136718750e-03
TWO_PI_C = 2 * np.pi - TWO_PI_A - TWO_PI_B
ROUNDER = 1.5 * 2.0 ** 23


def build(nc, x_t, pos, w_in, w_conv, w_mix, w_route, exp_u, exp_v, params, consts, gates, u_kept, out):
    with ExitStack() as ctx:
        base = -(-nc.sbuf_base // 32) * 32
        at = [base]

        def fixed(name, shape, dt):
            t = nc.alloc_sbuf_tensor_at(name, shape, dt, offset=at[0])
            at[0] += -(-4 * int(np.prod(shape[1:])) // 32) * 32
            return t

        act_hi = fixed("act_hi", [P, KD, S], F32R)
        act_lo = fixed("act_lo", [P, KD, S], F32R)
        mix = fixed("mix", [P, KD, S], F32)
        raw = [fixed(f"raw{i}", [P, 16, P], F32) for i in range(2)]
        w_hi = [fixed(f"w_hi{i}", [P, 16, P], F32R) for i in range(2)]
        w_lo = [fixed(f"w_lo{i}", [P, 16, P], F32R) for i in range(2)]
        ident = fixed("ident", [P, P], F32)
        iota = fixed("iota", [P, P], F32)
        ones = fixed("ones", [P, P], F32)
        par = fixed("par", [P, N_PARAM], F32)
        region = at[0]

        def shared(name, shape, dt, offset):
            return nc.alloc_sbuf_tensor_at(name, shape, dt, offset=region + offset)

        uT = shared("uT", [P, KC + 1, SLOT], F32, 0)
        kT = shared("kT", [P, N_KV, S], F32, 19520)
        vN = shared("vN", [P, NB, N_KV * HEAD], F32, 27712)
        mask = shared("mask", [P, 2 * P], F32, 31808)
        rope_m = shared("rope_m", [P, 5 * P + 1], F32, 32832)
        cosT = shared("cosT", [P, S], F32, 35424)
        sinT = shared("sinT", [P, S], F32, 37472)
        zt = [shared(f"zt{i}", [P, S], F32, 39520 + 2048 * i) for i in range(2)]
        t1 = [shared(f"t1_{i}", [P, S], F32, 43616 + 2048 * i) for i in range(2)]
        t2 = [shared(f"t2_{i}", [P, S], F32, 47712 + 2048 * i) for i in range(2)]
        half_b = shared("half_b", [P, 2 * KC], F32, 51808)
        posi = shared("posi", [P, S], I32, 51872)
        odd_taps = shared("odd_taps", [P, S], F32, 53920)
        lnc_mean = shared("lnc_mean", [P, S], F32, 51872)
        lnc_tt = shared("lnc_tt", [P, S], F32, 51872)
        lnc_sq = [shared("lnc_sq0", [P, S], F32, 17344), shared("lnc_sq1", [P, S], F32, 53920)]
        lnc_var = shared("lnc_var", [P, S], F32, 53920)
        lnc_sd = shared("lnc_sd", [P, S], F32, 55968)
        lnc_rs = shared("lnc_rs", [P, S], F32, 58016)
        lnc_usum = shared("lnc_usum", [P, S], F32, 55968)
        lnc_qsum = shared("lnc_qsum", [P, S], F32, 58016)
        prob = [shared(f"prob{i}", [P, 4, 2, 2 * P + 1], F32, 8224 * i) for i in range(2)]
        prT = shared("prT", [P, 4, S], F32, 51872)
        smax = shared("smax", [P, 2, 4, 8], F32, 60064)
        sig_b = [shared(f"sig_b{i}", [P, S], F32, 35904 + 2048 * i) for i in range(2)]
        u_back = shared("u_back", [P, KC, S], F32, 0)
        u_lo = shared("u_lo", [P, KC, S], F32R, 0)
        u_hi = shared("u_hi", [P, KC, S], F32R, 19520)
        sig_a = [shared(f"sig_a{i}", [P, S], F32, 40000 + 2048 * i) for i in range(2)]

        def ln_buffers(tag, offset, w):
            at_ = [offset]

            def buf(name, n=1):
                at_[0] += 2048 * n
                return shared(f"{tag}_{name}", [P, n, S] if n > 1 else [P, S], F32, at_[0] - 2048 * n)

            b = {m: buf(m, w) for m in ("sq0", "sq1", "sum_d", "sum_q")}
            b.update({m: buf(m) for m in ("shift", "mean", "var", "sd", "rs")})
            b["tt"] = b["shift"]
            return b

        ln1 = ln_buffers("ln1", 4096, 1)
        ln2 = ln_buffers("ln2", 32768, 2)
        x_res = [shared(f"x_res{i}", [P, S], F32, 44096 + 2048 * i) for i in range(2)]
        rq = [shared(f"rq{i}", [P, S], F32, 22528 + 2048 * i) for i in range(2)]
        rest = shared("rest", [P, NB, NKEY], F32, 0)
        val = shared("val", [P, 2, NB, TOPK], F32, 2048)
        idx = shared("idx", [P, 2, NB, TOPK], U32, 2560)
        idxf = shared("idxf", [P, 2, NB, TOPK], F32, 3072)
        cand = shared("cand", [P, NB, TOPK * TOPK], F32, 3584)
        cand2 = shared("cand2", [P, NB, TOPK * TOPK], F32, 7680)
        best = shared("best", [P, NB, TOPK], F32, 11776)
        place = shared("place", [P, NB, TOPK], U32, 12032)
        digit = shared("digit", [P, 2, NB, TOPK], U32, 12288)
        digitf = shared("digitf", [P, 2, NB * TOPK], F32, 12800)
        expo = shared("expo", [P, 2, NB, TOPK], F32, 13312)
        esum = shared("esum", [P, 2, NB], F32, 13824)
        pick = shared("pick", [P, 2, NB * TOPK, TOPK], F32, 26624)
        sel_i = shared("sel_i", [P, 2, NB, P], F32, 34816)
        sel_g = shared("sel_g", [P, NB, P], F32, 38912)
        hot = shared("hot", [P, 2, 16, P], F32, 0)
        i_t = shared("i_t", [P, 2, S], F32, 53248)
        g_t = shared("g_t", [P, S], F32, 57344)
        stage = [shared(f"stage{i}", [P, NKEY, CG], F32, 32768 + 8192 * i) for i in range(2)]
        a_hi = shared("a_hi", [P, EG, S], F32R, 0)
        a_lo = shared("a_lo", [P, EG, S], F32R, 16384)
        hid_0 = shared("hid_0", [P, EG, S], F32, 16384)
        gate = shared("gate", [P, N_CG, EG * CG], F32, 32768)
        hid = [shared(f"hid{i}", [P, S], F32, 49152 + 2048 * i) for i in range(2)]
        gated = [shared(f"gated{i}", [P, S], F32, 53248 + 2048 * i) for i in range(2)]

        z = ctx.enter_context(nc.psum_tensor("z", [P, 4, S], F32))
        aux = ctx.enter_context(nc.psum_tensor("aux", [P, 4, S], F32))

        def sem(name):
            return ctx.enter_context(nc.semaphore(name))

        w_landed = [sem("w_landed0"), sem("w_landed1")]
        hi_ready, lo_ready, tile_done = sem("hi_ready"), sem("lo_ready"), sem("tile_done")
        z_read = [sem("z_read0"), sem("z_read1")]
        x_landed = [sem(f"x_landed{i}") for i in range(len(X_PARTS))]
        const_landed, pos_landed = sem("const_landed"), sem("pos_landed")
        x_hi_ready, x_lo_ready = sem("x_hi_ready"), sem("x_lo_ready")
        pads_ready, ones_ready = sem("pads_ready"), sem("ones_ready")
        angle_ready, sincos_ready = sem("angle_ready"), sem("sincos_ready")
        zt_used, k_rot = sem("zt_used"), sem("k_rot")
        v_turned, v_ready = sem("v_turned"), sem("v_ready")
        q_rot, rope_part, roped = sem("q_rot"), sem("rope_part"), sem("roped")
        u_summed, sq_summed = sem("u_summed"), sem("sq_summed")
        tap_done, convolved = sem("tap_done"), sem("convolved")
        lnc = {m: sem("lnc_" + m) for m in
               ("sum", "centred", "squared", "sqsum", "var", "sd", "rs", "scaled", "done")}
        lns = {tag: {m: sem(f"ln{tag}_{m}") for m in
                     ("shift_sum", "shifted", "squared", "summed", "mean_sum", "sq_sum", "mean", "var", "sd", "rs",
                      "centred", "scaled")} for tag in ("1", "2")}
        scored, masked, maxed, exped = sem("scored"), sem("masked"), sem("maxed"), sem("exped")
        sink_in, p_ready, p_turned, pT_ready = sem("sink_in"), sem("p_ready"), sem("p_turned"), sem("pT_ready")
        pv_done, y_ready = sem("pv_done"), sem("y_ready")
        u_stored, u_landed = sem("u_stored"), sem("u_landed")
        u_hi_ready, u_lo_ready, gated_y, prod_y, mixed = (sem("u_hi_ready"), sem("u_lo_ready"), sem("gated_y"),
                                                          sem("prod_y"), sem("mixed"))
        m_hi_ready, m_lo_ready = sem("m_hi_ready"), sem("m_lo_ready")
        x_res_landed = [sem("x_res_landed0"), sem("x_res_landed1")]
        x1_ready, x1_hi_ready, x1_lo_ready, acc_ready = (sem("x1_ready"), sem("x1_hi_ready"), sem("x1_lo_ready"),
                                                         sem("acc_ready"))
        key_scored, keys_taken, chain, asked, exp_ready = (sem("key_scored"), sem("keys_taken"), sem("chain"),
                                                           sem("asked"), sem("exp_ready"))
        picked, pick_scaled = sem("picked"), sem("pick_scaled")
        sel_ready, sel_turned, sel_t_ready = sem("sel_ready"), sem("sel_turned"), sem("sel_t_ready")
        hot_matched = sem("hot_matched")
        hot_ready, quad_done, quad_staged = sem("hot_ready"), sem("quad_done"), sem("quad_staged")
        stage_out = [sem("stage_out0"), sem("stage_out1")]
        gate_landed, hid_ready, gated_ready = sem("gate_landed"), sem("hid_ready"), sem("gated_ready")
        a_hi_ready, a_lo_ready = sem("a_hi_ready"), sem("a_lo_ready")
        out_ready, out_stored = sem("out_ready"), sem("out_stored")

        block = ctx.enter_context(nc.Block())
        gates_r = gates.rearrange("c p (g f) -> p c g f", f=EG * CG)

        @block.sync
        def _(sp):
            def load(n, b, src):
                if not (isinstance(n, int) and n < 2):
                    sp.wait_ge(lo_ready, n - 1)
                sp.dma_start(raw[b][:].rearrange("p k c -> p (k c)"), src).then_inc(w_landed[b], 16)

            load(0, 0, w_in[0])
            for c, (a, w) in enumerate(X_PARTS):
                sp.dma_start(mix[:, a:a + w, :], x_t[:, a:a + w, :]).then_inc(x_landed[c], 16)
            load(1, 1, w_in[1])
            for dst, a, b in ((ident, K_IDENT, K_IOTA), (iota, K_IOTA, K_MASK), (mask, K_MASK, K_ROT),
                              (rope_m, K_ROT, N_CONST)):
                sp.dma_start(dst[:, :], consts[:, a:b]).then_inc(const_landed, 16)
            sp.dma_start(par[:, :], params).then_inc(const_landed, 16)
            sp.dma_start(posi[:, :], pos.to_broadcast([P, S])).then_inc(pos_landed, 16)
            pair = w_in.rearrange("(a b) p f -> a b p f", b=2)
            with sp.Fori(1, T_GA // 2) as i:
                for b in range(2):
                    load(2 * i + b, b, pair[i, b])
            ga = w_in[T_GA:, :, :].rearrange("(i h q) p f -> i h q p f", h=2, q=2)
            conv = w_conv.rearrange("(i h) p f -> i h p f", h=2)
            with sp.Fori(0, KD // 4) as i:
                for h in range(2):
                    for q in range(3):
                        o = 3 * h + q
                        load(6 * i + T_GA + o, o % 2, ga[i, h, q] if q < 2 else conv[i, h])
            wm = w_mix.rearrange("(a b) p f -> a b p f", b=2)
            xr = x_t.rearrange("p (a b) s -> a b p s", b=2)
            for b in range(2):
                load(T_MIX + b, b, wm[0, b])
                sp.dma_start(x_res[b][:, :], xr[0, b]).then_inc(x_res_landed[b], 16)
            with sp.Fori(1, KD // 2) as i:
                for b in range(2):
                    load(2 * i + T_MIX + b, b, wm[i, b])
                    sp.wait_ge(z_read[b], i + T_MIX // 2)
                    sp.dma_start(x_res[b][:, :], xr[i, b]).then_inc(x_res_landed[b], 16)
            wr = w_route.rearrange("(a b) p f -> a b p f", b=2)
            with sp.Fori(0, HEADS_R) as i:
                for b in range(2):
                    load(2 * i + T_ROUTE + b, b, wr[i, b])
            u = exp_u.rearrange("(g e) p f -> g e p f", e=EG)
            v = exp_v.rearrange("(g e) p f -> g e p f", e=KD // 2)
            for e in range(EG - 1):
                load(T_PEER + e, e % 2, u[0, e])
            c = 0
            for e, quads in QUADS_OF.items():
                n = T_PEER + e + 3
                for r in range(4 * quads // CG):
                    if r == 3 and e - 1 in QUADS_OF:
                        load(n, n % 2, u[0, e + 3] if e + 3 < EG else v[0, e + 3 - EG])
                    sp.wait_ge(quad_staged, CG // 4 * (c + 1))
                    sp.dma_start(gates[c], stage[c % 2][:].rearrange("p k c -> p (k c)")).then_inc(stage_out[c % 2], 16)
                    c += 1
            sp.wait_ge(stage_out[0], 16 * (N_CG // 2))
            sp.wait_ge(stage_out[1], 16 * (N_CG // 2))
            sp.dma_start(gate[:], gates_r[:, :, 0, :]).then_inc(gate_landed, 16)
            load(T_PEER + EG + 1, 1, v[0, 1])

            def group(g, first, last):
                n = GROUP_TILES * g + T_PEER
                for e in range(0 if first else EG):
                    load(n + e, e % 2, u[g, e])
                for e in range(2 if first else 0, KD // 2):
                    load(n + EG + e, e % 2, v[g, e])
                    if e == 2 and not last:
                        sp.wait_ge(gated_ready, EG * g + EG)
                        sp.dma_start(gate[:], gates_r[:, :, g + 1, :]).then_inc(gate_landed, 16)

            group(0, True, False)
            with sp.Fori(1, N_GROUPS - 1) as g:
                group(g, False, False)
            group(N_GROUPS - 1, False, True)
            for k in range(KD):
                sp.wait_ge(out_ready, k + 1)
                sp.dma_start(out[:, k, :], mix[:, k, :]).then_inc(out_stored, 16)
            sp.wait_ge(out_stored, 16 * KD)

        @block.tensor
        def _(pe):
            def tile(n, b, hi, lo, ready=None):
                pe.wait_ge(hi_ready, n + 1)
                pe.wait_ge(lo_ready, n + 1)
                if not (isinstance(n, int) and n < 2):
                    pe.wait_ge(z_read[b], half(n, b))
                for k in range(KD):
                    if ready:
                        ready(k)
                    pe.matmul(z[:, 2 * b, :], w_hi[b][:, k, :], hi[:, k, :], start=k == 0, stop=False)
                    pe.matmul(z[:, 2 * b, :], w_hi[b][:, k, :], lo[:, k, :], start=False, stop=False)
                    m = pe.matmul(z[:, 2 * b, :], w_lo[b][:, k, :], hi[:, k, :], start=False, stop=k == KD - 1)
                m.then_inc(tile_done, 1)

            def tile2(n, b, hi, lo, ready=None):
                pe.wait_ge(hi_ready, n + 1)
                pe.wait_ge(lo_ready, n + 1)
                pe.wait_ge(z_read[b], half(n, b))
                for s in range(2):
                    for k in range(8):
                        if ready and s == 0:
                            ready(k)
                        pe.matmul(z[:, 2 * b + s, :], w_hi[b][:, 8 * s + k, :], hi[:, k, :], start=k == 0, stop=False)
                        pe.matmul(z[:, 2 * b + s, :], w_hi[b][:, 8 * s + k, :], lo[:, k, :], start=False, stop=False)
                        m = pe.matmul(z[:, 2 * b + s, :], w_lo[b][:, 8 * s + k, :], hi[:, k, :],
                                      start=False, stop=k == 7)
                m.then_inc(tile_done, 1)

            def half(n, b):
                return n // 2 if isinstance(n, int) else n.half

            class Tile:
                def __init__(self, i, per, base, b):
                    self.n, self.half = 2 * per * i + base + b, per * i + base // 2

                def __add__(self, k):
                    return self.n + k

            def x_ready(k):
                for c, (a, w) in enumerate(X_PARTS):
                    if k == a:
                        pe.wait_ge(x_hi_ready, c + 1)
                        pe.wait_ge(x_lo_ready, c + 1)

            tile(0, 0, act_hi, act_lo, x_ready)
            tile(1, 1, act_hi, act_lo)
            with pe.Fori(1, KC) as i:
                for b in range(2):
                    tile(Tile(i, 1, 0, b), b, act_hi, act_lo)
            pe.wait_ge(const_landed, 16 * 5)

            def keys(kt):
                pe.wait_ge(z_read[kt], T_K // 2 + 1)
                for g in range(2):
                    a, rot = 2 * g, 2 * g + 1
                    if kt:
                        pe.wait_ge(roped, g + 1)
                    pe.matmul(aux[:, a, :], rope_m[:, P * (1 + g):P * (2 + g)], zt[kt][:, :], start=True, stop=True)
                    pe.matmul(aux[:, rot, :], rope_m[:, P * (3 + g):P * (4 + g)], zt[kt][:, :],
                              start=True, stop=True).then_inc(k_rot, 1)

            def values(vt):
                pe.wait_ge(z_read[vt], T_V // 2 + 1)
                pe.wait_ge(roped, 4)
                for n in range(NB):
                    m = pe.transpose(aux[:, 2 + vt, n * P:n * P + P], zt[vt][:, n * P:n * P + P], ident[:, :])
                m.then_inc(v_turned, 1)

            def conv_sums():
                pe.wait_ge(ones_ready, 1)
                pe.wait_ge(u_summed, KC + 1)
                pe.matmul(z[:, 1, :], ones[:, :], lnc_usum[:, :], start=True, stop=True).then_inc(lnc["sum"], 1)

            def conv_squares():
                pe.wait_ge(sq_summed, KC + 1)
                pe.matmul(z[:, 3, :], ones[:, :], lnc_qsum[:, :], start=True, stop=True).then_inc(lnc["sqsum"], 1)

            def at_k(steps):
                return lambda k: steps[k]() if k in steps else None

            def rotate_pair(b, count, parts):
                pe.wait_ge(z_read[b], count)
                pe.wait_ge(rope_part, parts)
                pe.matmul(aux[:, b, :], rope_m[:, 0:P], zt[b][:, :], start=True, stop=True).then_inc(q_rot, 1)

            tile(T_K, 0, act_hi, act_lo)
            tile(T_K + 1, 1, act_hi, act_lo)
            tile(T_V, 0, act_hi, act_lo, at_k({3: lambda: keys(0)}))
            tile(T_V + 1, 1, act_hi, act_lo, at_k({3: lambda: keys(1), 13: conv_sums}))
            tile(T_Q, 0, act_hi, act_lo, at_k({4: lambda: values(0), 11: lambda: values(1)}))
            tile(T_Q + 1, 1, act_hi, act_lo, at_k({4: lambda: rotate_pair(0, T_Q // 2 + 1, 2 * N_KV), 13: conv_squares}))
            with pe.Fori(1, LOOP_Q // 2) as i:
                tile(Tile(i, 1, T_Q, 0), 0, act_hi, act_lo,
                     at_k({4: lambda: rotate_pair(1, i + T_Q // 2, 4 * i + 2 * N_KV - 4)}))
                tile(Tile(i, 1, T_Q, 1), 1, act_hi, act_lo,
                     at_k({4: lambda: rotate_pair(0, i + T_Q // 2 + 1, 4 * i + 2 * N_KV - 2)}))

            units = [(g, n) for g in range(N_KV) for n in range(NB)]

            def scores(u, j):
                g, n = units[u]
                lo_c, w = max(n - 1, 0) * P, P if n == 0 else 2 * P
                if n == 0 and j == 0:
                    pe.wait_ge(roped, N_KV + max(4 * g + 4, LOOP_Q))
                if u or j:
                    pe.wait_ge(masked, 4 * u + j)
                for e in range(2):
                    m = pe.matmul(aux[:, e, 0:w], mix[64 * e:64 * e + 64, 4 * g + j, n * P:n * P + P],
                                  kT[64 * e:64 * e + 64, g, lo_c:lo_c + w], start=True, stop=True)
                m.then_inc(scored, 1)

            def turned_before(u):
                return sum(2 if n == 0 else 4 for g, n in units[:u])

            def turn(u, t):
                g, n = units[u]
                w = 1 if n == 0 else 2
                e, kb = t // w, t % w
                if t == 0:
                    pe.wait_ge(p_ready, u + 1)
                before = turned_before(u) + t - 1
                if before >= 1:
                    pe.wait_ge(pT_ready, before)
                else:
                    pe.wait_ge(v_ready, 2)
                for j in range(4):
                    m = pe.transpose(aux[:, 2 + t % 2, j * P:j * P + P],
                                     prob[u % 2][:, j, e, 1 + kb * P:1 + kb * P + P], ident[:, :])
                m.then_inc(p_turned, 1)

            def values_out(u, e):
                g, n = units[u]
                w = 1 if n == 0 else 2
                if u and e == 0:
                    pe.wait_ge(y_ready, u)
                for kb in range(w):
                    pe.wait_ge(pT_ready, turned_before(u) + w * e + kb + 1)
                    m = pe.matmul(z[64 * e:64 * e + 64, 1, :], vN[:, n - w + 1 + kb, g * HEAD:g * HEAD + HEAD],
                                  prT[:, w * e + kb, :], start=kb == 0, stop=kb == w - 1)
                if e == 1:
                    m.then_inc(pv_done, 1)

            def rotate(q):
                pe.wait_ge(z_read[q % 2], (T_Q + q) // 2 + 1)
                if q == LOOP_Q:
                    pe.wait_ge(lnc["var"], 1)
                else:
                    pe.wait_ge(rope_part, 2 * N_KV + 2 * q - 1)
                pe.matmul(z[:, 3, :], rope_m[:, 0:P], zt[q % 2][:, :], start=True, stop=True).then_inc(q_rot, 1)

            for s in range(N_SLOTS):
                score_at = (1, 4, 7, 10) if s else (7, 9, 11, 13)

                def beside(k):
                    if s == 0 and k == 2:
                        rotate_pair(1, (T_Q + LOOP_Q) // 2, 2 * LOOP_Q + 2 * N_KV - 4)
                    if s < N_UNITS and k in score_at:
                        scores(s, score_at.index(k))
                    if 1 <= s <= N_UNITS and k >= 11:
                        t = {11: 0, 12: 1, 14: 2, 15: 3}.get(k)
                        if t is not None and t < (2 if units[s - 1][1] == 0 else 4):
                            turn(s - 1, t)
                    if 2 <= s < N_UNITS + 2 and k in (2, 5):
                        values_out(s - 2, k // 3)
                    if 1 <= s <= KD - LOOP_Q and k == 8:
                        rotate(LOOP_Q + s - 1)
                tile(T_SLOT + s, s % 2, act_hi, act_lo, beside)

            with pe.Fori(0, KD // 4) as i:
                for h in range(2):
                    for q in range(3):
                        o = 3 * h + q
                        n = Tile(i, 3, T_GA + o - o % 2, o % 2)
                        if q < 2:
                            tile(n, o % 2, act_hi, act_lo)
                        else:
                            pe.wait_ge(u_hi_ready, 1)
                            pe.wait_ge(u_lo_ready, 1)
                            tile2(n, o % 2, u_hi, u_lo)

            def m_ready(k):
                for c, (a, w) in enumerate(M_PARTS):
                    if k == a:
                        pe.wait_ge(m_hi_ready, c + 1)
                        pe.wait_ge(m_lo_ready, c + 1)

            def norm_shift(tag, n):
                pe.wait_ge(z_read[n % 2], n // 2 + 1)
                pe.matmul(aux[:, 0, :], ones[:, :], mix[:, 0, :], start=True, stop=True)\
                  .then_inc(lns[tag]["shift_sum"], 1)

            def norm_sums(tag, bufs, steps, w):
                for bank, src, count, done in ((1, "sum_d", 2 * steps - 3, "mean_sum"), (2, "sum_q", 2 * steps - 1, "sq_sum")):
                    pe.wait_ge(lns[tag]["summed"], count)
                    for k in range(w):
                        row = bufs[src][:, k, :] if w > 1 else bufs[src][:, :]
                        m = pe.matmul(aux[:, bank, :], ones[:, :], row, start=k == 0, stop=k == w - 1)
                    m.then_inc(lns[tag][done], 1)

            tile(T_MIX, 0, act_hi, act_lo, m_ready)
            tile(T_MIX + 1, 1, act_hi, act_lo, lambda k: norm_shift("1", T_MIX) if k == 4 else None)
            with pe.Fori(1, KD // 2) as i:
                for b in range(2):
                    tile(Tile(i, 1, T_MIX, b), b, act_hi, act_lo)
            norm_sums("1", ln1, KD, 1)

            def key_scores(t):
                pe.wait_ge(z_read[t % 2], (T_ROUTE + t) // 2 + 1)
                if t >= 4:
                    pe.wait_ge(keys_taken, t - 3)
                for c in range(NB):
                    m = pe.matmul(aux[:, t % 4, c * P:c * P + P], rq[t % 2][:, c * P:c * P + P],
                                  par[:, C_KEYS + (t % 2) * NKEY:C_KEYS + (t % 2 + 1) * NKEY], start=True, stop=True)
                m.then_inc(key_scored, 1)

            def x1_block(k):
                pe.wait_ge(x1_hi_ready, k + 1)
                pe.wait_ge(x1_lo_ready, k + 1)

            for t in range(2 * HEADS_R):
                tile(T_ROUTE + t, t % 2, act_hi, act_lo,
                     lambda k: x1_block(k) if t == 0 else key_scores(t - 1) if k == 3 else None)

            def turn_chosen():
                pe.wait_ge(sel_ready, HEADS_R)
                for m_, src in enumerate((lambda c: sel_i[:, 0, c, :], lambda c: sel_i[:, 1, c, :],
                                          lambda c: sel_g[:, c, :])):
                    for c in range(NB):
                        m = pe.transpose(aux[:, m_, c * P:c * P + P], src(c), ident[:, :])
                    m.then_inc(sel_turned, 1)

            def quad_mm(q):
                pe.wait_ge(hot_ready, q + 1)
                if q >= 4:
                    pe.wait_ge(quad_staged, q - 3)
                else:
                    pe.wait_ge(sel_t_ready, 3)
                for c in range(4):
                    s_ = 4 * (q % 4) + c
                    m = pe.matmul(aux[:, q % 4, c * P:c * P + P], hot[:, 1, s_, :], hot[:, 0, s_, :],
                                  start=True, stop=True)
                m.then_inc(quad_done, 1)

            quads = [0]
            for e in range(EG):
                first_k = 8 if e == min(QUADS_OF) else 0
                per_k = QUADS_OF.get(e, 0) // (KD - first_k)

                def beside(k):
                    if e == 0 and k == 2:
                        key_scores(2 * HEADS_R - 1)
                    if e == min(QUADS_OF) and k == 5:
                        turn_chosen()
                    if k >= first_k:
                        for _ in range(per_k):
                            quad_mm(quads[0])
                            quads[0] += 1
                tile(T_PEER + e, e % 2, act_hi, act_lo, beside)

            def outputs(g, last=False):
                for j in range(KD // 2):
                    def a_ready(k):
                        if j == 0:
                            pe.wait_ge(a_hi_ready, EG * g + k + 1)
                            pe.wait_ge(a_lo_ready, EG * g + k + 1)
                        if last and j == 1 and k == 2:
                            norm_shift("2", GROUP_TILES * g + T_PEER + EG)
                    n = GROUP_TILES * g + T_PEER + EG + j if isinstance(g, int) else Tile(g, EG, T_PEER + EG + j - j % 2, j % 2)
                    tile2(n, j % 2, a_hi, a_lo, a_ready)

            outputs(0)
            with pe.Fori(1, N_GROUPS - 1) as g:
                for e in range(EG):
                    tile(Tile(g, EG, T_PEER + e - e % 2, e % 2), e % 2, act_hi, act_lo)
                outputs(g)
            for e in range(EG):
                tile(N_TILES - GROUP_TILES + e, e % 2, act_hi, act_lo)
            outputs(N_GROUPS - 1, True)
            norm_sums("2", ln2, KD // 2, 2)

        @block.scalar
        def _(act):
            def hi(n, b):
                act.wait_ge(w_landed[b], 16 * (n // 2) + 16 if isinstance(n, int) else 8 * n + 16 - 8 * b)
                if not (isinstance(n, int) and n < 2):
                    act.wait_ge(tile_done, n - 1)
                act.activation(w_hi[b][:], raw[b][:], ACT.Copy).then_inc(hi_ready, 1)

            hi(0, 0)
            for c, (a, w) in enumerate(X_PARTS):
                act.wait_ge(x_landed[c], 16)
                act.activation(act_hi[:, a:a + w, :], mix[:, a:a + w, :], ACT.Copy)\
                   .then_inc(x_hi_ready, 1)
            hi(1, 1)

            with act.Fori(0, KC) as i:
                act.wait_ge(zt_used, i + 1)
                act.wait_ge(tile_done, 2 * i + 1)
                act.activation(zt[0][:, :], z[:, 0, :], ACT.Identity, scale=0.5,
                               bias=half_b[:, ds(2 * i, 1)]).then_inc(z_read[0], 1)
                hi(2 * i + 2, 0)
                act.wait_ge(tile_done, 2 * i + 2)
                act.activation(zt[1][:, :], z[:, 2, :], ACT.Tanh, scale=0.5,
                               bias=half_b[:, ds(2 * i + 1, 1)]).then_inc(z_read[1], 1)
                hi(2 * i + 3, 1)
            act.wait_ge(angle_ready, 1)
            act.activation(sinT[:, :], t1[0][:, :], ACT.Sin).then_inc(sincos_ready, 1)
            act.wait_ge(angle_ready, 2)
            act.activation(cosT[:, :], t1[1][:, :], ACT.Sin).then_inc(sincos_ready, 1)
            act.wait_ge(zt_used, KC + 1)
            for t in range(2):
                n = T_K + t
                act.wait_ge(tile_done, n + 1)
                act.activation(zt[t][:, :], z[:, 2 * t, :], ACT.Identity, bias=par[:, n:n + 1]).then_inc(z_read[t], 1)
                hi(n + 2, t)
            for t in range(2):
                n = T_V + t
                act.wait_ge(tile_done, n + 1)
                act.wait_ge(roped, 2 * t + 2)
                act.activation(zt[t][:, :], z[:, 2 * t, :], ACT.Identity, bias=par[:, n:n + 1]).then_inc(z_read[t], 1)
                hi(n + 2, t)
            for k in range(KC):
                act.wait_ge(lnc["centred"], k + 1)
                if k >= 2:
                    act.wait_ge(sq_summed, k)
                act.activation(lnc_sq[k % 2][:, :], uT[:, k, 0:S], ACT.Square).then_inc(lnc["squared"], 1)
            act.wait_ge(v_turned, 2)
            for vt in range(2):
                act.activation(vN[:, :, vt * P:vt * P + P], aux[:, 2 + vt, :].rearrange("p (n f) -> p n f", n=NB),
                               ACT.Copy).then_inc(v_ready, 1)

            def queries(q, n, b, bias):
                act.wait_ge(rope_part, 2 * q + 2 * N_KV - 2)
                act.wait_ge(tile_done, n + 1)
                act.activation(zt[b][:, :], z[:, 2 * b, :], ACT.Identity, bias=bias).then_inc(z_read[b], 1)

            def conv_silu(first):
                for k in range(first, first + 4):
                    act.wait_ge(lnc["scaled"], k + 1)
                    act.activation(uT[:, k, 0:S], uT[:, k, 0:S], ACT.Silu, scale=par[:, C_CLNG + k:C_CLNG + k + 1],
                                   bias=par[:, C_CLNB + k:C_CLNB + k + 1]).then_inc(lnc["done"], 1)

            for q in range(4):
                b = q % 2
                queries(q, T_Q + q, b, par[:, T_Q + q:T_Q + q + 1])
                hi(T_Q + q + 2, b)
                if q == 1:
                    act.wait_ge(lnc["var"], 1)
                    act.activation(lnc_sd[:, :], lnc_var[:, :], ACT.Sqrt).then_inc(lnc["sd"], 1)
                if q >= 2:
                    conv_silu(4 * q - 8)
            act.wait_ge(lnc["done"], KC)
            act.dma_start(u_kept, uT[:, 0:KC, 0:S]).then_inc(u_stored, 16)
            with act.Fori(2, LOOP_Q // 2) as i:
                for b in range(2):
                    n = 2 * i + T_Q + b
                    queries(2 * i + b, n, b, par[:, ds(n, 1)])
                    hi(n + 2, b)

            def square(tag, bufs, t, b, rows):
                sems = lns[tag]
                act.wait_ge(sems["shifted"], t + 1)
                if not (isinstance(t, int) and t < 2):
                    act.wait_ge(sems["summed"], 2 * t - 2)
                dst = bufs[f"sq{b}"]
                act.activation(dst[:], rows, ACT.Square).then_inc(sems["squared"], 1)

            def root(tag, bufs):
                act.wait_ge(lns[tag]["var"], 1)
                act.activation(bufs["sd"][:, :], bufs["var"][:, :], ACT.Sqrt).then_inc(lns[tag]["sd"], 1)

            units = [(g, n) for g in range(N_KV) for n in range(NB)]
            turned = [0]

            def exps(u):
                g, n = units[u]
                w = P if n == 0 else 2 * P
                act.wait_ge(maxed, u + 1)
                for j in range(4):
                    for e in range(2):
                        row = prob[u % 2][:, j, e, 0:1 + w]
                        m = act.activation(row, row, ACT.Exp, bias=smax[:, u % 2, 1, 2 * j + e:2 * j + e + 1],
                                           accum_out=smax[:, u % 2, 2, 2 * j + e:2 * j + e + 1])
                m.then_inc(exped, 1)

            def copies(u):
                g, n = units[u]
                if u:
                    act.wait_ge(pv_done, u)
                for t in range(2 if n == 0 else 4):
                    act.wait_ge(p_turned, turned[0] + 1)
                    act.activation(prT[:, t, :], aux[:, 2 + t % 2, :], ACT.Copy).then_inc(pT_ready, 1)
                    turned[0] += 1

            def heads_out(u):
                g, n = units[u]
                act.wait_ge(pv_done, u + 1)
                act.activation(mix[:, 4 * g:4 * g + 4, n * P:n * P + P],
                               z[:, 1, :].rearrange("p (j q) -> p j q", j=4), ACT.Copy).then_inc(y_ready, 1)

            def take(s):
                n, b = T_SLOT + s, s % 2
                if n < T_GB:
                    queries(n - T_Q, n, b, par[:, n:n + 1])
                else:
                    if n - T_GB >= 2:
                        act.wait_ge(gated_y, n - T_GB - 1)
                    elif n == T_GB:
                        act.wait_ge(roped, N_KV + KD)
                    act.wait_ge(tile_done, n + 1)
                    act.activation(sig_b[b][:, :], z[:, 2 * b, :], ACT.Sigmoid, bias=par[:, n:n + 1])\
                       .then_inc(z_read[b], 1)
                hi(n + 2, b)

            for s in range(N_SLOTS):
                if s:
                    take(s - 1)
                if 2 <= s < N_UNITS + 2:
                    heads_out(s - 2)
                if 1 <= s <= N_UNITS:
                    copies(s - 1)
                if s < N_UNITS:
                    exps(s)
                if s == N_UNITS + 1:
                    act.wait_ge(p_turned, turned[0])
                    act.wait_ge(u_stored, 16)
                    act.dma_start(u_back[:], u_kept).then_inc(u_landed, 16)
            take(N_SLOTS - 1)
            act.wait_ge(u_landed, 16)
            act.wait_ge(y_ready, N_UNITS)
            act.activation(u_hi[:], u_back[:], ACT.Copy).then_inc(u_hi_ready, 1)
            def m_hi(c):
                a_, w = M_PARTS[c]
                act.wait_ge(mixed, a_ + w)
                act.activation(act_hi[:, a_:a_ + w, :], mix[:, a_:a_ + w, :], ACT.Copy).then_inc(m_hi_ready, 1)

            def conv_gates(i, last):
                for h in range(2):
                    for q in range(3):
                        o = 3 * h + q
                        b = o % 2
                        n = 6 * i + T_GA + o
                        act.wait_ge(tile_done, n + 1)
                        if q < 2:
                            act.wait_ge(lo_ready, n + 2)
                            col = 4 * i + (T_GA + 2 * h + q)
                            act.activation(sig_a[q][:, :], z[:, 2 * b, :], ACT.Sigmoid,
                                           bias=par[:, ds(col, 1)]).then_inc(z_read[b], 1)
                        hi(n + 2, b)
                        if last and o == 4:
                            for c in range(len(M_PARTS) - 1):
                                m_hi(c)

            with act.Fori(0, KD // 4 - 1) as i:
                conv_gates(i, False)
            conv_gates(KD // 4 - 1, True)
            m_hi(len(M_PARTS) - 1)
            for b in range(2):
                act.wait_ge(tile_done, T_MIX + b + 1)
                hi(T_MIX + b + 2, b)
            for b in range(2):
                square("1", ln1, b, b, mix[:, b, :])
            with act.Fori(1, KD // 2) as i:
                for b in range(2):
                    n = 2 * i + T_MIX + b
                    act.wait_ge(tile_done, n + 1)
                    hi(n + 2, b)
                    square("1", ln1, 2 * i + b, b, mix[:, ds(2 * i + b, 1), :].rearrange("p o s -> p (o s)"))
            root("1", ln1)
            for k in range(KD + 1):
                if k < KD:
                    act.wait_ge(lns["1"]["scaled"], k + 1)
                    act.activation(act_hi[:, k, :], mix[:, k, :], ACT.Identity, bias=par[:, C_LN1B + k:C_LN1B + k + 1])\
                       .then_inc(x1_hi_ready, 1)
                if k:
                    act.wait_ge(x1_hi_ready, k)
                    act.activation(mix[:, k - 1, :], mix[:, k - 1, :], ACT.Identity,
                                   bias=par[:, C_LN1B + k - 1:C_LN1B + k]).then_inc(x1_ready, 1)

            def exp_head(h):
                act.wait_ge(asked, h + 1)
                act.activation(expo[:, 1, :, :], expo[:, 0, :, :], ACT.Exp).then_inc(exp_ready, 1)

            for t in range(2 * HEADS_R):
                b, n = t % 2, T_ROUTE + t
                act.wait_ge(tile_done, n + 1)
                if t >= 2:
                    act.wait_ge(key_scored, t - 1)
                act.activation(rq[b][:, :], z[:, 2 * b, :], ACT.Copy).then_inc(z_read[b], 1)
                hi(n + 2, b)
                if t % 2 and t > 1:
                    exp_head(t // 2 - 1)
                if 2 <= t < 6:
                    act.wait_ge(x1_lo_ready, KD)
                    part = mix[:, 4 * (t - 2):4 * (t - 2) + 4, :]
                    act.activation(part, part, ACT.Copy, scale=ALPHA).then_inc(acc_ready, 1)

            def quad_copy(q):
                act.wait_ge(quad_done, q + 1)
                c, r = divmod(q, CG // 4)
                if r == 0 and c >= 2:
                    act.wait_ge(stage_out[c % 2], 16 * (c // 2))
                dst = stage[c % 2][:, :, 4 * r:4 * r + 4].rearrange("p k c -> p c k")
                act.activation(dst, aux[:, q % 4, :].rearrange("p (c k) -> p c k", c=4), ACT.Copy)\
                   .then_inc(quad_staged, 1)

            quads = 0
            for e in range(EG):
                if e == min(QUADS_OF) - 1:
                    exp_head(HEADS_R - 1)
                if e == min(QUADS_OF):
                    for m_, dst in enumerate((i_t[:, 0, :], i_t[:, 1, :], g_t[:, :])):
                        act.wait_ge(sel_turned, m_ + 1)
                        act.activation(dst, aux[:, m_, :], ACT.Copy).then_inc(sel_t_ready, 1)
                for _ in range(QUADS_OF.get(e, 0)):
                    quad_copy(quads)
                    quads += 1
                act.wait_ge(tile_done, T_PEER + e + 1)
                if e == 3:
                    act.wait_ge(sel_ready, HEADS_R)
                act.activation(hid_0[:, e, :], z[:, 2 * (e % 2), :], ACT.Gelu).then_inc(z_read[e % 2], 1)
                hi(T_PEER + e + 2, e % 2)
            for e in range(EG):
                act.wait_ge(gated_ready, e + 1)
                act.activation(a_hi[:, e, :], gated[e % 2][:, :], ACT.Copy).then_inc(a_hi_ready, 1)

            def group(g, last):
                n0 = GROUP_TILES * g + T_PEER
                for e in range(0 if isinstance(g, int) and g == 0 else EG):
                    b = e % 2
                    act.wait_ge(gated_ready, EG * g + e - 1)
                    act.wait_ge(tile_done, n0 + e + 1)
                    act.activation(hid[b][:, :], z[:, 2 * b, :], ACT.Gelu).then_inc(z_read[b], 1)
                    act.wait_ge(gated_ready, EG * g + e + 1)
                    act.activation(a_hi[:, e, :], gated[b][:, :], ACT.Copy).then_inc(a_hi_ready, 1)
                    hi(n0 + e + 2, b)
                for j in range(KD // 2):
                    if not (last and j >= KD // 2 - 2):
                        act.wait_ge(tile_done, n0 + EG + j + 1)
                        hi(n0 + EG + j + 2, j % 2)
                    if last and j:
                        for t in ((0, 1) if j == 1 else (j,)):
                            square("2", ln2, t, t % 2, mix[:, 2 * t:2 * t + 2, :])

            group(0, False)
            with act.Fori(1, N_GROUPS - 1) as g:
                group(g, False)
            group(N_GROUPS - 1, True)
            root("2", ln2)
            for k in range(KD):
                act.wait_ge(lns["2"]["scaled"], k + 1)
                act.activation(mix[:, k, :], mix[:, k, :], ACT.Identity, bias=par[:, C_LN2B + k:C_LN2B + k + 1])\
                   .then_inc(out_ready, 1)

        @block.vector
        def _(dve):
            links = [0]

            def link(ins):
                links[0] += 1
                ins.then_inc(chain, 1)
                dve.wait_ge(chain, links[0])

            def lo(n, b):
                dve.wait_ge(hi_ready, n + 1)
                dve.tensor_tensor(w_lo[b][:], raw[b][:], w_hi[b][:].bitcast(F32), ALU.subtract).then_inc(lo_ready, 1)

            lo(0, 0)
            for c, (a, w) in enumerate(X_PARTS):
                dve.wait_ge(x_hi_ready, c + 1)
                dve.tensor_tensor(act_lo[:, a:a + w, :], mix[:, a:a + w, :],
                                  act_hi[:, a:a + w, :].bitcast(F32), ALU.subtract).then_inc(x_lo_ready, 1)
            lo(1, 1)
            dve.wait_ge(const_landed, 16 * 5)
            dve.tensor_scalar(half_b[:, :], par[:, C_BIAS:C_BIAS + 2 * KC], 0.5, None, ALU.mult).then_inc(zt_used, 1)
            dve.wait_ge(pos_landed, 16)
            link(dve.tensor_copy(t2[0][:, :], posi[:, :]))
            link(dve.tensor_scalar(cosT[:, :], t2[0][:, :], rope_m[:, 5 * P:5 * P + 1], None, ALU.mult))
            link(dve.tensor_scalar(t2[0][:, :], cosT[:, :], float(1 / (2 * np.pi)), ROUNDER, ALU.mult, ALU.add))
            link(dve.tensor_scalar(t2[1][:, :], t2[0][:, :], ROUNDER, None, ALU.subtract))
            for c in (TWO_PI_A, TWO_PI_B, TWO_PI_C):
                link(dve.scalar_tensor_tensor(out=cosT[:, :], in0=t2[1][:, :], scalar=-float(c), in1=cosT[:, :],
                                              op0=ALU.mult, op1=ALU.add))
            dve.tensor_scalar(t1[0][:, :], cosT[:, :], 3.1415925, -3.1415925, ALU.min, ALU.max)\
               .then_inc(angle_ready, 1)
            dve.wait_ge(angle_ready, 1)
            link(dve.scalar_tensor_tensor(out=t2[0][:, :], in0=t1[0][:, :], scalar=-1.0, in1=t1[0][:, :],
                                          op0=ALU.mult, op1=ALU.max))
            dve.tensor_scalar(t1[1][:, :], t2[0][:, :], -1.0, float(np.pi / 2), ALU.mult, ALU.add)\
               .then_inc(angle_ready, 1)
            dve.wait_ge(angle_ready, 2)

            dve.wait_ge(pads_ready, 1)
            with dve.Fori(0, KC) as i:
                dve.wait_ge(z_read[0], i + 1)
                dve.wait_ge(z_read[1], i + 1)
                dve.scalar_tensor_tensor(out=uT[:, ds(i + 1, 1), PAD:SLOT].rearrange("p o s -> p (o s)"),
                                         in0=zt[1][:, :], scalar=1.0, in1=zt[0][:, :],
                                         op0=ALU.add, op1=ALU.mult).then_inc(zt_used, 1)
                row = uT[:, ds(i, 1), 0:S].rearrange("p o s -> p (o s)")
                for w in range(TAPS):
                    src = uT[:, ds(i + 1, 1), w:w + S].rearrange("p o s -> p (o s)")
                    dst = odd_taps[:, :] if w % 2 else row
                    tap = par[:, ds(TAPS * i + C_TAPS + w, 1)]
                    dve.wait_ge(*((tap_done, TAPS * i + w - 1) if w >= 2 else (zt_used, i + 2)))
                    if w == 0:
                        m = dve.tensor_scalar(dst, src, tap, par[:, ds(i + C_CONVB, 1)], ALU.mult, ALU.add)
                    elif w == 1:
                        m = dve.tensor_scalar(dst, src, tap, None, ALU.mult)
                    else:
                        m = dve.scalar_tensor_tensor(out=dst, in0=src, scalar=tap, in1=dst, op0=ALU.mult, op1=ALU.add)
                    m.then_inc(tap_done, 1)
                dve.wait_ge(tap_done, TAPS * i + TAPS)
                dve.tensor_tensor(row, row, odd_taps[:, :], ALU.add).then_inc(convolved, 1)

            dve.wait_ge(sincos_ready, 2)

            def rope_keys(g):
                dve.wait_ge(k_rot, g + 1)
                a = 2 * (g % 2)
                dve.tensor_tensor(t1[0][:, :], aux[:, a + 1, :], sinT[:, :], ALU.mult).then_inc(rope_part, 1)
                dve.tensor_tensor(t2[0][:, :], aux[:, a, :], cosT[:, :], ALU.mult).then_inc(rope_part, 1)
                dve.wait_ge(rope_part, 2 * g + 2)
                dve.tensor_tensor(kT[:, g, :], t1[0][:, :], t2[0][:, :], ALU.add).then_inc(roped, 1)
                dve.wait_ge(roped, g + 1)

            rope_keys(0)
            rope_keys(1)
            dve.wait_ge(lnc["sum"], 1)
            link(dve.tensor_copy(lnc_mean[:, :], z[:, 1, :]))
            for k in range(KC):
                dve.tensor_tensor(uT[:, k, 0:S], uT[:, k, 0:S], lnc_mean[:, :], ALU.subtract).then_inc(lnc["centred"], 1)
            rope_keys(2)
            rope_keys(3)

            def newton(rs, tt, sd, var, ready):
                link(dve.reciprocal(rs[:, :], sd[:, :]))
                link(dve.scalar_tensor_tensor(out=tt[:, :], in0=rs[:, :], scalar=-0.5, in1=rs[:, :],
                                              op0=ALU.mult, op1=ALU.mult))
                link(dve.tensor_tensor(tt[:, :], tt[:, :], var[:, :], ALU.mult))
                dve.scalar_tensor_tensor(out=rs[:, :], in0=tt[:, :], scalar=1.5, in1=rs[:, :],
                                         op0=ALU.add, op1=ALU.mult).then_inc(ready, 1)
                dve.wait_ge(ready, 1)

            def rope_query(q, b, rotated, row):
                dve.wait_ge(roped, q + N_KV - 1)
                dve.wait_ge(q_rot, q + 1)
                dve.tensor_tensor(t1[b][:, :], rotated, sinT[:, :], ALU.mult).then_inc(rope_part, 1)
                dve.tensor_tensor(t2[b][:, :], zt[b][:, :], cosT[:, :], ALU.mult).then_inc(rope_part, 1)
                dve.wait_ge(rope_part, 2 * q + 2 * N_KV + 2)
                dve.tensor_tensor(row, t1[b][:, :], t2[b][:, :], ALU.add).then_inc(roped, 1)

            rope_query(0, 0, aux[:, 0, :], mix[:, 0, :])
            dve.wait_ge(lnc["sqsum"], 1)
            dve.tensor_scalar(lnc_var[:, :], z[:, 3, :], EPS, None, ALU.add).then_inc(lnc["var"], 1)
            dve.wait_ge(lnc["sd"], 1)
            newton(lnc_rs, lnc_tt, lnc_sd, lnc_var, lnc["rs"])
            rope_query(1, 1, aux[:, 1, :], mix[:, 1, :])
            for k in range(KC):
                dve.tensor_tensor(uT[:, k, 0:S], uT[:, k, 0:S], lnc_rs[:, :], ALU.mult).then_inc(lnc["scaled"], 1)
            with dve.Fori(1, LOOP_Q // 2) as i:
                for b in range(2):
                    rope_query(2 * i + b, b, aux[:, b, :], mix[:, ds(2 * i + b, 1), :].rearrange("p o s -> p (o s)"))

            def wide(row, w):
                return row[:, :] if w == 1 else row[:, :].unsqueeze(1).to_broadcast([P, w, S])

            def norm_start(tag, bufs, rows, w):
                sems = lns[tag]
                dve.wait_ge(sems["shift_sum"], 1)
                link(dve.tensor_scalar(bufs["shift"][:, :], aux[:, 0, :], CC / P, None, ALU.mult))
                for t in range(2):
                    dve.tensor_tensor(rows(t), rows(t), wide(bufs["shift"], w), ALU.subtract).then_inc(sems["shifted"], 1)
                dve.wait_ge(sems["shifted"], 2)
                dve.tensor_tensor(bufs["sum_d"][:], rows(0), rows(1), ALU.add).then_inc(sems["summed"], 1)
                dve.wait_ge(sems["squared"], 1)
                dve.tensor_copy(bufs["sum_q"][:], bufs["sq0"][:]).then_inc(sems["summed"], 1)

            def norm_step(tag, bufs, t, b, row, w, between=None):
                sems = lns[tag]
                dve.tensor_tensor(row, row, wide(bufs["shift"], w), ALU.subtract).then_inc(sems["shifted"], 1)
                dve.wait_ge(sems["shifted"], t + 1)
                dve.wait_ge(sems["summed"], 2 * t - 2)
                dve.tensor_tensor(bufs["sum_d"][:], bufs["sum_d"][:], row, ALU.add).then_inc(sems["summed"], 1)
                if between:
                    between()
                dve.wait_ge(sems["squared"], t)
                dve.tensor_tensor(bufs["sum_q"][:], bufs["sum_q"][:], bufs[f"sq{1 - b}"][:], ALU.add)\
                   .then_inc(sems["summed"], 1)

            def norm_end(tag, bufs, steps):
                sems = lns[tag]
                dve.wait_ge(sems["squared"], steps)
                dve.wait_ge(sems["summed"], 2 * steps - 2)
                dve.tensor_tensor(bufs["sum_q"][:], bufs["sum_q"][:], bufs[f"sq{(steps - 1) % 2}"][:], ALU.add)\
                   .then_inc(sems["summed"], 1)
                dve.wait_ge(sems["mean_sum"], 1)
                dve.tensor_scalar(bufs["mean"][:, :], aux[:, 1, :], CC / D, None, ALU.mult).then_inc(sems["mean"], 1)
                dve.wait_ge(sems["mean"], 1)
                link(dve.tensor_tensor(bufs["tt"][:, :], bufs["mean"][:, :], bufs["mean"][:, :], ALU.mult))
                dve.wait_ge(sems["sq_sum"], 1)
                link(dve.scalar_tensor_tensor(out=bufs["var"][:, :], in0=aux[:, 2, :], scalar=CC / D, in1=bufs["tt"][:, :],
                                              op0=ALU.mult, op1=ALU.subtract))
                dve.tensor_scalar(bufs["var"][:, :], bufs["var"][:, :], 0.0, EPS, ALU.max, ALU.add).then_inc(sems["var"], 1)
                dve.wait_ge(sems["sd"], 1)
                newton(bufs["rs"], bufs["tt"], bufs["sd"], bufs["var"], sems["rs"])

            def scale(tag, bufs, k, gain):
                dve.wait_ge(lns[tag]["centred"], k + 1)
                dve.scalar_tensor_tensor(out=mix[:, k, :], in0=mix[:, k, :], scalar=par[:, gain + k:gain + k + 1],
                                         in1=bufs["rs"][:, :], op0=ALU.mult, op1=ALU.mult)\
                   .then_inc(lns[tag]["scaled"], 1)

            units = [(g, n) for g in range(N_KV) for n in range(NB)]

            def turned_upto(u):
                return sum(2 if n == 0 else 4 for g, n in units[:u + 1])

            def sinks(u):
                if u == 0:
                    dve.wait_ge(u_stored, 16)
                if u >= 2:
                    dve.wait_ge(p_turned, turned_upto(u - 2))
                g = units[u][0]
                dve.tensor_copy(prob[u % 2][:, :, :, 0:1].rearrange("p j e o -> p (j e o)"),
                                par[:, C_SINK + 8 * g:C_SINK + 8 * g + 8]).then_inc(sink_in, 1)

            def mask_scores(u, j):
                w = P if units[u][1] == 0 else 2 * P
                dve.wait_ge(scored, 4 * u + j + 1)
                dve.scalar_tensor_tensor(
                    out=prob[u % 2][:, j, :, 1:1 + w], in0=aux[:, 0:2, 0:w], scalar=SCALE,
                    in1=mask[:, 2 * P - w:2 * P].unsqueeze(1).to_broadcast([P, 2, w]),
                    op0=ALU.mult, op1=ALU.add).then_inc(masked, 1)

            def row_max(u):
                w = P if units[u][1] == 0 else 2 * P
                dve.wait_ge(masked, 4 * u + 4)
                dve.wait_ge(sink_in, u + 1)
                link(dve.tensor_reduce(smax[:, u % 2, 0, :],
                                       prob[u % 2][:, :, :, 0:1 + w].rearrange("p j e k -> p (j e) k"), AX, ALU.max))
                dve.tensor_scalar(smax[:, u % 2, 1, :], smax[:, u % 2, 0, :], -1.0, None, ALU.mult).then_inc(maxed, 1)

            def normalise(u):
                w = P if units[u][1] == 0 else 2 * P
                dve.wait_ge(exped, u + 1)
                link(dve.reciprocal(smax[:, u % 2, 3, :], smax[:, u % 2, 2, :]))
                for j in range(4):
                    for e in range(2):
                        row = prob[u % 2][:, j, e, 1:1 + w]
                        m = dve.tensor_scalar(row, row, smax[:, u % 2, 3, 2 * j + e:2 * j + e + 1], None, ALU.mult)
                m.then_inc(p_ready, 1)

            for s in range(N_SLOTS + 2):
                if s < N_UNITS:
                    sinks(s)
                    mask_scores(s, 0)
                    mask_scores(s, 1)
                if 1 <= s <= N_UNITS:
                    normalise(s - 1)
                k = T_SLOT + s - 2 - T_GB
                if k >= 0:
                    dve.wait_ge(z_read[k % 2], (T_GB + k) // 2 + 1)
                    dve.wait_ge(y_ready, NB * (k // 4 + 1))
                    dve.tensor_tensor(mix[:, k, :], mix[:, k, :], sig_b[k % 2][:, :], ALU.mult).then_inc(gated_y, 1)
                if s < N_UNITS:
                    mask_scores(s, 2)
                if 1 <= s <= KD - LOOP_Q:
                    q = LOOP_Q + s - 1
                    rope_query(q, q % 2, z[:, 3, :], mix[:, q, :])
                if s < N_UNITS:
                    mask_scores(s, 3)
                    row_max(s)

            dve.wait_ge(u_hi_ready, 1)
            dve.tensor_tensor(u_lo[:], u_back[:], u_hi[:].bitcast(F32), ALU.subtract).then_inc(u_lo_ready, 1)
            dve.wait_ge(lo_ready, POOL_A[1] + 1)
            dve.wait_ge(gated_y, KD)
            def m_lo(c):
                a_, w = M_PARTS[c]
                dve.wait_ge(m_hi_ready, c + 1)
                dve.tensor_tensor(act_lo[:, a_:a_ + w, :], mix[:, a_:a_ + w, :], act_hi[:, a_:a_ + w, :].bitcast(F32),
                                  ALU.subtract).then_inc(m_lo_ready, 1)

            def conv_gates(i, last):
                for h in range(2):
                    for q in range(3):
                        o = 3 * h + q
                        b = o % 2
                        n = 6 * i + T_GA + o
                        if q == 2:
                            for j in range(2):
                                if j == 0:
                                    dve.wait_ge(tile_done, n + 1)
                                    dve.wait_ge(z_read[1 - b], 3 * i + (T_GA + o - 1) // 2 + 1)
                                m = dve.tensor_tensor(sig_a[j][:, :], sig_a[j][:, :], z[:, 2 * b + j, :], ALU.mult)
                                m.then_inc(*((z_read[b], 1) if j else (prod_y, 1)))
                            for j in range(2):
                                row = mix[:, ds(4 * i + 2 * h + j, 1), :].rearrange("p o s -> p (o s)")
                                if j == 0:
                                    dve.wait_ge(prod_y, 2 * i + h + 1)
                                    dve.wait_ge(z_read[b], 3 * i + (T_GA + o) // 2 + 1)
                                dve.tensor_tensor(row, row, sig_a[j][:, :], ALU.add).then_inc(mixed, 1)
                        lo(n + 2, b)
                        if last and o == 4:
                            for c in range(len(M_PARTS) - 1):
                                m_lo(c)

            with dve.Fori(0, KD // 4 - 1) as i:
                conv_gates(i, False)
            conv_gates(KD // 4 - 1, True)
            m_lo(len(M_PARTS) - 1)
            dve.wait_ge(m_lo_ready, len(M_PARTS))
            def residual(n, b, x_count, row):
                dve.wait_ge(x_res_landed[b], x_count)
                dve.wait_ge(tile_done, n + 1)
                dve.scalar_tensor_tensor(out=row, in0=x_res[b][:, :], scalar=ALPHA, in1=z[:, 2 * b, :],
                                         op0=ALU.mult, op1=ALU.add).then_inc(z_read[b], 1)

            for b in range(2):
                residual(T_MIX + b, b, 16, mix[:, b, :])
                lo(T_MIX + b + 2, b)
            dve.wait_ge(z_read[1], T_MIX // 2 + 1)
            norm_start("1", ln1, lambda t: mix[:, t, :], 1)
            with dve.Fori(1, KD // 2) as i:
                for b in range(2):
                    row = mix[:, ds(2 * i + b, 1), :].rearrange("p o s -> p (o s)")
                    residual(2 * i + T_MIX + b, b, 16 * i + 16, row)
                    dve.wait_ge(z_read[b], i + T_MIX // 2 + 1)
                    norm_step("1", ln1, 2 * i + b, b, row, 1, lambda: lo(2 * i + T_MIX + b + 2, b))
            norm_end("1", ln1, KD)
            for k in range(KD + 2):
                if k < KD:
                    scale("1", ln1, k, C_LN1G)
                if k >= 2:
                    dve.wait_ge(x1_ready, k - 1)
                    dve.tensor_tensor(act_lo[:, k - 2, :], mix[:, k - 2, :], act_hi[:, k - 2, :].bitcast(F32),
                                      ALU.subtract).then_inc(x1_lo_ready, 1)

            def top16(dst_v, dst_i, src, spare, last):
                for c in range(NB):
                    m = dve.max(dst_v[:, c, 0:8], src[:, c, :])
                link(m)
                for c in range(NB):
                    dve.max_index(dst_i[:, c, 0:8], dst_v[:, c, 0:8], src[:, c, :])
                for c in range(NB):
                    m = dve.match_replace(spare[:, c, :], dst_v[:, c, 0:8], src[:, c, :], NEG)
                    if c == NB - 1 and last is not None:
                        m.then_inc(last, 1)
                if last is None:
                    link(m)
                else:
                    takes[0] += 1
                    dve.wait_ge(last, takes[0])
                for c in range(NB):
                    m = dve.max(dst_v[:, c, 8:16], spare[:, c, :])
                link(m)
                for c in range(NB):
                    m = dve.max_index(dst_i[:, c, 8:16], dst_v[:, c, 8:16], spare[:, c, :])
                link(m)

            takes = [0]

            def combine(h):
                link(dve.tensor_copy(idxf[:], idx[:]))
                link(dve.tensor_tensor(cand[:].rearrange("p c (a b) -> p c a b", a=TOPK),
                                       val[:, 0, :, :].unsqueeze(3).to_broadcast([P, NB, TOPK, TOPK]),
                                       val[:, 1, :, :].unsqueeze(2).to_broadcast([P, NB, TOPK, TOPK]), ALU.add))
                top16(best, place, cand, cand2, None)
                dve.tensor_tensor(expo[:, 0, :, :], best[:], best[:, :, 0:1].to_broadcast([P, NB, TOPK]), ALU.subtract)\
                   .then_inc(asked, 1)
                dve.tensor_scalar(digit[:, 0, :, :], place[:], 4, None, ALU.logical_shift_right)
                link(dve.tensor_scalar(digit[:, 1, :, :], place[:], 15, None, ALU.bitwise_and))
                link(dve.tensor_copy(digitf[:], digit[:].rearrange("p d c k -> p d (c k)")))
                for d in range(2):
                    dve.tensor_tensor(pick[:, d, :, :], digitf[:, d, :].unsqueeze(2).to_broadcast([P, NB * TOPK, TOPK]),
                                      iota[:, 0:TOPK].unsqueeze(1).to_broadcast([P, NB * TOPK, TOPK]), ALU.is_equal)\
                       .then_inc(picked, 1)

            def keep(h):
                for d in range(2):
                    dve.wait_ge(pick_scaled, 2 * h + d + 1)
                    dve.tensor_reduce(sel_i[:, d, :, h * TOPK:h * TOPK + TOPK],
                                      pick[:, d, :, :].rearrange("p (c k) a -> p c k a", c=NB), AX, ALU.add)
                dve.wait_ge(exp_ready, h + 1)
                link(dve.tensor_reduce(esum[:, 0, :], expo[:, 1, :, :], AX, ALU.add))
                link(dve.reciprocal(esum[:, 1, :], esum[:, 0, :]))
                dve.tensor_tensor(sel_g[:, :, h * TOPK:h * TOPK + TOPK], expo[:, 1, :, :],
                                  esum[:, 1, :].unsqueeze(2).to_broadcast([P, NB, TOPK]), ALU.mult)\
                   .then_inc(sel_ready, 1)
                dve.wait_ge(sel_ready, h + 1)

            for t in range(2 * HEADS_R):
                dve.wait_ge(key_scored, t + 1)
                top16(val[:, t % 2, :, :], idx[:, t % 2, :, :],
                      aux[:, t % 4, :].rearrange("p (c k) -> p c k", c=NB), rest, keys_taken)
                if t % 2:
                    combine(t // 2)
                elif t:
                    keep(t // 2 - 1)
            keep(HEADS_R - 1)

            dve.wait_ge(sel_t_ready, 3)
            for q in range(S // 4):
                if q in QUAD_LO:
                    dve.wait_ge(lo_ready, QUAD_LO[q])
                    lo(QUAD_LO[q], QUAD_LO[q] % 2)
                if q >= 4:
                    dve.wait_ge(quad_done, q - 3)
                dve.tensor_tensor(hot[:, :, 4 * (q % 4):4 * (q % 4) + 4, :],
                                  iota[:, :].unsqueeze(1).unsqueeze(1).to_broadcast([P, 2, 4, P]),
                                  i_t[:, :, 4 * q:4 * q + 4].unsqueeze(3).to_broadcast([P, 2, 4, P]),
                                  ALU.is_equal).then_inc(hot_matched, 1)

            def group(g, last):
                n0 = GROUP_TILES * g + T_PEER
                first = isinstance(g, int) and g == 0
                dve.wait_ge(gate_landed, 16 * g + 16)
                for e in range(EG):
                    b = e % 2
                    dve.wait_ge(z_read[b], EG * g + T_PEER // 2 + e // 2 + 1)
                    if not (first and e < 2):
                        dve.wait_ge(a_lo_ready, EG * g + e - 1)
                    src = hid_0[:, e, :] if first else hid[b][:, :]
                    dve.tensor_tensor(gated[b][:, :].rearrange("p (c s) -> p c s", c=N_CG),
                                      src.rearrange("p (c s) -> p c s", c=N_CG),
                                      gate[:, :, e * CG:e * CG + CG], ALU.mult).then_inc(gated_ready, 1)
                    dve.wait_ge(a_hi_ready, EG * g + e + 1)
                    dve.tensor_tensor(a_lo[:, e, :], gated[b][:, :], a_hi[:, e, :].bitcast(F32), ALU.subtract)\
                       .then_inc(a_lo_ready, 1)
                    if not first:
                        lo(n0 + e + 2, b)
                if first:
                    dve.wait_ge(lo_ready, POOL_R[1] + 1)
                for j in range(KD // 2):
                    b = j % 2
                    dve.wait_ge(tile_done, n0 + EG + j + 1)
                    if isinstance(g, int) and g == 0:
                        dve.wait_ge(acc_ready, 4)
                    else:
                        dve.wait_ge(z_read[b], EG * g + (T_PEER + EG - GROUP_TILES + j - b) // 2 + 1)
                    for s_ in range(2):
                        k = 2 * j + s_
                        m = dve.tensor_tensor(mix[:, k, :], mix[:, k, :], z[:, 2 * b + s_, :], ALU.add)
                    m.then_inc(z_read[b], 1)
                    if not (last and j >= KD // 2 - 2):
                        lo(n0 + EG + j + 2, b)
                    if last and j:
                        dve.wait_ge(z_read[b], (n0 + EG + j) // 2 + 1)
                        if j == 1:
                            norm_start("2", ln2, lambda t: mix[:, 2 * t:2 * t + 2, :], 2)
                        else:
                            norm_step("2", ln2, j, b, mix[:, 2 * j:2 * j + 2, :], 2)

            group(0, False)
            with dve.Fori(1, N_GROUPS - 1) as g:
                group(g, False)
            group(N_GROUPS - 1, True)
            norm_end("2", ln2, KD // 2)
            for k in range(KD):
                scale("2", ln2, k, C_LN2G)

        @block.gpsimd
        def _(pool):
            pool.memset(uT[:, :, 0:PAD], 0.0).then_inc(pads_ready, 1)
            pool.memset(ones[:, :], 1.0 / CC).then_inc(ones_ready, 1)

            def lo(n, b):
                pool.wait_ge(hi_ready, n + 1)
                pool.tensor_tensor(w_lo[b][:], raw[b][:], w_hi[b][:].bitcast(F32), ALU.subtract).then_inc(lo_ready, 1)

            pool.wait_ge(lo_ready, POOL_A[0])
            pool.memset(lnc_usum[:, :], 0.0).then_inc(u_summed, 1)
            pool.memset(lnc_qsum[:, :], 0.0).then_inc(sq_summed, 1)

            def add_conv(k, row):
                pool.wait_ge(convolved, k + 1)
                pool.wait_ge(u_summed, k + 1)
                pool.tensor_tensor(lnc_usum[:, :], lnc_usum[:, :], row, ALU.add).then_inc(u_summed, 1)

            for b in range(2):
                lo(2 + b, b)
            with pool.Fori(1, KC) as i:
                for b in range(2):
                    lo(2 * i + 2 + b, b)
                add_conv(i - 1, uT[:, ds(i - 1, 1), 0:S].rearrange("p o s -> p (o s)"))
            for b in range(2):
                lo(T_V + b, b)
            lo(T_Q, 0)
            add_conv(KC - 1, uT[:, KC - 1, 0:S])
            lo(T_Q + 1, 1)
            for k in range(KC):
                pool.wait_ge(lnc["squared"], k + 1)
                pool.wait_ge(sq_summed, k + 1)
                pool.tensor_tensor(lnc_qsum[:, :], lnc_qsum[:, :], lnc_sq[k % 2][:, :], ALU.add).then_inc(sq_summed, 1)
            with pool.Fori(T_Q // 2 + 1, (POOL_A[1] + 1) // 2) as i:
                for b in range(2):
                    lo(2 * i + b, b)

            def centre(tag, bufs, steps):
                pool.wait_ge(lns[tag]["mean"], 1)
                pool.wait_ge(lns[tag]["squared"], steps)
                for k in range(KD):
                    pool.tensor_tensor(mix[:, k, :], mix[:, k, :], bufs["mean"][:, :], ALU.subtract)\
                        .then_inc(lns[tag]["centred"], 1)

            centre("1", ln1, KD)

            def scale_pick(h):
                for d in range(2):
                    v4 = pick[:, d, :, :].rearrange("p (c k) a -> p c k a", c=NB)
                    pool.wait_ge(picked, 2 * h + d + 1)
                    pool.tensor_tensor(v4, v4, idxf[:, d, :, :].unsqueeze(2).to_broadcast([P, NB, TOPK, TOPK]),
                                       ALU.mult).then_inc(pick_scaled, 1)

            pool.wait_ge(lo_ready, POOL_R[0])
            for t in range(2 * HEADS_R + 2):
                lo(T_ROUTE + t + 2, t % 2)
                if t >= 3 and t % 2:
                    scale_pick(t // 2 - 1)

            quads = 0
            for e in range(2, EG):
                if e == min(QUADS_OF):
                    pool.wait_ge(sel_t_ready, 3)
                for _ in range(QUADS_OF.get(e, 0)):
                    s_ = 4 * (quads % 4)
                    pool.wait_ge(hot_matched, quads + 1)
                    pool.tensor_tensor(hot[:, 0, s_:s_ + 4, :], hot[:, 0, s_:s_ + 4, :],
                                       g_t[:, 4 * quads:4 * quads + 4].unsqueeze(2).to_broadcast([P, 4, P]),
                                       ALU.mult).then_inc(hot_ready, 1)
                    quads += 1
                if T_PEER + e + 2 not in QUAD_LO.values():
                    if e == max(QUADS_OF):
                        pool.wait_ge(lo_ready, T_PEER + e + 2)
                    lo(T_PEER + e + 2, e % 2)
            centre("2", ln2, KD // 2)


def _constants():
    c = np.zeros((P, N_CONST), np.float32)
    r = np.arange(P)
    c[:, K_IDENT:K_IDENT + P] = np.eye(P)
    c[:, K_IOTA:K_IOTA + P] = r
    c[:, K_MASK:K_MASK + P] = np.where(r[None, :] > r[:, None], 0.0, NEG)
    c[:, K_MASK + P:K_MASK + 2 * P] = np.where(r[None, :] <= r[:, None], 0.0, NEG)
    rot = np.zeros((P, P), np.float32)
    for m in range(P):
        if m % HEAD < ROT // 2:
            rot[m + ROT // 2, m] = -1.0
        elif m % HEAD < ROT:
            rot[m - ROT // 2, m] = 1.0
    c[:, K_ROT:K_ROT + P] = rot
    for g in range(2):
        for m in range(P):
            c[64 * g + m % 64, K_DUP + P * g + m] = 1.0
            c[64 * g:64 * g + 64, K_RDUP + P * g + m] = rot[0:64, m % 64]
    freq = np.float32(THETA) ** (-np.arange(0, ROT, 2, dtype=np.float32) / np.float32(ROT))
    c[:, K_FREQ] = [freq[m % HEAD % (ROT // 2)] if m % HEAD < ROT else 0.0 for m in range(P)]
    return c


def _tiles(w, n_in=KD):
    s = 16 // n_in
    t = w.reshape(n_in, P, -1, s, P).transpose(2, 1, 3, 0, 4)
    return np.ascontiguousarray(t).reshape(-1, P, 16 * P)


def _columns(v):
    return v.reshape(-1, P).T


def kernel(**inputs):
    import concourse.bacc as _bacc
    from concourse.bass_utils import run_bass_kernel_spmd as _run

    a = {k: np.asarray(v) for k, v in inputs.items()}
    nq, nk = KD, 2
    q0, k0 = 2 * KC, 2 * KC + nq
    v0, a0 = k0 + nk, k0 + 2 * nk
    order = [t for i in range(KC) for t in (i, KC + i)] + list(range(k0, a0)) + list(range(q0, k0))
    order += list(range(a0 + KD, a0 + 2 * KD)) + list(range(a0, a0 + KD))
    w_v = a["expert_v"][0].reshape(N_GROUPS, EG, P, KD // 2, 2, P).transpose(0, 3, 2, 4, 1, 5)
    params = np.concatenate([
        _columns(a["b_in"][0])[:, order],
        a["conv_dw_w"][0, :, 0, :].reshape(TAPS, KC, P).transpose(2, 1, 0).reshape(P, KC * TAPS),
        _columns(a["conv_dw_b"][0]), _columns(a["conv_ln_g"][0]), _columns(a["conv_ln_b"][0]),
        np.broadcast_to(a["attn_sinks"][0][None, :], (P, N_HEADS)),
        _columns(a["ln1_g"][0]), _columns(a["ln1_b"][0]), _columns(a["ln2_g"][0]), _columns(a["ln2_b"][0]),
        a["sub_keys_1"][0].T, a["sub_keys_2"][0].T], axis=1)
    arrays = {
        "x_t": a["x"][0].T.reshape(KD, P, S).transpose(1, 0, 2),
        "pos": a["positions"],
        "w_in": _tiles(a["w_in"][0])[order],
        "w_conv": _tiles(a["w_conv_out"][0], KC),
        "w_mix": _tiles(a["w_mix_out"][0]),
        "w_route": _tiles(a["w_peer_q"][0]),
        "exp_u": _tiles(a["expert_u"][0].T),
        "exp_v": w_v.reshape(N_GROUPS * KD // 2, P, 16 * P),
        "params": params,
        "consts": _constants(),
    }
    arrays = {k: np.ascontiguousarray(v) for k, v in arrays.items()}
    nc = _bacc.Bacc("TRN2", target_bir_lowering=False, num_devices=1)
    args = [nc.dram_tensor(k, v.shape, mybir.dt.from_np(v.dtype), kind="ExternalInput").ap() for k, v in arrays.items()]
    args.append(nc.dram_tensor("gates", (N_CG, P, NKEY * CG), F32, kind="Internal").ap())
    args.append(nc.dram_tensor("u_kept", (P, KC, S), F32, kind="Internal").ap())
    args.append(nc.dram_tensor("out", (P, KD, S), F32, kind="ExternalOutput").ap())
    build(nc, *args)
    r = _run(nc, [arrays], core_ids=[0])
    return r.results[0]["out"].transpose(1, 0, 2).reshape(1, D, S).transpose(0, 2, 1)
```
